# Optimizing a Trainium2 kernel written in Bass

```python
import jax, jax.numpy as jnp
from jax import lax
import numpy as np
import math

D_MODEL = 1024
BATCH = 1
SEQ = 256
DEPTH = 2

N_EVEN = (DEPTH + 1) // 2
N_ODD = DEPTH // 2
D_PLE = 256
D_FF = 2816
EPS = 1e-6
N_NORMS = 5
NEG_BIG = -1e30
F_MIN = 1e-6
LB_MAX = 0.999

A_HEADS = 8
A_HEAD_DIM = 64
A_WIDTH = A_HEADS * A_HEAD_DIM
A_CHUNK = 128
B_HEADS = 4
B_KEY_DIM = 128
B_VAL_DIM = 128
B_KW = B_HEADS * B_KEY_DIM
B_VW = B_HEADS * B_VAL_DIM
B_CHUNK = 64
EVEN_IN = 2 * A_WIDTH + 2 * B_KW + 2 * B_VW
EVEN_OUT = A_WIDTH + B_VW
C_HEADS = 8
C_NOPE = 128
C_ROPE = 64
C_V = 128
C_QK = C_NOPE + C_ROPE
Q_LORA = 384
KV_LORA = 256
ODD_IN = Q_LORA + KV_LORA + C_ROPE
ATTN_BLOCK = 128
ROPE_THETA = 10000.0
ATTN_SCALE = C_QK ** -0.5


def rms_norm(x, g):
    x32 = x.astype(jnp.float32)
    y = x32 * lax.rsqrt(jnp.mean(x32 * x32, axis=-1, keepdims=True) + EPS)
    return (y * g.astype(jnp.float32)).astype(x.dtype)

def swiglu(h, w_gate, w_up, w_down):
    return (jax.nn.silu(h @ w_gate) * (h @ w_up)) @ w_down

def gmlp_spatial(u, v, v_norm, w_s, b_s):
    bsz, seq = u.shape[:2]
    n_chunks = seq // A_CHUNK
    v = rms_norm(v, v_norm)
    vc = v.reshape(bsz, n_chunks, A_CHUNK, A_HEADS, A_HEAD_DIM)
    causal = jnp.tril(jnp.ones((A_CHUNK, A_CHUNK), dtype=bool))
    w = jnp.where(causal[None], w_s, 0.0).astype(vc.dtype)
    mixed = jnp.einsum('hts,bcshd->bcthd', w, vc) + b_s.T[None, None, :, :, None].astype(vc.dtype)
    return u * mixed.reshape(bsz, seq, A_HEADS, A_HEAD_DIM)

def hgrn2_chunkwise(q, log_f, k, v):
    bsz, seq = q.shape[:2]
    n = seq // B_CHUNK

    def to_chunks(t):
        t = t.astype(jnp.float32).reshape(bsz, n, B_CHUNK, B_HEADS, t.shape[-1])
        return jnp.transpose(t, (1, 0, 3, 2, 4))

    qc, kc, vc = to_chunks(q), to_chunks(k), to_chunks(v)
    bc = jnp.cumsum(to_chunks(log_f), axis=3)
    causal = jnp.tril(jnp.ones((B_CHUNK, B_CHUNK), dtype=bool))[:, :, None]

    def step(state, xs):
        q_, k_, v_, b_ = xs
        diff = b_[:, :, :, None, :] - b_[:, :, None, :, :]
        decay = jnp.exp(jnp.where(causal, diff, NEG_BIG))
        scores = jnp.einsum('bhtd,bhtsd->bhts', q_, decay * k_[:, :, None, :, :])
        o = jnp.einsum('bhts,bhse->bhte', scores, v_)
        o = o + jnp.einsum('bhtd,bhde->bhte', q_ * jnp.exp(b_), state)
        b_last = b_[:, :, -1:, :]
        state = jnp.exp(b_last)[:, :, 0, :, None] * state + jnp.einsum(
            'bhsd,bhse->bhde', k_ * jnp.exp(b_last - b_), v_)
        return state, o

    state0 = jnp.zeros((bsz, B_HEADS, B_KEY_DIM, B_VAL_DIM), jnp.float32)
    _, oc = lax.scan(step, state0, (qc, kc, vc, bc))
    return jnp.transpose(oc, (1, 0, 3, 2, 4)).reshape(bsz, seq, B_HEADS, B_VAL_DIM)

def even_mixer(h, w_in, v_norm, w_s, b_s, lb, out_norm, w_out):
    bsz, seq, _ = h.shape
    z = h @ w_in
    a_u, a_v, b_q, b_f, b_i, b_g = jnp.split(
        z, [A_WIDTH, 2 * A_WIDTH, 2 * A_WIDTH + B_KW, 2 * A_WIDTH + 2 * B_KW,
            2 * A_WIDTH + 2 * B_KW + B_VW], axis=-1)
    a_u = jax.nn.gelu(a_u).reshape(bsz, seq, A_HEADS, A_HEAD_DIM)
    a_v = jax.nn.gelu(a_v).reshape(bsz, seq, A_HEADS, A_HEAD_DIM)
    a_out = gmlp_spatial(a_u, a_v, v_norm, w_s, b_s).reshape(bsz, seq, A_WIDTH)
    zf = b_f.astype(jnp.float32)
    f = lb + (1.0 - lb) * jax.nn.sigmoid(zf)
    log_f = jnp.log(jnp.maximum(f, F_MIN))
    k = 1.0 - f
    o = hgrn2_chunkwise(b_q.reshape(bsz, seq, B_HEADS, B_KEY_DIM),
                        log_f.reshape(bsz, seq, B_HEADS, B_KEY_DIM),
                        k.reshape(bsz, seq, B_HEADS, B_KEY_DIM),
                        b_i.reshape(bsz, seq, B_HEADS, B_VAL_DIM))
    o = rms_norm(o, out_norm).astype(h.dtype) * jax.nn.silu(b_g.reshape(bsz, seq, B_HEADS, B_VAL_DIM))
    mixed = jnp.concatenate([a_out, o.reshape(bsz, seq, B_VW)], axis=-1)
    return mixed @ w_out

def rotate_half(x, cos, sin):
    x1, x2 = jnp.split(x, 2, axis=-1)
    return jnp.concatenate([x1 * cos - x2 * sin, x2 * cos + x1 * sin], axis=-1).astype(x.dtype)

def mla_mixer(h, positions, w_in, q_a_norm, kv_a_norm, w_q_b, w_kv_b, q_norm, k_norm, w_out):
    bsz, seq, _ = h.shape
    z = h @ w_in
    c_q, c_kv, k_rope = jnp.split(z, [Q_LORA, Q_LORA + KV_LORA], axis=-1)
    q = (rms_norm(c_q, q_a_norm) @ w_q_b).reshape(bsz, seq, C_HEADS, C_QK)
    kv = (rms_norm(c_kv, kv_a_norm) @ w_kv_b).reshape(bsz, seq, C_HEADS, C_NOPE + C_V)
    k_nope, v = jnp.split(kv, [C_NOPE], axis=-1)
    k_rope = jnp.broadcast_to(k_rope[:, :, None, :], (bsz, seq, C_HEADS, C_ROPE))
    k = jnp.concatenate([k_nope, k_rope], axis=-1)
    q = rms_norm(q, q_norm)
    k = rms_norm(k, k_norm)
    inv_freq = ROPE_THETA ** (-jnp.arange(0, C_ROPE, 2, dtype=jnp.float32) / C_ROPE)
    ang = positions.astype(jnp.float32)[..., None] * inv_freq
    cos = jnp.cos(ang)[:, :, None, :]
    sin = jnp.sin(ang)[:, :, None, :]
    q = jnp.concatenate([q[..., :C_NOPE], rotate_half(q[..., C_NOPE:], cos, sin)], axis=-1)
    k = jnp.concatenate([k[..., :C_NOPE], rotate_half(k[..., C_NOPE:], cos, sin)], axis=-1)
    q = jnp.transpose(q, (0, 2, 1, 3))
    k = jnp.transpose(k, (0, 2, 1, 3))
    v = jnp.transpose(v, (0, 2, 1, 3))
    n_blocks = seq // ATTN_BLOCK
    q_blocks = jnp.transpose(q.reshape(bsz, C_HEADS, n_blocks, ATTN_BLOCK, C_QK), (2, 0, 1, 3, 4))
    key_pos = jnp.arange(seq)

    def attend(args):
        qb, start = args
        s = jnp.einsum('bhqd,bhkd->bhqk', qb, k).astype(jnp.float32) * ATTN_SCALE
        q_pos = start + jnp.arange(ATTN_BLOCK)
        s = jnp.where(key_pos[None, :] <= q_pos[:, None], s, NEG_BIG)
        pr = jax.nn.softmax(s, axis=-1).astype(v.dtype)
        return jnp.einsum('bhqk,bhkd->bhqd', pr, v)

    out = lax.map(attend, (q_blocks, jnp.arange(n_blocks) * ATTN_BLOCK))
    out = jnp.transpose(out, (1, 0, 3, 2, 4)).reshape(bsz, seq, C_HEADS * C_V)
    return out @ w_out

def per_layer_embedding(h, p_i, w_gate, w_proj, post_norm):
    return rms_norm(jax.nn.sigmoid(h @ w_gate) * (p_i @ w_proj), post_norm)

def first_inputs(seed: int = 0) -> dict:
    key = jax.random.key(seed)
    ks = jax.random.split(key, 32)
    f32 = jnp.float32

    def nrm(k, shape, fan_in):
        return jax.random.normal(k, shape, f32) * (fan_in ** -0.5)

    def gain(k, shape):
        return 1.0 + 0.02 * jax.random.normal(k, shape, f32)

    x = jax.random.normal(ks[0], (BATCH, SEQ, D_MODEL), f32)
    p = jax.random.normal(ks[1], (DEPTH, BATCH, SEQ, D_PLE), f32)
    offset = jax.random.randint(ks[2], (BATCH, 1), 0, 1024, dtype=jnp.int32)
    positions = offset + jnp.arange(SEQ, dtype=jnp.int32)[None, :]
    return {
        'x': x,
        'p': p,
        'positions': positions,
        'norm_gains': gain(ks[3], (DEPTH, N_NORMS, D_MODEL)),
        'ffn_w_gate': nrm(ks[4], (DEPTH, 2, D_MODEL, D_FF), D_MODEL),
        'ffn_w_up': nrm(ks[5], (DEPTH, 2, D_MODEL, D_FF), D_MODEL),
        'ffn_w_down': nrm(ks[6], (DEPTH, 2, D_FF, D_MODEL), D_FF),
        'ple_w_gate': nrm(ks[7], (DEPTH, D_MODEL, D_MODEL), D_MODEL),
        'ple_w_proj': nrm(ks[8], (DEPTH, D_PLE, D_MODEL), D_PLE),
        'even_w_in': nrm(ks[9], (N_EVEN, D_MODEL, EVEN_IN), D_MODEL),
        'gmlp_v_norm': gain(ks[10], (N_EVEN, A_HEADS, A_HEAD_DIM)),
        'gmlp_w_s': nrm(ks[11], (N_EVEN, A_HEADS, A_CHUNK, A_CHUNK), A_CHUNK),
        'gmlp_b_s': 1.0 + 0.01 * jax.random.normal(ks[12], (N_EVEN, A_HEADS, A_CHUNK), f32),
        'hgrn_lb_raw': 0.5 * jax.random.normal(ks[13], (N_EVEN, B_KW), f32),
        'hgrn_out_norm': gain(ks[14], (N_EVEN, B_VAL_DIM)),
        'even_w_out': nrm(ks[15], (N_EVEN, EVEN_OUT, D_MODEL), EVEN_OUT),
        'mla_w_in': nrm(ks[16], (N_ODD, D_MODEL, ODD_IN), D_MODEL),
        'mla_q_a_norm': gain(ks[17], (N_ODD, Q_LORA)),
        'mla_kv_a_norm': gain(ks[18], (N_ODD, KV_LORA)),
        'mla_w_q_b': nrm(ks[19], (N_ODD, Q_LORA, C_HEADS * C_QK), Q_LORA),
        'mla_w_kv_b': nrm(ks[20], (N_ODD, KV_LORA, C_HEADS * (C_NOPE + C_V)), KV_LORA),
        'mla_q_norm': gain(ks[21], (N_ODD, C_QK)),
        'mla_k_norm': gain(ks[22], (N_ODD, C_QK)),
        'mla_w_out': nrm(ks[23], (N_ODD, C_HEADS * C_V, D_MODEL), C_HEADS * C_V),
    }

def first_block(x, p, positions, norm_gains, ffn_w_gate, ffn_w_up, ffn_w_down,
              ple_w_gate, ple_w_proj, even_w_in, gmlp_v_norm, gmlp_w_s, gmlp_b_s,
              hgrn_lb_raw, hgrn_out_norm, even_w_out, mla_w_in, mla_q_a_norm,
              mla_kv_a_norm, mla_w_q_b, mla_w_kv_b, mla_q_norm, mla_k_norm, mla_w_out):
    lb_sm = jax.nn.softmax(hgrn_lb_raw.astype(jnp.float32), axis=0)
    lower_bounds = jnp.clip(jnp.cumsum(lb_sm, axis=0) - lb_sm[0], 0.0, LB_MAX)
    for i in range(DEPTH):
        g = norm_gains[i]
        x = x + 0.5 * swiglu(rms_norm(x, g[0]), ffn_w_gate[i, 0], ffn_w_up[i, 0], ffn_w_down[i, 0])
        h = rms_norm(x, g[1])
        j = i // 2
        if i % 2 == 0:
            m = even_mixer(h, even_w_in[j], gmlp_v_norm[j], gmlp_w_s[j], gmlp_b_s[j],
                           lower_bounds[j], hgrn_out_norm[j], even_w_out[j])
        else:
            m = mla_mixer(h, positions, mla_w_in[j], mla_q_a_norm[j], mla_kv_a_norm[j],
                          mla_w_q_b[j], mla_w_kv_b[j], mla_q_norm[j], mla_k_norm[j], mla_w_out[j])
        x = x + m
        x = x + 0.5 * swiglu(rms_norm(x, g[2]), ffn_w_gate[i, 1], ffn_w_up[i, 1], ffn_w_down[i, 1])
        x = x + per_layer_embedding(rms_norm(x, g[3]), p[i], ple_w_gate[i], ple_w_proj[i], g[4])
    return x


DEPTH_2 = 1

ATTN_HEADS = 6
ATTN_HEAD_DIM = 64
ATTN_WIDTH = ATTN_HEADS * ATTN_HEAD_DIM
MOBA_BLOCK = 256
MOBA_TOPK = 3
MOBA_QUERY_CHUNK = 64
SSD_HEADS = 6
SSD_HEAD_DIM = 64
SSD_WIDTH = SSD_HEADS * SSD_HEAD_DIM
SSD_GROUPS = 2
SSD_STATE = 128
SSD_CONV = 4
SSD_CHUNK = 128
XBC_WIDTH = SSD_WIDTH + 2 * SSD_GROUPS * SSD_STATE
POOL_WINDOWS = (2, 4, 8, 16)
POOL_GROUPS = len(POOL_WINDOWS)
POOL_GROUP_DIM = 64
POOL_WIDTH = POOL_GROUPS * POOL_GROUP_DIM
MIX_WIDTH = ATTN_WIDTH + SSD_WIDTH + POOL_WIDTH
IN_PROJ_WIDTH = 3 * ATTN_WIDTH + SSD_WIDTH + XBC_WIDTH + SSD_HEADS + POOL_WIDTH
FFN_HIDDEN = ((8 * D_MODEL // 3 + 255) // 256) * 256
NORM_EPS = 1e-6
NEG_INF = -1e30


def rmsnorm(x, g):
    xf = x.astype(jnp.float32)
    xf = xf * lax.rsqrt(jnp.mean(xf * xf, axis=-1, keepdims=True) + NORM_EPS)
    return xf.astype(x.dtype) * g

def causal_depthwise_conv(x, w, b):
    k_width, ch = w.shape
    y = lax.conv_general_dilated(
        x, w[:, None, :], window_strides=(1,), padding=[(k_width - 1, 0)],
        dimension_numbers=('NWC', 'WIO', 'NWC'), feature_group_count=ch)
    return y + b

def moba_attention(q, k, v):
    bsz, n_heads, seq, hd = q.shape
    n_blocks = -(-seq // MOBA_BLOCK)
    pad = n_blocks * MOBA_BLOCK - seq
    k_p = jnp.pad(k, ((0, 0), (0, 0), (0, pad), (0, 0)))
    v_p = jnp.pad(v, ((0, 0), (0, 0), (0, pad), (0, 0)))
    k_blocks = k_p.reshape(bsz, n_heads, n_blocks, MOBA_BLOCK, hd)
    v_blocks = v_p.reshape(bsz, n_heads, n_blocks, MOBA_BLOCK, hd)
    k_mean = jnp.mean(k_blocks, axis=3)
    n_sel = min(MOBA_TOPK, n_blocks)
    scale = hd ** -0.5
    b_idx = jnp.arange(bsz)[:, None, None, None]
    h_idx = jnp.arange(n_heads)[None, :, None, None]
    block_ids = jnp.arange(n_blocks)

    def query_chunk(c):
        q0 = c * MOBA_QUERY_CHUNK
        qc = lax.dynamic_slice_in_dim(q, q0, MOBA_QUERY_CHUNK, axis=2)
        blk = q0 // MOBA_BLOCK
        gate = jnp.einsum('bhqd,bhnd->bhqn', qc, k_mean).astype(jnp.float32)
        gate = jnp.where(block_ids < blk, gate, NEG_INF)
        _, idx = lax.top_k(gate, n_sel)
        valid = jnp.arange(n_sel) < blk
        k_sel = k_blocks[b_idx, h_idx, idx]
        v_sel = v_blocks[b_idx, h_idx, idx]
        s_sel = jnp.einsum('bhqd,bhqnkd->bhqnk', qc, k_sel).astype(jnp.float32) * scale
        s_sel = jnp.where(valid[:, None], s_sel, NEG_INF)
        s_sel = s_sel.reshape(bsz, n_heads, MOBA_QUERY_CHUNK, n_sel * MOBA_BLOCK)
        k_own = lax.dynamic_index_in_dim(k_blocks, blk, axis=2, keepdims=False)
        v_own = lax.dynamic_index_in_dim(v_blocks, blk, axis=2, keepdims=False)
        s_own = jnp.einsum('bhqd,bhkd->bhqk', qc, k_own).astype(jnp.float32) * scale
        q_pos = q0 + jnp.arange(MOBA_QUERY_CHUNK)
        k_pos = blk * MOBA_BLOCK + jnp.arange(MOBA_BLOCK)
        s_own = jnp.where(k_pos[None, :] <= q_pos[:, None], s_own, NEG_INF)
        p = jax.nn.softmax(jnp.concatenate([s_sel, s_own], axis=-1), axis=-1).astype(v.dtype)
        p_sel = p[..., :n_sel * MOBA_BLOCK].reshape(bsz, n_heads, MOBA_QUERY_CHUNK, n_sel, MOBA_BLOCK)
        p_own = p[..., n_sel * MOBA_BLOCK:]
        return (jnp.einsum('bhqnk,bhqnkd->bhqd', p_sel, v_sel)
                + jnp.einsum('bhqk,bhkd->bhqd', p_own, v_own))

    out = lax.map(query_chunk, jnp.arange(seq // MOBA_QUERY_CHUNK))
    return out.transpose(1, 0, 3, 2, 4).reshape(bsz, seq, n_heads * hd)

def ssd_mixer(xbc, z, dt_raw, conv_w, conv_b, dt_bias, a_log, d_skip, norm_w):
    bsz, seq, _ = xbc.shape
    n_chunks = seq // SSD_CHUNK
    rep = SSD_HEADS // SSD_GROUPS
    xbc = jax.nn.silu(causal_depthwise_conv(xbc, conv_w, conv_b)).astype(jnp.float32)
    xs, b_in, c_in = jnp.split(xbc, [SSD_WIDTH, SSD_WIDTH + SSD_GROUPS * SSD_STATE], axis=-1)
    x_h = xs.reshape(bsz, seq, SSD_HEADS, SSD_HEAD_DIM)
    b_h = jnp.repeat(b_in.reshape(bsz, seq, SSD_GROUPS, SSD_STATE), rep, axis=2)
    c_h = jnp.repeat(c_in.reshape(bsz, seq, SSD_GROUPS, SSD_STATE), rep, axis=2)
    dt = jax.nn.softplus(dt_raw.astype(jnp.float32) + dt_bias.astype(jnp.float32))
    a = -jnp.exp(a_log.astype(jnp.float32))

    def chunks(t):
        return t.reshape((bsz, n_chunks, SSD_CHUNK) + t.shape[2:])

    xdt = chunks(x_h * dt[..., None])
    b_c, c_c = chunks(b_h), chunks(c_h)
    a_cum = jnp.cumsum(chunks(dt * a).transpose(0, 3, 1, 2), axis=-1)
    causal = jnp.tril(jnp.ones((SSD_CHUNK, SSD_CHUNK), dtype=bool))
    decay = jnp.exp(jnp.where(causal, a_cum[..., :, None] - a_cum[..., None, :], -jnp.inf))
    y_diag = jnp.einsum('bclhn,bcshn,bhcls,bcshp->bclhp', c_c, b_c, decay, xdt)
    decay_to_end = jnp.exp(a_cum[..., -1:] - a_cum)
    states = jnp.einsum('bclhn,bhcl,bclhp->bchpn', b_c, decay_to_end, xdt)
    chunk_decay = jnp.exp(a_cum[..., -1])

    def step(h, inp):
        st, d = inp
        return h * d[..., None, None] + st, h

    _, prev = lax.scan(step, jnp.zeros_like(states[:, 0]),
                       (states.transpose(1, 0, 2, 3, 4), chunk_decay.transpose(2, 0, 1)))
    prev = prev.transpose(1, 0, 2, 3, 4)
    y_off = jnp.einsum('bclhn,bchpn,bhcl->bclhp', c_c, prev, jnp.exp(a_cum))
    y = (y_diag + y_off).reshape(bsz, seq, SSD_HEADS, SSD_HEAD_DIM) + x_h * d_skip.astype(jnp.float32)[:, None]
    y = y.reshape(bsz, seq, SSD_WIDTH) * jax.nn.silu(z.astype(jnp.float32))
    yg = y.reshape(bsz, seq, SSD_GROUPS, SSD_WIDTH // SSD_GROUPS)
    yg = yg * lax.rsqrt(jnp.mean(yg * yg, axis=-1, keepdims=True) + NORM_EPS)
    return (yg.reshape(bsz, seq, SSD_WIDTH) * norm_w.astype(jnp.float32)).astype(z.dtype)

def pool_mixer(p, pool_w, pool_scale):
    bsz, seq, _ = p.shape
    pg = p.astype(jnp.float32).reshape(bsz, seq, POOL_GROUPS, POOL_GROUP_DIM)
    csum = jnp.concatenate([jnp.zeros_like(pg[:, :1]), jnp.cumsum(pg, axis=1)], axis=1)
    t = jnp.arange(seq)[:, None]
    win = jnp.asarray(POOL_WINDOWS, dtype=jnp.int32)[None, :]
    start = jnp.maximum(t + 1 - win, 0)
    lower = csum[:, start, jnp.arange(POOL_GROUPS)[None, :], :]
    count = jnp.minimum(t + 1, win).astype(jnp.float32)
    mean = (csum[:, 1:] - lower) / count[None, :, :, None]
    mixed = jnp.einsum('bsgc,gcd->bsgd', mean - pg, pool_w.astype(jnp.float32))
    return (mixed.reshape(bsz, seq, POOL_WIDTH) * pool_scale.astype(jnp.float32)).astype(p.dtype)

def hybrid_layer(x, norm_mix, w_in, conv_w, conv_b, dt_bias, a_log, d_skip, ssd_norm,
                 pool_w, pool_scale, w_out, norm_ffn, w_gate_up, w_down):
    bsz, seq, _ = x.shape
    h = rmsnorm(x, norm_mix)
    u = h @ w_in
    sizes = (ATTN_WIDTH, ATTN_WIDTH, ATTN_WIDTH, SSD_WIDTH, XBC_WIDTH, SSD_HEADS, POOL_WIDTH)
    offsets = []
    acc = 0
    for s in sizes[:-1]:
        acc += s
        offsets.append(acc)
    q, k, v, z, xbc, dt_raw, p_in = jnp.split(u, offsets, axis=-1)

    def heads(t):
        return t.reshape(bsz, seq, ATTN_HEADS, ATTN_HEAD_DIM).transpose(0, 2, 1, 3)

    y_attn = moba_attention(heads(q), heads(k), heads(v))
    y_ssd = ssd_mixer(xbc, z, dt_raw, conv_w, conv_b, dt_bias, a_log, d_skip, ssd_norm)
    y_pool = pool_mixer(p_in, pool_w, pool_scale)
    x = x + jnp.concatenate([y_attn, y_ssd, y_pool], axis=-1) @ w_out
    h = rmsnorm(x, norm_ffn)
    gate, up = jnp.split(h @ w_gate_up, 2, axis=-1)
    return x + (jax.nn.silu(gate) * up) @ w_down

def second_inputs(seed: int = 0) -> dict:
    key = jax.random.key(seed)
    ks = jax.random.split(key, 16)
    nrm = jax.random.normal
    dt0 = jnp.exp(jax.random.uniform(ks[5], (DEPTH_2, SSD_HEADS), minval=math.log(1e-3), maxval=math.log(1e-1)))
    return {
        'x': nrm(ks[0], (BATCH, SEQ, D_MODEL), jnp.float32),
        'norm_mix': 1.0 + 0.05 * nrm(ks[1], (DEPTH_2, D_MODEL), jnp.float32),
        'w_in': nrm(ks[2], (DEPTH_2, D_MODEL, IN_PROJ_WIDTH), jnp.float32) * D_MODEL ** -0.5,
        'conv_w': nrm(ks[3], (DEPTH_2, SSD_CONV, XBC_WIDTH), jnp.float32) * SSD_CONV ** -0.5,
        'conv_b': 0.02 * nrm(ks[4], (DEPTH_2, XBC_WIDTH), jnp.float32),
        'dt_bias': dt0 + jnp.log(-jnp.expm1(-dt0)),
        'a_log': jnp.log(jax.random.uniform(ks[6], (DEPTH_2, SSD_HEADS), minval=1.0, maxval=16.0)),
        'd_skip': 1.0 + 0.1 * nrm(ks[7], (DEPTH_2, SSD_HEADS), jnp.float32),
        'ssd_norm': 1.0 + 0.05 * nrm(ks[8], (DEPTH_2, SSD_WIDTH), jnp.float32),
        'pool_w': nrm(ks[9], (DEPTH_2, POOL_GROUPS, POOL_GROUP_DIM, POOL_GROUP_DIM), jnp.float32) * POOL_GROUP_DIM ** -0.5,
        'pool_scale': 1.0 + 0.1 * nrm(ks[10], (DEPTH_2, POOL_WIDTH), jnp.float32),
        'w_out': nrm(ks[11], (DEPTH_2, MIX_WIDTH, D_MODEL), jnp.float32) * MIX_WIDTH ** -0.5,
        'norm_ffn': 1.0 + 0.05 * nrm(ks[12], (DEPTH_2, D_MODEL), jnp.float32),
        'w_gate_up': nrm(ks[13], (DEPTH_2, D_MODEL, 2 * FFN_HIDDEN), jnp.float32) * D_MODEL ** -0.5,
        'w_down': nrm(ks[14], (DEPTH_2, FFN_HIDDEN, D_MODEL), jnp.float32) * FFN_HIDDEN ** -0.5,
        'norm_final': 1.0 + 0.05 * nrm(ks[15], (D_MODEL,), jnp.float32),
    }

def second_block(x, norm_mix, w_in, conv_w, conv_b, dt_bias, a_log, d_skip, ssd_norm,
              pool_w, pool_scale, w_out, norm_ffn, w_gate_up, w_down, norm_final):
    for l in range(DEPTH_2):
        x = hybrid_layer(x, norm_mix[l], w_in[l], conv_w[l], conv_b[l], dt_bias[l], a_log[l],
                         d_skip[l], ssd_norm[l], pool_w[l], pool_scale[l], w_out[l],
                         norm_ffn[l], w_gate_up[l], w_down[l])
    return rmsnorm(x, norm_final)


def setup_inputs(seed=0):
    out = dict(first_inputs(seed))
    for name, value in second_inputs(seed + 1).items():
        if name != "x":
            out[name + "_2"] = value
    return out


def reference(
    x, p, positions, norm_gains, ffn_w_gate, ffn_w_up, ffn_w_down, ple_w_gate, ple_w_proj,
    even_w_in, gmlp_v_norm, gmlp_w_s, gmlp_b_s, hgrn_lb_raw, hgrn_out_norm, even_w_out,
    mla_w_in, mla_q_a_norm, mla_kv_a_norm, mla_w_q_b, mla_w_kv_b, mla_q_norm, mla_k_norm,
    mla_w_out, norm_mix_2, w_in_2, conv_w_2, conv_b_2, dt_bias_2, a_log_2, d_skip_2, ssd_norm_2,
    pool_w_2, pool_scale_2, w_out_2, norm_ffn_2, w_gate_up_2, w_down_2, norm_final_2,
):
    x = first_block(
        x, p, positions, norm_gains, ffn_w_gate, ffn_w_up, ffn_w_down, ple_w_gate, ple_w_proj,
        even_w_in, gmlp_v_norm, gmlp_w_s, gmlp_b_s, hgrn_lb_raw, hgrn_out_norm, even_w_out,
        mla_w_in, mla_q_a_norm, mla_kv_a_norm, mla_w_q_b, mla_w_kv_b, mla_q_norm, mla_k_norm,
        mla_w_out,
    )
    return second_block(
        x, norm_mix_2, w_in_2, conv_w_2, conv_b_2, dt_bias_2, a_log_2, d_skip_2, ssd_norm_2,
        pool_w_2, pool_scale_2, w_out_2, norm_ffn_2, w_gate_up_2, w_down_2, norm_final_2,
    )


_drawn_inputs = setup_inputs


def setup_inputs(seed=0):
    import zlib

    import numpy as np

    out = dict(_drawn_inputs(seed))
    spreads = {}
    factors = {'gmlp_v_norm': 8.0,
     'gmlp_b_s': 8.0,
     'hgrn_out_norm': 8.0,
     'mla_q_a_norm': 8.0,
     'mla_kv_a_norm': 8.0,
     'mla_q_norm': 8.0,
     'mla_k_norm': 8.0,
     'conv_b_2': 7.12,
     'd_skip_2': 23.657,
     'ssd_norm_2': 15.111,
     'norm_ffn_2': 2.918,
     'norm_mix_2': 3.086,
     'dt_bias_2': 2.812,
     'a_log_2': 3.428,
     'pool_scale_2': 8.0}
    for name, (base, spread) in spreads.items():
        noise = np.random.default_rng([zlib.crc32(name.encode()), seed]).standard_normal(out[name].shape)
        drawn = base * np.exp(spread * noise) if base else spread * noise
        out[name] = __import__('jax').numpy.asarray(drawn.astype(out[name].dtype))
    for name, factor in factors.items():
        out[name] = (out[name] * factor).astype(out[name].dtype)
    return out
```

```python
import math
from contextlib import ExitStack

import concourse.bass as bass
from concourse import mybir


class Steps:

    def __init__(self, sem, names, calls=1):
        self.sem, self.names, self.calls, self.said = sem, names, calls, 0

    def after(self, name, call=0):
        return call * len(self.names) + self.names.index(name) + 1

    def done(self, instruction, name, call=0):
        self.said += 1
        assert self.said == self.after(name, call), (name, self.names[(self.said - 1) % len(self.names)])
        instruction.then_inc(self.sem, 1)


def build_block(nc, io, out, stages=99, dump=None):
    f32, f32r, i32 = mybir.dt.float32, mybir.dt.float32r, mybir.dt.int32
    ALU, ACT, AX = mybir.AluOpType, mybir.ActivationFunctionType, mybir.AxisListType

    P = 128
    T, D = io["x"].shape[1:]
    TT = T // P
    KT = D // P
    FF = io["ffn_w_gate"].shape[3]
    HC = 256
    NCH = FF // HC
    EPS = 1e-6
    assert T == 256 and D == 1024 and FF % HC == 0

    SLOT = 2048
    RING = 3
    FFN_SLOTS = 3 * NCH
    PLAN = ["ffn", "even", "ffn", "ple", "ffn", "mla", "ffn", "ple", "hybrid", "ffn"][:stages]
    SLOTS_OF = {"ffn": FFN_SLOTS, "even": 16, "ple": 5, "mla": 12, "hybrid": 16}
    base, total = [], 0
    for name in PLAN:
        base.append(total)
        total += SLOTS_OF[name]

    FEATURES_OF = {"ffn": [KT], "even": [KT, KT], "ple": [KT, 2], "mla": [KT, 5, KT], "hybrid": [KT, KT]}
    features_base, banks_so_far, calls_so_far = [], 0, 0
    call_base, bank_base = [], []
    for name in PLAN:
        call_base.append([])
        bank_base.append([])
        for c, n in enumerate(FEATURES_OF[name]):
            call_base[-1].append(calls_so_far)
            bank_base[-1].append(banks_so_far)
            banks_so_far += (n + 1) // 2
            calls_so_far += not (name == "ple" and c == 1)

    GAINS, MIX2, FFN2, QA, KVA, BS, LB, QN, KN = 0, 80, 88, 96, 99, 101, 109, 113, 114
    ROWS_A = 115
    CONVW, CONVB, ROWS_B = 0, 28, 35

    with ExitStack() as stack:
        def sb(name, shape, dt=f32):
            return stack.enter_context(nc.sbuf_tensor(name, shape, dt))

        def sem(name):
            return stack.enter_context(nc.semaphore(name))

        raw = sb("raw", [P, RING, SLOT])
        wh = sb("wh", [P, RING, SLOT], f32r)
        wl = sb("wl", [P, RING, SLOT], f32r)
        x = sb("x_rows", [P, TT, D])
        xn = sb("xn", [P, TT, D])
        hth = sb("hth", [P, KT, T], f32r)
        htl = sb("htl", [P, KT, T], f32r)
        silu_g = sb("silu_g", [P, TT, HC])
        prod = sb("prod", [P, TT, HC])
        prod_h = sb("prod_h", [P, 2, T], f32r)
        prod_l = sb("prod_l", [P, 2, T], f32r)
        ident = sb("ident", [P, P])
        rows_a = sb("rows_a", [P, P])
        rows_b = sb("rows_b", [P, P])
        cols = sb("cols", [P, ROWS_A])
        conv_cols = sb("conv_cols", [P, ROWS_B])
        mean_sq = sb("mean_sq", [P, TT])
        rstd = sb("rstd", [P, TT])
        minus_half = sb("minus_half", [P, 16])
        gain_row = sb("gain_row", [P, D])
        vnorm = sb("vnorm", [P, 512])
        onorm = sb("onorm", [P, 128])
        qk_norm = sb("qk_norm", [P, 2, 64])
        ssd_gain = sb("ssd_gain", [P, 384])
        pool_gain = sb("pool_gain", [P, 256])
        dt_bias = sb("dt_bias", [P, 6])
        a_log = sb("a_log", [P, 6])
        d_skip = sb("d_skip", [P, 6])
        inv_freq = sb("inv_freq", [P, 32])
        pos_i = sb("pos_i", [P, TT], i32)
        lb = sb("lb", [P, 3, 4])
        arena = sb("arena", [P, 20100])
        ps = stack.enter_context(nc.psum_tensor("ps", [P, 8, 512], f32))

        def bank(b, w=512):
            return ps[:, b, 0:w]

        raw_loaded = [sem(f"raw_loaded{r}") for r in range(RING)]
        high_ready = sem("high_ready")
        split_ready = sem("split_ready")
        weights_used = sem("weights_used")
        x_loaded = sem("x_loaded")
        params_loaded = sem("params_loaded")
        rows_loaded = sem("rows_loaded")
        ident_ready = sem("ident_ready")
        consts_ready = sem("consts_ready")
        cols_turned = sem("cols_turned")
        cols_ready = sem("cols_ready")
        x_ready = sem("x_ready")
        sq_ready = sem("sq_ready")
        rstd_ready = sem("rstd_ready")
        rows_ready = sem("rows_ready")
        turned = sem("turned")
        cols_high = sem("cols_high")
        cols_low = sem("cols_low")
        silu_ready = sem("silu_ready")
        prod_ready = sem("prod_ready")
        prod_turned = sem("prod_turned")
        prod_high = sem("prod_high")
        prod_low = sem("prod_low")
        gain_loaded = sem("gain_loaded")
        stored = sem("stored")
        lb_steps = sem("lb_steps")
        act_chain, dve_chain, pool_chain = sem("act_chain"), sem("dve_chain"), sem("pool_chain")

        class Chain:

            def __init__(self, s):
                self.sem, self.n = s, 0

            def __call__(self, eng, instruction):
                self.n += 1
                instruction.then_inc(self.sem, 1)
                eng.wait_ge(self.sem, self.n)

        act_link, dve_link, pool_link = Chain(act_chain), Chain(dve_chain), Chain(pool_chain)

        def load_slot(sp, n, pieces):
            if n >= RING:
                sp.wait_ge(split_ready, n - RING + 1)
            assert len(pieces) == 2
            for dst, src in pieces:
                sp.dma_start(dst, src).then_inc(raw_loaded[n % RING], 16)

        def raw_view(n, k, w):
            return raw[:, n % RING, 0:k * w].rearrange("p (k n) -> p k n", k=k)

        width = [SLOT] * total
        for s, name in enumerate(PLAN):
            if name == "mla":
                width[base[s] + 2] = 8 * 192
                for j in range(3):
                    width[base[s] + 3 + j] = 3 * 512
            if name == "hybrid":
                for j in range(2):
                    width[base[s] + 2 + j] = 4 * 384
                    width[base[s] + 4 + j] = 4 * 262

        def split_high(act, n):
            act.wait_ge(raw_loaded[n % RING], 32 * (n // RING + 1))
            if n >= RING:
                act.wait_ge(weights_used, n - RING + 1)
            nc.scalar.activation(wh[:, n % RING, 0:width[n]], raw[:, n % RING, 0:width[n]], ACT.Copy)\
              .then_inc(high_ready, 1)

        def split_low(dve, n):
            dve.wait_ge(high_ready, n + 1)
            nc.vector.tensor_tensor(wl[:, n % RING, 0:width[n]], raw[:, n % RING, 0:width[n]],
                                    wh[:, n % RING, 0:width[n]].bitcast(f32), ALU.subtract)\
              .then_inc(split_ready, 1)

        class Ahead:

            def __init__(self, split):
                self.split, self.n = split, 0

            def through(self, eng, n):
                while self.n <= min(n, total - 1):
                    self.split(eng, self.n)
                    self.n += 1

            def before(self, eng, n):
                self.through(eng, n + RING - 1)

        act_ahead, dve_ahead = Ahead(split_high), Ahead(split_low)

        def take_slot(pe, n):
            pe.wait_ge(split_ready, n + 1)

        def by_rows(outs, k, n, kk, w, first, last, off=0, cols_n=None):
            c = cols_n or w
            a, b = wh[:, n % RING, kk * w + off:kk * w + off + c], wl[:, n % RING, kk * w + off:kk * w + off + c]
            for tt in range(TT):
                h, l = hth[:, k, tt * P:(tt + 1) * P], htl[:, k, tt * P:(tt + 1) * P]
                nc.tensor.matmul(outs[tt], h, b, start=first, stop=False)
                nc.tensor.matmul(outs[tt], h, a, start=False, stop=False)
                m = nc.tensor.matmul(outs[tt], l, a, start=False, stop=last)
            return m

        def by_columns(o, k, n, kk, w, off, first, last):
            c = kk * w + off
            a, b = wh[:, n % RING, c:c + P], wl[:, n % RING, c:c + P]
            nc.tensor.matmul(o, b, hth[:, k, :], start=first, stop=False)
            nc.tensor.matmul(o, a, hth[:, k, :], start=False, stop=False)
            return nc.tensor.matmul(o, a, htl[:, k, :], start=False, stop=last)

        def project_out(pe, n):
            for s in range(4):
                take_slot(pe, n + s)
                for kk in range(2):
                    k = 2 * s + kk
                    for half in range(2):
                        m = by_rows([bank(4 + half), bank(6 + half)], k, n + s, kk, D, k == 0, k == KT - 1,
                                    off=half * 512, cols_n=512)
                m.then_inc(weights_used, 1)

        def load_square(sp, n, w):
            v = w.rearrange("(k p) n -> p k n", p=P)
            for s in range(4):
                load_slot(sp, n + s, [(raw_view(n + s, 2, D)[:, j:j + 1, :], v[:, 2 * s + j:2 * s + j + 1, :])
                                      for j in range(2)])

        def load_columns(sp, n, w, c0, c):
            v = w.rearrange("(k p) n -> p k n", p=P)
            for s in range(2):
                load_slot(sp, n + s, [(raw_view(n + s, 4, c)[:, 2 * j:2 * j + 2, :],
                                       v[:, 4 * s + 2 * j:4 * s + 2 * j + 2, c0:c0 + c]) for j in range(2)])

        def rows_product(pe, n, outs):
            for s in range(2):
                take_slot(pe, n + s)
                for kk in range(4):
                    m = by_rows(outs, 4 * s + kk, n + s, kk, 512, s + kk == 0, s + kk == 4)
                m.then_inc(weights_used, 1)
            return m

        def columns_product(pe, n, outs, w):
            for s in range(2):
                take_slot(pe, n + s)
                for kk in range(4):
                    for j, o in enumerate(outs):
                        m = by_columns(o, 4 * s + kk, n + s, kk, w, j * P, s + kk == 0, s + kk == 4)
                m.then_inc(weights_used, 1)

        def turn_pe(pe, s, c, src, n_k, first_bank=0, loaded=False):
            if not loaded:
                pe.wait_ge(rows_ready, TT * (call_base[s][c] + 1))
            for b in range((n_k + 1) // 2):
                for k in range(2 * b, min(2 * b + 2, n_k)):
                    for tt in range(TT):
                        at = (k % 2) * T + tt * P
                        m = nc.tensor.transpose(ps[:, first_bank + b, at:at + P], src[:, tt, k * P:(k + 1) * P], ident[:, :])
                m.then_inc(turned, 1)

        def turn_act(act, s, c, n_k, gain=None, first_bank=0, dst=None):
            dst = hth if dst is None else dst
            for b in range((n_k + 1) // 2):
                act.wait_ge(turned, bank_base[s][c] + b + 1)
                for k in range(2 * b, min(2 * b + 2, n_k)):
                    o = (k % 2) * T
                    g = 1.0 if gain is None else cols[:, gain + k:gain + k + 1]
                    m = nc.scalar.activation(dst[:, k, :], ps[:, first_bank + b, o:o + T], ACT.Copy, scale=g)
                m.then_inc(cols_high, 1)

        def turn_dve(dve, s, c, n_k, gain=None, first_bank=0, dst=None, dst_h=None):
            dst = htl if dst is None else dst
            dst_h = hth if dst_h is None else dst_h
            for b in range((n_k + 1) // 2):
                dve.wait_ge(cols_high, bank_base[s][c] + b + 1)
                for k in range(2 * b, min(2 * b + 2, n_k)):
                    o = (k % 2) * T
                    g = 1.0 if gain is None else cols[:, gain + k:gain + k + 1]
                    m = nc.vector.scalar_tensor_tensor(out=dst[:, k, :], in0=ps[:, first_bank + b, o:o + T], scalar=g,
                                                       in1=dst_h[:, k, :].bitcast(f32), op0=ALU.mult, op1=ALU.subtract)
                m.then_inc(cols_low, 1)

        def turned_by(pe, s, c, banks_n):
            pe.wait_ge(cols_low, bank_base[s][c] + banks_n)

        def norm_act(act, s, gain):
            for tt in range(TT):
                if s == 0:
                    act.wait_ge(x_loaded, 16 * TT)
                else:
                    act.wait_ge(x_ready, TT * (s - 1) + tt + 1)
                nc.scalar.activation(xn[:, tt, :], x[:, tt, :], ACT.Square, scale=1 / math.sqrt(D),
                                     accum_out=mean_sq[:, tt:tt + 1]).then_inc(sq_ready, 1)
            if gain is not None:
                turn_act(act, s, 0, KT, gain)

        def norm_pool(pool, s):
            for tt in range(TT):
                pool.wait_ge(sq_ready, TT * s + tt + 1)
                pool_link(pool, nc.gpsimd.tensor_scalar(mean_sq[:, tt:tt + 1], mean_sq[:, tt:tt + 1], EPS, None, ALU.add))
                nc.gpsimd.tensor_tensor(rstd[:, tt:tt + 1], mean_sq[:, tt:tt + 1], minus_half[:, 0:1], ALU.pow)\
                  .then_inc(rstd_ready, 1)

        def norm_dve(dve, s, gain):
            for tt in range(TT):
                dve.wait_ge(rstd_ready, TT * s + tt + 1)
                nc.vector.tensor_scalar(xn[:, tt, :], x[:, tt, :], rstd[:, tt:tt + 1], None, ALU.mult)\
                  .then_inc(rows_ready, 1)
            turn_dve(dve, s, 0, KT, gain)

        def add_result(dve, s, scale):
            dve_ahead.before(dve, base[s] + SLOTS_OF[PLAN[s]] - 1)
            dve.wait_ge(weights_used, base[s] + SLOTS_OF[PLAN[s]])
            for tt in range(TT):
                for half in range(2):
                    a = x[:, tt, half * 512:(half + 1) * 512]
                    m = nc.vector.scalar_tensor_tensor(out=a, in0=bank(4 + 2 * tt + half), scalar=scale, in1=a,
                                                       op0=ALU.mult, op1=ALU.add)
                m.then_inc(x_ready, 1)

        def ffn_load(sp, n, w_gate, w_up, w_down):
            g = w_gate.rearrange("(k p) n -> p k n", p=P)
            u = w_up.rearrange("(k p) n -> p k n", p=P)
            d = w_down.rearrange("(k p) n -> p k n", p=P)

            def gate_up(slot, half, c0):
                v = raw_view(slot, 4, 2 * HC)
                return [(v[:, :, 0:HC], g[:, 4 * half:4 * half + 4, bass.ds(c0, HC)]),
                        (v[:, :, HC:2 * HC], u[:, 4 * half:4 * half + 4, bass.ds(c0, HC)])]

            def down(slot, k0):
                v = raw_view(slot, 2, D)
                return [(v[:, j:j + 1, :], d[:, bass.ds(k0 + j, 1), :]) for j in range(2)]

            for j in range(2):
                load_slot(sp, n + j, gate_up(n + j, j, 0))
            with sp.Fori(0, NCH - 1) as i:
                for j in range(3):
                    sp.wait_ge(split_ready, i * 3 + (n + 2 + j - RING + 1))
                    pieces = gate_up(n + 2 + j, j, i * HC + HC) if j < 2 else down(n + 4, i * 2)
                    for dst, src in pieces:
                        sp.dma_start(dst, src).then_inc(raw_loaded[(n + 2 + j) % RING], 16)
            load_slot(sp, n + FFN_SLOTS - 1, down(n + FFN_SLOTS - 1, 2 * (NCH - 1)))

        def ffn_pe(pe, n, s, f):
            def gate_up(place, half):
                for kk in range(4):
                    m = by_rows([bank(0), bank(1)], 4 * half + kk, place, kk, 2 * HC, half + kk == 0, half + kk == 4)
                m.then_inc(weights_used, 1)

            def down(place, first, last):
                for kk in range(2):
                    for tt in range(TT):
                        h, l = prod_h[:, kk, tt * P:(tt + 1) * P], prod_l[:, kk, tt * P:(tt + 1) * P]
                        for half in range(2):
                            c = kk * D + half * 512
                            a, b = wh[:, place % RING, c:c + 512], wl[:, place % RING, c:c + 512]
                            o = bank(4 + 2 * tt + half)
                            nc.tensor.matmul(o, h, b, start=first and kk == 0, stop=False, skip_group_check=True)
                            nc.tensor.matmul(o, h, a, start=False, stop=False, skip_group_check=True)
                            m = nc.tensor.matmul(o, l, a, start=False, stop=last and kk == 1, skip_group_check=True)
                m.then_inc(weights_used, 1)

            def turn_product():
                for kk in range(2):
                    for tt in range(TT):
                        at = kk * T + tt * P
                        m = nc.tensor.transpose(ps[:, 2, at:at + P], prod[:, tt, kk * P:(kk + 1) * P], ident[:, :])
                m.then_inc(prod_turned, 1)

            def chunk(c, first):
                for half in range(2):
                    pe.wait_ge(split_ready, c * 3 + (n + half))
                    gate_up(n + 2 + half, half)
                pe.wait_ge(prod_low, c + f * NCH)
                pe.wait_ge(split_ready, c * 3 + (n + 2))
                down(n + 4, first, False)
                pe.wait_ge(prod_ready, c + (f * NCH + 1))
                turn_product()

            for half in range(2):
                turned_by(pe, s, 0, 2 * half + 2)
                take_slot(pe, n + half)
                gate_up(n + half, half)
            pe.wait_ge(prod_ready, f * NCH + 1)
            turn_product()
            chunk(1, True)
            with pe.Fori(2, NCH) as c:
                chunk(c, False)
            pe.wait_ge(prod_low, (f + 1) * NCH)
            take_slot(pe, n + FFN_SLOTS - 1)
            down(n + FFN_SLOTS - 1, False, True)

        def ffn_act(act, n, s, f):
            def silu(used):
                act.wait_ge(weights_used, used)
                for tt in range(TT):
                    nc.scalar.activation(silu_g[:, tt, :], ps[:, tt, 0:HC], ACT.Silu).then_inc(silu_ready, 1)

            def high(c):
                act.wait_ge(prod_turned, c + (f * NCH + 1))
                nc.scalar.activation(prod_h[:, :, :], bank(2).rearrange("p (k t) -> p k t", k=2), ACT.Copy)\
                  .then_inc(prod_high, 1)

            def split(c, j):
                r = (n + j) % RING
                act.wait_ge(raw_loaded[r], c * 32 + 32 * ((n + j) // RING + 1))
                act.wait_ge(weights_used, c * 3 + (n + j - RING + 1))
                nc.scalar.activation(wh[:, r, :], raw[:, r, :], ACT.Copy).then_inc(high_ready, 1)

            norm_act(act, s, FFN_GAIN[f])
            act_ahead.through(act, n + 3)
            silu(n + 2)
            high(0)
            with act.Fori(1, NCH - 1) as c:
                split(c, 1)
                split(c, 2)
                silu(c * 3 + (n + 1))
                split(c, 3)
                high(c)
            act_ahead.n += 3 * (NCH - 2)
            act_ahead.through(act, n + FFN_SLOTS - 1)
            silu(n + 3 * (NCH - 1) + 1)
            act_ahead.through(act, n + FFN_SLOTS)
            high(NCH - 1)
            act_ahead.before(act, n + FFN_SLOTS - 1)

        def ffn_dve(dve, n, s, f):
            def multiply(c):
                for tt in range(TT):
                    dve.wait_ge(silu_ready, c * TT + (f * NCH * TT + tt + 1))
                    m = nc.vector.tensor_tensor(prod[:, tt, :], ps[:, tt, HC:2 * HC], silu_g[:, tt, :], ALU.mult)
                m.then_inc(prod_ready, 1)

            def low(c):
                dve.wait_ge(prod_high, c + (f * NCH + 1))
                nc.vector.tensor_tensor(prod_l[:, :, :], bank(2).rearrange("p (k t) -> p k t", k=2),
                                        prod_h[:, :, :].bitcast(f32), ALU.subtract).then_inc(prod_low, 1)

            def split(c, j):
                r = (n + j) % RING
                dve.wait_ge(high_ready, c * 3 + (n + j + 1))
                nc.vector.tensor_tensor(wl[:, r, :], raw[:, r, :], wh[:, r, :].bitcast(f32), ALU.subtract)\
                  .then_inc(split_ready, 1)

            norm_dve(dve, s, FFN_GAIN[f])
            dve_ahead.through(dve, n + 3)
            multiply(0)
            low(0)
            with dve.Fori(1, NCH - 1) as c:
                split(c, 1)
                split(c, 2)
                multiply(c)
                split(c, 3)
                low(c)
            dve_ahead.n += 3 * (NCH - 2)
            dve_ahead.through(dve, n + FFN_SLOTS - 1)
            multiply(NCH - 1)
            dve_ahead.through(dve, n + FFN_SLOTS)
            low(NCH - 1)
            add_result(dve, s, 0.5 if f < 4 else 1.0)

        FFN_GAIN = [GAINS, GAINS + 2 * KT, GAINS + 5 * KT, GAINS + 7 * KT, FFN2]
        fs = {s: PLAN[:s].count("ffn") for s in range(len(PLAN))}

        ple_gate = Steps(sem("ple_act"), ["sigmoid", "squares0", "squares1"], 2)
        ple_vector = Steps(sem("ple_dve"), ["product0", "product1"], 2)
        ple_rstd = Steps(sem("ple_pool"), ["rstd0", "rstd1"], 2)
        p_loaded = sem("p_loaded")
        p_rows = arena[:, 0:TT * HC].rearrange("p (t n) -> p t n", t=TT)
        ple_sq = arena[:, 1024:1024 + TT * D].rearrange("p (t n) -> p t n", t=TT)
        ples = {s: PLAN[:s].count("ple") for s in range(len(PLAN))}

        def ple_load(sp, s, l):
            n = base[s]
            load_square(sp, n, io["ple_w_gate"][l])
            v = io["ple_w_proj"][l].rearrange("(k p) n -> p k n", p=P)
            load_slot(sp, n + 4, [(raw_view(n + 4, 2, D)[:, j:j + 1, :], v[:, j:j + 1, :]) for j in range(2)])

        def ple_pe(pe, s, l):
            n = base[s]
            turn_pe(pe, s, 0, xn, KT)
            pe.wait_ge(p_loaded, 16 * (l + 1))
            turned_by(pe, s, 0, 1)
            turn_pe(pe, s, 1, p_rows, 2, loaded=True)
            turned_by(pe, s, 0, 4)
            project_out(pe, n)
            turned_by(pe, s, 1, 1)
            take_slot(pe, n + 4)
            for kk in range(2):
                for tt in range(TT):
                    h, lo = prod_h[:, kk, tt * P:(tt + 1) * P], prod_l[:, kk, tt * P:(tt + 1) * P]
                    for half in range(2):
                        c = kk * D + half * 512
                        a, b = wh[:, (n + 4) % RING, c:c + 512], wl[:, (n + 4) % RING, c:c + 512]
                        o = bank(2 * tt + half)
                        nc.tensor.matmul(o, h, b, start=kk == 0, stop=False)
                        nc.tensor.matmul(o, h, a, start=False, stop=False)
                        m = nc.tensor.matmul(o, lo, a, start=False, stop=kk == 1)
            m.then_inc(weights_used, 1)

        def ple_act(act, s, l):
            n = base[s]
            norm_act(act, s, None)
            act.dma_start(gain_row[:, :], io["norm_gains"][l, 4:5, :].partition_broadcast(P)).then_inc(gain_loaded, 16)
            act.dma_start(p_rows, io["p"][l, 0].rearrange("(t p) n -> p t n", p=P)).then_inc(p_loaded, 16)
            turn_act(act, s, 0, KT, GAINS + (5 * l + 3) * KT)
            turn_act(act, s, 1, 2, dst=prod_h)
            act_ahead.before(act, n + 3)
            act.wait_ge(weights_used, n + 4)
            ple_gate.done(nc.scalar.activation(xn[:, :, :], ps[:, 4:8, :], ACT.Sigmoid), "sigmoid", l)
            act_ahead.before(act, n + 4)
            for tt in range(TT):
                act.wait_ge(ple_vector.sem, ple_vector.after(f"product{tt}", l))
                ple_gate.done(nc.scalar.activation(ple_sq[:, tt, :], xn[:, tt, :], ACT.Square, scale=1 / math.sqrt(D),
                                                   accum_out=mean_sq[:, tt:tt + 1]), f"squares{tt}", l)

        def ple_pool(pool, s, l):
            for tt in range(TT):
                pool.wait_ge(ple_gate.sem, ple_gate.after(f"squares{tt}", l))
                pool_link(pool, nc.gpsimd.tensor_scalar(mean_sq[:, tt:tt + 1], mean_sq[:, tt:tt + 1], EPS, None, ALU.add))
                ple_rstd.done(nc.gpsimd.tensor_tensor(rstd[:, tt:tt + 1], mean_sq[:, tt:tt + 1], minus_half[:, 0:1],
                                                      ALU.pow), f"rstd{tt}", l)

        def ple_dve(dve, s, l):
            n = base[s]
            norm_dve(dve, s, GAINS + (5 * l + 3) * KT)
            turn_dve(dve, s, 1, 2, dst=prod_l, dst_h=prod_h)
            dve_ahead.before(dve, n + 4)
            dve.wait_ge(ple_gate.sem, ple_gate.after("sigmoid", l))
            dve.wait_ge(weights_used, n + 5)
            for tt in range(TT):
                ple_vector.done(nc.vector.tensor_tensor(xn[:, tt, :], xn[:, tt, :], ps[:, 2 * tt:2 * tt + 2, :], ALU.mult),
                                f"product{tt}", l)
            dve.wait_ge(gain_loaded, 16 * (l + 1))
            for tt in range(TT):
                dve.wait_ge(ple_rstd.sem, ple_rstd.after(f"rstd{tt}", l))
                dve_link(dve, nc.vector.scalar_tensor_tensor(out=xn[:, tt, :], in0=xn[:, tt, :], scalar=rstd[:, tt:tt + 1],
                                                             in1=gain_row[:, :], op0=ALU.mult, op1=ALU.mult))
                nc.vector.tensor_tensor(x[:, tt, :], x[:, tt, :], xn[:, tt, :], ALU.add).then_inc(x_ready, 1)

        class Arena:
            def __init__(self):
                self.at = 0

            def __call__(self, n, pattern=None, **sizes):
                v = arena[:, self.at:self.at + n]
                self.at += n
                assert self.at <= arena.shape[1], self.at
                return v.rearrange(pattern, **sizes) if pattern else v

        def repeated(v, axis, n):
            v = v.unsqueeze(axis)
            return v.broadcast_to([n if i == axis else d for i, d in enumerate(v.shape)])

        H, BC, SB = 4, 64, 8
        NC, NB = T // BC, BC // SB
        AH, AD = 8, 64
        ar = Arena()
        e_f = ar(H * T, "p (h t) -> p h t", h=H)
        e_k = ar(H * T, "p (h t) -> p h t", h=H)
        e_b = ar(H * T, "p (h t) -> p h t", h=H)
        e_mid = ar(H * T, "p (h t) -> p h t", h=H)
        e_exp = ar(H * T, "p (h t) -> p h t", h=H)
        e_last = ar(H * T, "p (h t) -> p h t", h=H)
        e_qm = ar(H * T, "p (h t) -> p h t", h=H)
        e_q0 = ar(H * T, "p (h t) -> p h t", h=H)
        e_kd = [ar(NC * NB * BC, "p (c i s) -> p c i s", c=NC, i=NB) for _ in range(2)]
        e_reset = ar(H * T)
        e_v = ar(TT * 512, "p (t n) -> p t n", t=TT)
        e_keys = ar(TT * 512, "p (t n) -> p t n", t=TT)
        e_mask = silu_g[:, :, :].rearrange("p a b -> p (a b)").rearrange("p (n t) -> p n t", t=BC)
        e_scores = prod[:, :, :].rearrange("p a b -> p (a b)").rearrange("p (n t) -> p n t", t=BC)
        e_state = ar(3 * 512, "p (c h e) -> p c h e", c=3, h=H)
        e_u = ar(TT * 512, "p (t n) -> p t n", t=TT)
        e_av = ar(TT * 512, "p (t n) -> p t n", t=TT)
        e_g = ar(TT * 512, "p (t n) -> p t n", t=TT)
        e_ss = ar(16)
        e_rs = ar(16)
        e_os = ar(8)
        e_or = ar(8)
        e_w = e_keys.rearrange("p h t -> p (h t)").rearrange("p (h s) -> p h s", h=AH)
        e_wt = e_f.rearrange("p h t -> p (h t)").rearrange("p (h s) -> p h s", h=AH)
        e_sq = e_mid.rearrange("p h t -> p (h t)")
        e_o = e_reset.rearrange("p (t n) -> p t n", t=TT)
        EV_PE = Steps(sem("even_pe"), ["w_turned", "scores0", "scores1", "keys_turned", "scores2", "scores3", "deltas", "mixed", "o"])
        EV_ACT = Steps(sem("even_act"), ["sigmoid", "log", "exp_mid", "exp_b", "exp_last", "exp0", "v", "w_cols", "exp1", "av",
                                         "exp2", "u", "keys", "exp3", "g", "o_copied"])
        EV_DVE = Steps(sem("even_dve"), ["floor", "cum", "diff_mid", "diff_last", "decayed", "queries", "keys0", "keys1",
                                         "v_squares", "v_normed", "keys2", "keys3", "states", "masked", "o_squares"])
        EV_POOL = Steps(sem("even_pool"), ["reset", "w_masked", "diff0", "diff1", "zeros", "v_rstd", "diff2", "diff3", "o_rstd"])
        w_loaded = sem("gmlp_w_loaded")

        def even_load(sp, s):
            n, w = base[s], io["even_w_in"][0]
            for j, c0 in enumerate((1536, 1024, 2048, 512, 0, 2560)):
                load_columns(sp, n + 2 * j, w, c0, 512)
            load_square(sp, n + 12, io["even_w_out"][0])

        def flat(v):
            return v.rearrange("p h t -> p (h t)")

        middles = flat(e_b).rearrange("p (c i s) -> p c i s", i=NB, s=SB)[:, :, :, SB // 2 - 1]
        lasts = flat(e_b).rearrange("p (c s) -> p c s", s=BC)[:, :, BC - 1]

        def even_pe(pe, s):
            n = base[s]

            def scores(h):
                pe.wait_ge(EV_DVE.sem, EV_DVE.after(f"keys{h}"))
                for c in range(NC):
                    p0 = (c % 2) * BC
                    for i in range(NB):
                        o = (h * TT + c // 2) * BC + i * SB
                        m = nc.tensor.matmul(ps[p0:p0 + BC, 0, o:o + SB], e_kd[h % 2][:, c, i, :],
                                             e_qm[:, h, c * BC + i * SB:c * BC + (i + 1) * SB], start=True, stop=True)
                EV_PE.done(m, f"scores{h}")

            turn_pe(pe, s, 0, xn, KT)
            turned_by(pe, s, 0, 4)
            columns_product(pe, n, [bank(4 + h, T) for h in range(H)], 512)
            columns_product(pe, n + 2, [bank(h, T) for h in range(H)], 512)
            pe.wait_ge(EV_ACT.sem, EV_ACT.after("sigmoid"))
            rows_product(pe, n + 4, [bank(4), bank(5)])
            pe.wait_ge(EV_POOL.sem, EV_POOL.after("w_masked"))
            pe.wait_ge(EV_DVE.sem, EV_DVE.after("queries"))
            for h in range(AH):
                m = nc.tensor.transpose(ps[:, 2 + h // 4, (h % 4) * P:(h % 4 + 1) * P], e_w[:, h, :], ident[:, :])
            EV_PE.done(m, "w_turned")
            scores(0)
            rows_product(pe, n + 6, [bank(6), bank(7)])
            scores(1)
            pe.wait_ge(EV_ACT.sem, EV_ACT.after("w_cols"))
            for tt in range(TT):
                for h in range(H):
                    m = nc.tensor.transpose(ps[:, 1 + tt, h * P:(h + 1) * P], e_last[:, h, tt * P:(tt + 1) * P], ident[:, :])
            EV_PE.done(m, "keys_turned")
            pe.wait_ge(EV_ACT.sem, EV_ACT.after("v"))
            rows_product(pe, n + 8, [bank(4), bank(5)])
            scores(2)
            pe.wait_ge(EV_ACT.sem, EV_ACT.after("av"))
            rows_product(pe, n + 10, [bank(6), bank(7)])
            scores(3)
            pe.wait_ge(EV_ACT.sem, EV_ACT.after("keys"))
            for c, b in ((0, 3), (1, 1), (2, 2)):
                p0 = (c % 2) * BC
                for h in range(H):
                    m = nc.tensor.matmul(ps[:, b, h * P:(h + 1) * P], e_keys[p0:p0 + BC, c // 2, h * P:(h + 1) * P],
                                         e_v[p0:p0 + BC, c // 2, h * P:(h + 1) * P], start=True, stop=True)
            EV_PE.done(m, "deltas")
            pe.wait_ge(EV_DVE.sem, EV_DVE.after("v_normed"))
            pe.wait_ge(EV_ACT.sem, EV_ACT.after("u"))
            for h in range(AH):
                m = nc.tensor.matmul(ps[:, 4 + h // 4, (h % 4) * P:(h % 4 + 1) * P].rearrange("p (t d) -> p t d", t=TT),
                                     e_wt[:, h, :], e_av[:, :, h * AD:(h + 1) * AD], start=True, stop=True)
            EV_PE.done(m, "mixed")
            pe.wait_ge(EV_DVE.sem, EV_DVE.after("masked"))
            pe.wait_ge(EV_ACT.sem, EV_ACT.after("g"))
            for c in range(NC):
                p0, tt = (c % 2) * BC, c // 2
                for h in range(H):
                    o = ps[p0:p0 + BC, 6 + tt, h * P:(h + 1) * P]
                    m = nc.tensor.matmul(o, e_scores[p0:p0 + BC, h * TT + tt, :], e_v[p0:p0 + BC, tt, h * P:(h + 1) * P],
                                         start=True, stop=c == 0)
                    if c:
                        m = nc.tensor.matmul(o, e_q0[:, h, c * BC:(c + 1) * BC], e_state[:, c - 1, h, :], start=False, stop=True)
            EV_PE.done(m, "o")
            turn_pe(pe, s, 1, xn, KT)
            turned_by(pe, s, 1, 4)
            project_out(pe, n + 12)

        def even_act(act, s):
            n = base[s]
            norm_act(act, s, None)
            act.dma_start(e_w, io["gmlp_w_s"][0].rearrange("h t s -> t h s")).then_inc(w_loaded, 16)
            turn_act(act, s, 0, KT, GAINS + KT)
            act_ahead.before(act, n + 1)
            act.wait_ge(weights_used, n + 2)
            EV_ACT.done(nc.scalar.activation(e_f, ps[:, 4:8, 0:T], ACT.Sigmoid), "sigmoid")
            act.wait_ge(EV_DVE.sem, EV_DVE.after("floor"))
            EV_ACT.done(nc.scalar.activation(e_last, e_f, ACT.Ln), "log")
            act.wait_ge(EV_DVE.sem, EV_DVE.after("diff_mid"))
            EV_ACT.done(nc.scalar.activation(e_mid, e_mid, ACT.Exp), "exp_mid")
            EV_ACT.done(nc.scalar.activation(e_exp, e_b, ACT.Exp), "exp_b")
            act.wait_ge(EV_DVE.sem, EV_DVE.after("diff_last"))
            EV_ACT.done(nc.scalar.activation(e_last, e_last, ACT.Exp), "exp_last")

            def exp(h):
                act.wait_ge(EV_POOL.sem, EV_POOL.after(f"diff{h}"))
                EV_ACT.done(nc.scalar.activation(e_kd[h % 2], e_kd[h % 2], ACT.Exp), f"exp{h}")

            act_ahead.before(act, n + 3)
            exp(0)
            act_ahead.before(act, n + 5)
            act.wait_ge(weights_used, n + 6)
            EV_ACT.done(nc.scalar.activation(e_v, ps[:, 4:6, :], ACT.Copy), "v")
            act.wait_ge(EV_PE.sem, EV_PE.after("w_turned"))
            EV_ACT.done(nc.scalar.activation(e_wt, ps[:, 2:4, :], ACT.Copy), "w_cols")
            exp(1)
            act_ahead.before(act, n + 7)
            act.wait_ge(weights_used, n + 8)
            EV_ACT.done(nc.scalar.activation(e_av, ps[:, 6:8, :], ACT.Gelu_apprx_tanh), "av")
            exp(2)
            act_ahead.before(act, n + 9)
            act.wait_ge(weights_used, n + 10)
            EV_ACT.done(nc.scalar.activation(e_u, ps[:, 4:6, :], ACT.Gelu_apprx_tanh), "u")
            act.wait_ge(EV_PE.sem, EV_PE.after("keys_turned"))
            EV_ACT.done(nc.scalar.activation(e_keys, ps[:, 1:3, :], ACT.Copy), "keys")
            exp(3)
            act_ahead.before(act, n + 11)
            act.wait_ge(weights_used, n + 12)
            EV_ACT.done(nc.scalar.activation(e_g, ps[:, 6:8, :], ACT.Silu), "g")
            act.wait_ge(EV_PE.sem, EV_PE.after("o"))
            EV_ACT.done(nc.scalar.activation(e_o, ps[:, 6:8, :], ACT.Copy), "o_copied")
            turn_act(act, s, 1, KT)
            act_ahead.before(act, n + 15)

        def even_pool(pool, s):
            pool_link(pool, nc.gpsimd.memset(e_reset, 1.0))
            EV_POOL.done(nc.gpsimd.memset(e_reset.rearrange("p (c s) -> p c s", s=BC)[:, :, 0:1], 0.0), "reset")
            pool.wait_ge(w_loaded, 16)
            EV_POOL.done(nc.gpsimd.affine_select(out=e_w, in_=e_w, compare_op=ALU.is_ge, fill=0.0, base=0,
                                                 pattern=[[0, AH], [-1, P]], channel_multiplier=1), "w_masked")

            def diff(h):
                if h == 0:
                    pool.wait_ge(EV_DVE.sem, EV_DVE.after("cum"))
                if h >= 2:
                    pool.wait_ge(EV_PE.sem, EV_PE.after(f"scores{h - 2}"))
                mid = repeated(middles[:, h * NC:(h + 1) * NC, :], 3, BC)
                b = repeated(e_b[:, h, :].rearrange("p (c s) -> p c s", c=NC), 2, NB)
                EV_POOL.done(nc.gpsimd.tensor_tensor(e_kd[h % 2], mid, b, ALU.subtract), f"diff{h}")

            diff(0)
            diff(1)
            pool_link(pool, nc.gpsimd.memset(e_mask, 1.0))
            for p0 in (0, BC):
                v = e_mask[p0:p0 + BC, :, :]
                pool_link(pool, nc.gpsimd.affine_select(out=v, in_=v, compare_op=ALU.is_ge, fill=0.0, base=0,
                                                        pattern=[[0, H * TT], [1, BC]], channel_multiplier=-1))
            EV_POOL.done(nc.gpsimd.memset(e_scores, 0.0), "zeros")
            pool.wait_ge(EV_DVE.sem, EV_DVE.after("v_squares"))
            pool_link(pool, nc.gpsimd.tensor_scalar(e_ss, e_ss, 1.0 / AD, EPS, ALU.mult, ALU.add))
            EV_POOL.done(nc.gpsimd.tensor_tensor(e_rs, e_ss, minus_half[:, 0:16], ALU.pow), "v_rstd")
            diff(2)
            diff(3)
            pool.wait_ge(EV_DVE.sem, EV_DVE.after("o_squares"))
            pool_link(pool, nc.gpsimd.tensor_scalar(e_os, e_os, 1.0 / P, EPS, ALU.mult, ALU.add))
            EV_POOL.done(nc.gpsimd.tensor_tensor(e_or, e_os, minus_half[:, 0:8], ALU.pow), "o_rstd")

        def even_dve(dve, s):
            n = base[s]
            norm_dve(dve, s, GAINS + KT)
            dve_ahead.before(dve, n + 1)
            dve.wait_ge(EV_ACT.sem, EV_ACT.after("sigmoid"))
            for h in range(H):
                m = nc.vector.tensor_scalar(e_f[:, h, :], e_f[:, h, :], lb[:, 1, h:h + 1], lb[:, 0, h:h + 1], ALU.mult, ALU.add)
            dve_link(dve, m)
            nc.vector.tensor_scalar(e_k, e_f, -1.0, 1.0, ALU.mult, ALU.add)
            EV_DVE.done(nc.vector.tensor_scalar(e_f, e_f, 1e-6, None, ALU.max), "floor")
            dve.wait_ge(EV_ACT.sem, EV_ACT.after("log"))
            dve.wait_ge(EV_POOL.sem, EV_POOL.after("reset"))
            EV_DVE.done(nc.vector.tensor_tensor_scan(flat(e_b), e_reset, flat(e_last), 0.0, ALU.mult, ALU.add), "cum")
            dve.wait_ge(EV_DVE.sem, EV_DVE.after("cum"))
            b8 = flat(e_b).rearrange("p (c s) -> p c s", s=SB)
            mid = repeated(b8[:, :, SB // 2 - 1], 2, SB)
            EV_DVE.done(nc.vector.tensor_tensor(flat(e_mid).rearrange("p (c s) -> p c s", s=SB), b8, mid, ALU.subtract), "diff_mid")
            b64 = flat(e_b).rearrange("p (c s) -> p c s", s=BC)
            EV_DVE.done(nc.vector.tensor_tensor(flat(e_last).rearrange("p (c s) -> p c s", s=BC), repeated(lasts, 2, BC), b64,
                                                ALU.subtract), "diff_last")
            dve.wait_ge(EV_ACT.sem, EV_ACT.after("exp_last"))
            EV_DVE.done(nc.vector.tensor_tensor(e_last, e_last, e_k, ALU.mult), "decayed")
            dve_ahead.before(dve, n + 3)
            dve.wait_ge(weights_used, n + 4)
            nc.vector.tensor_tensor(e_q0, e_exp, ps[:, 0:4, 0:T], ALU.mult)
            EV_DVE.done(nc.vector.tensor_tensor(e_qm, e_mid, ps[:, 0:4, 0:T], ALU.mult), "queries")

            def keys(h):
                dve.wait_ge(EV_ACT.sem, EV_ACT.after(f"exp{h}"))
                k = repeated(e_k[:, h, :].rearrange("p (c s) -> p c s", c=NC), 2, NB)
                EV_DVE.done(nc.vector.tensor_tensor(e_kd[h % 2], e_kd[h % 2], k, ALU.mult), f"keys{h}")

            keys(0)
            dve_ahead.before(dve, n + 5)
            keys(1)
            dve_ahead.before(dve, n + 7)
            dve.wait_ge(EV_ACT.sem, EV_ACT.after("av"))
            dve_link(dve, nc.vector.tensor_tensor(e_sq, e_av.rearrange("p t n -> p (t n)"), e_av.rearrange("p t n -> p (t n)"), ALU.mult))
            EV_DVE.done(nc.vector.tensor_reduce(e_ss, e_sq.rearrange("p (n d) -> p n d", d=AD), AX.X, ALU.add), "v_squares")
            dve.wait_ge(EV_POOL.sem, EV_POOL.after("v_rstd"))
            av = e_av.rearrange("p t n -> p (t n)").rearrange("p (n d) -> p n d", d=AD)
            dve_link(dve, nc.vector.tensor_tensor(av, av, repeated(e_rs, 2, AD), ALU.mult))
            EV_DVE.done(nc.vector.tensor_tensor(e_av, e_av, repeated(vnorm[:, :], 1, TT), ALU.mult), "v_normed")
            keys(2)
            dve_ahead.before(dve, n + 9)
            keys(3)
            dve_ahead.before(dve, n + 11)
            dve.wait_ge(EV_PE.sem, EV_PE.after("deltas"))
            dve_link(dve, nc.vector.tensor_copy(e_state[:, 0, :, :], bank(3).rearrange("p (h e) -> p h e", h=H)))
            for c in (1, 2):
                for h in range(H):
                    m = nc.vector.scalar_tensor_tensor(out=e_state[:, c, h, :], in0=e_state[:, c - 1, h, :],
                                                       scalar=e_exp[:, h, c * BC + BC - 1:c * BC + BC],
                                                       in1=ps[:, c, h * P:(h + 1) * P], op0=ALU.mult, op1=ALU.add)
                if c == 1:
                    dve_link(dve, m)
            EV_DVE.done(m, "states")
            dve.wait_ge(EV_POOL.sem, EV_POOL.after("zeros"))
            EV_DVE.done(nc.vector.copy_predicated(e_scores, e_mask.bitcast(i32), bank(0).rearrange("p (n t) -> p n t", t=BC)), "masked")
            dve.wait_ge(EV_PE.sem, EV_PE.after("mixed"))
            for h in range(AH):
                o = slice(h * AD, (h + 1) * AD)
                nc.vector.scalar_tensor_tensor(out=xn[:, :, o], in0=ps[:, 4 + h // 4, (h % 4) * P:(h % 4 + 1) * P].rearrange("p (t d) -> p t d", t=TT),
                                               scalar=cols[:, BS + h:BS + h + 1], in1=e_u[:, :, o], op0=ALU.add, op1=ALU.mult)
            dve.wait_ge(EV_ACT.sem, EV_ACT.after("o_copied"))
            o8 = e_o.rearrange("p t n -> p (t n)").rearrange("p (n d) -> p n d", d=P)
            sq8 = e_sq.rearrange("p (n d) -> p n d", d=P)
            dve_link(dve, nc.vector.tensor_tensor(sq8, o8, o8, ALU.mult))
            EV_DVE.done(nc.vector.tensor_reduce(e_os, sq8, AX.X, ALU.add), "o_squares")
            dve_link(dve, nc.vector.tensor_tensor(o8, o8, repeated(onorm[:, :], 1, 8), ALU.mult))
            dve_link(dve, nc.vector.tensor_tensor(e_o, e_o, e_g, ALU.mult))
            dve.wait_ge(EV_POOL.sem, EV_POOL.after("o_rstd"))
            o4 = e_o.rearrange("p t (h d) -> p t h d", h=H)
            rs4 = repeated(e_or.rearrange("p (t h) -> p t h", t=TT), 3, P)
            nc.vector.tensor_tensor(xn[:, :, 512:1024].rearrange("p t (h d) -> p t h d", h=H), o4, rs4, ALU.mult)\
              .then_inc(rows_ready, TT)
            turn_dve(dve, s, 1, KT)
            add_result(dve, s, 1.0)

        class Attention:

            def __init__(self, name, heads, dv, parts, value, scale, o_bank, rows, probs, probs_t, small):
                self.heads, self.dv, self.parts, self.value, self.scale = heads, dv, parts, value, scale
                self.o_bank, self.rows, self.probs, self.probs_t, self.small = o_bank, rows, probs, probs_t, small
                hs = range(heads)
                names = ["scores0"]
                for h in hs:
                    names += [f"scores{h + 1}"] * (h + 1 < heads) + [f"turned{h}", f"output{h}"]
                self.pe_done = Steps(sem(name + "_attn_pe"), names)
                names = ["probs0"]
                for h in hs:
                    names += [f"probs{h + 1}"] * (h + 1 < heads) + [f"columns{h}"]
                self.act_done = Steps(sem(name + "_attn_act"), names)
                names = ["max0"]
                for h in hs:
                    names += [f"max{h + 1}"] * (h + 1 < heads) + [f"rows{h}"]
                self.dve_done = Steps(sem(name + "_attn_dve"), names)

            def pe(self, pe):
                def scores(h):
                    for qt in range(TT):
                        c0, w = qt * P, (qt + 1) * P
                        parts = self.parts(h)
                        for j, (q, k) in enumerate(parts):
                            m = nc.tensor.matmul(ps[:, 4 + h % 2, c0:c0 + w], q[:, qt * P:(qt + 1) * P], k[:, 0:w],
                                                 start=j == 0, stop=j == len(parts) - 1)
                    self.pe_done.done(m, f"scores{h}")

                scores(0)
                for h in range(self.heads):
                    if h + 1 < self.heads:
                        scores(h + 1)
                    pe.wait_ge(self.act_done.sem, self.act_done.after(f"probs{h}"))
                    for j in range(3):
                        m = nc.tensor.transpose(ps[:, 6 + h % 2, j * P:(j + 1) * P], self.probs[h % 2][:, j * P:(j + 1) * P],
                                                ident[:, :])
                    self.pe_done.done(m, f"turned{h}")
                    pe.wait_ge(self.act_done.sem, self.act_done.after(f"columns{h}"))
                    if h >= 2:
                        pe.wait_ge(self.dve_done.sem, self.dve_done.after(f"rows{h - 2}"))
                    o = [ps[:, self.o_bank + h % 2, qt * self.dv:(qt + 1) * self.dv] for qt in range(TT)]
                    pt = self.probs_t[h % 2]
                    nc.tensor.matmul(o[0], pt[:, 0:P], self.value(h, 0), start=True, stop=True)
                    nc.tensor.matmul(o[1], pt[:, P:2 * P], self.value(h, 0), start=True, stop=False)
                    m = nc.tensor.matmul(o[1], pt[:, 2 * P:3 * P], self.value(h, 1), start=False, stop=True)
                    self.pe_done.done(m, f"output{h}")

            def act(self, act):
                def probs(h):
                    act.wait_ge(self.dve_done.sem, self.dve_done.after(f"max{h}"))
                    pr, sm = self.probs[h % 2], self.small[h % 2]
                    nc.scalar.activation(pr[:, 0:P], pr[:, 0:P], ACT.Exp, bias=sm[:, 0:1], accum_out=sm[:, 2:3])
                    m = nc.scalar.activation(pr[:, P:3 * P], pr[:, P:3 * P], ACT.Exp, bias=sm[:, 1:2], accum_out=sm[:, 3:4])
                    self.act_done.done(m, f"probs{h}")

                probs(0)
                for h in range(self.heads):
                    if h + 1 < self.heads:
                        probs(h + 1)
                    act.wait_ge(self.pe_done.sem, self.pe_done.after(f"turned{h}"))
                    self.act_done.done(nc.scalar.activation(self.probs_t[h % 2], bank(6 + h % 2, 3 * P), ACT.Copy), f"columns{h}")

            def dve(self, dve):
                def maxima(h):
                    dve.wait_ge(self.pe_done.sem, self.pe_done.after(f"scores{h}"))
                    pr, sm = self.probs[h % 2], self.small[h % 2]
                    nc.vector.scalar_tensor_tensor(out=pr[:, 0:P], in0=ps[:, 4 + h % 2, 0:P], scalar=self.scale(h, 0),
                                                   in1=causal[:, 0:P], op0=ALU.mult, op1=ALU.add)
                    dve_link(dve, nc.vector.scalar_tensor_tensor(out=pr[:, P:3 * P], in0=ps[:, 4 + h % 2, P:3 * P],
                                                                 scalar=self.scale(h, 1), in1=causal[:, P:3 * P],
                                                                 op0=ALU.mult, op1=ALU.add))
                    nc.vector.tensor_reduce(sm[:, 0:1], pr[:, 0:P], AX.X, ALU.max, negate=True)
                    self.dve_done.done(nc.vector.tensor_reduce(sm[:, 1:2], pr[:, P:3 * P], AX.X, ALU.max, negate=True), f"max{h}")

                maxima(0)
                for h in range(self.heads):
                    if h + 1 < self.heads:
                        maxima(h + 1)
                    dve.wait_ge(self.pe_done.sem, self.pe_done.after(f"output{h}"))
                    sm = self.small[h % 2]
                    dve_link(dve, nc.vector.reciprocal(sm[:, 4:6], sm[:, 2:4]))
                    for qt in range(TT):
                        m = nc.vector.tensor_scalar(self.rows(h, qt), ps[:, self.o_bank + h % 2, qt * self.dv:(qt + 1) * self.dv],
                                                    sm[:, 4 + qt:5 + qt], None, ALU.mult)
                    self.dve_done.done(m, f"rows{h}")

        causal = silu_g[:, :, :].rearrange("p a b -> p (a b)")[:, 0:3 * P]

        def make_causal(pool):
            pool_link(pool, nc.gpsimd.memset(causal, 0.0))
            nc.gpsimd.affine_select(out=causal[:, 0:P], in_=causal[:, 0:P], compare_op=ALU.is_ge, fill=-1e30, base=0,
                                    pattern=[[-1, P]], channel_multiplier=1)
            return nc.gpsimd.affine_select(out=causal[:, 2 * P:3 * P], in_=causal[:, 2 * P:3 * P], compare_op=ALU.is_ge,
                                           fill=-1e30, base=0, pattern=[[-1, P]], channel_multiplier=1)

        MH, NOPE, ROPE, QL, KVL = 8, 128, 64, 384, 256
        QK = NOPE + ROPE
        ar = Arena()
        m_c = ar(TT * (QL + KVL), "p (t n) -> p t n", t=TT)
        m_kr = ar(TT * ROPE, "p (t n) -> p t n", t=TT)
        m_q = ar(TT * MH * QK, "p (t h d) -> p t h d", t=TT, h=MH)
        m_qr = ar(TT * MH * ROPE, "p (t h d) -> p t h d", t=TT, h=MH)
        m_k = ar(TT * MH * NOPE, "p (t h d) -> p t h d", t=TT, h=MH)
        m_krot = ar(TT * MH * ROPE, "p (t h d) -> p t h d", t=TT, h=MH)
        m_v = ar(TT * MH * NOPE, "p (t h d) -> p t h d", t=TT, h=MH)
        m_qt = ar(MH * T, "p (h t) -> p h t", h=MH)
        m_kt = ar(MH * T, "p (h t) -> p h t", h=MH)
        m_qrt = ar(MH // 2 * T, "p (h t) -> p h t", h=MH // 2)
        m_krt = ar(MH // 2 * T, "p (h t) -> p h t", h=MH // 2)
        m_pos = ar(TT)
        m_ang = ar(4 * 32, "p (a t f) -> p a t f", a=2, t=TT)
        m_n = ar(4 * 32, "p (a t f) -> p a t f", a=2, t=TT)
        m_cos = ar(4 * ROPE, "p (a t f) -> p a t f", a=2, t=TT)
        m_sin = ar(4 * ROPE, "p (a t f) -> p a t f", a=2, t=TT)
        m_css = ar(4)
        m_crs = ar(4)
        m_ss = ar(2 * TT * MH, "p (a t h) -> p a t h", a=2, t=TT)
        m_rs = ar(2 * TT * MH, "p (a t h) -> p a t h", a=2, t=TT)
        m_krs = ar(TT)
        m_small = [ar(6), ar(6)]
        m_sq = [m_qt.rearrange("p h t -> p (h t)"), m_kt.rearrange("p h t -> p (h t)")]
        m_tmp = xn[:, :, :].rearrange("p t n -> p (t n)")
        m_probs = [m_q.rearrange("p t h d -> p (t h d)")[:, j * 384:(j + 1) * 384] for j in range(2)]
        m_probs_t = [m_q.rearrange("p t h d -> p (t h d)")[:, (2 + j) * 384:(3 + j) * 384] for j in range(2)]
        m_ksq = m_tmp
        ML_PE = Steps(sem("mla_pe"), ["q_turned", "k_turned", "q_rope_turned", "k_rope_turned"])
        ML_ACT = Steps(sem("mla_act"), ["sin", "c0", "c1", "c_sq", "q0", "q1", "q2", "kv0", "q_sq", "k_sq", "q_cols", "q_rope_cols"])
        ML_DVE = Steps(sem("mla_dve"), ["angles", "kv1", "kr_sq", "squares", "q_rope", "k_scaled", "k_rope", "k_cols", "k_rope_cols"])
        ML_POOL = Steps(sem("mla_pool"), ["causal", "c_rstd", "rstd", "q_scale"])

        mla_attn = Attention(
            "mla", MH, NOPE,
            lambda h: [(m_qt[:, h, :], m_kt[:, h, :]),
                       (m_qrt[64 * (h % 2):64 * (h % 2) + 64, h // 2, :], m_krt[64 * (h % 2):64 * (h % 2) + 64, h // 2, :])],
            lambda h, t: m_v[:, t, h, :], lambda h, t: m_rs[:, 0, t, h:h + 1], 0,
            lambda h, t: xn[:, t, h * NOPE:(h + 1) * NOPE], m_probs, m_probs_t, m_small)

        def mla_load(sp, s):
            n = base[s]
            load_columns(sp, n, io["mla_w_in"][0], 0, 512)
            v = io["mla_w_in"][0].rearrange("(k p) n -> p k n", p=P)
            load_slot(sp, n + 2, [(raw_view(n + 2, 8, 192)[:, 4 * j:4 * j + 4, :], v[:, 4 * j:4 * j + 4, 512:704]) for j in range(2)])
            v = io["mla_w_q_b"][0].rearrange("(k p) n -> p k n", p=P)
            for c in range(3):
                load_slot(sp, n + 3 + c, [(raw_view(n + 3 + c, 3, 512)[:, a:b, :], v[:, a:b, c * 512:(c + 1) * 512])
                                          for a, b in ((0, 2), (2, 3))])
            v = io["mla_w_kv_b"][0].rearrange("(k p) n -> p k n", p=P)
            for c in range(2):
                load_slot(sp, n + 6 + c, [(raw_view(n + 6 + c, 2, D)[:, j:j + 1, :], v[:, j:j + 1, c * D:(c + 1) * D])
                                          for j in range(2)])
            load_square(sp, n + 8, io["mla_w_out"][0])

        def mla_pe(pe, s):
            n = base[s]
            turn_pe(pe, s, 0, xn, KT)
            turned_by(pe, s, 0, 4)
            rows_product(pe, n, [bank(0), bank(1)])
            take_slot(pe, n + 2)
            for k in range(KT):
                m = by_rows([bank(2, 192), bank(3, 192)], k, n + 2, k, 192, k == 0, k == KT - 1)
            m.then_inc(weights_used, 1)
            turn_pe(pe, s, 1, xn, 5)
            turned_by(pe, s, 1, 3)
            for c in range(3):
                if c == 2:
                    pe.wait_ge(ML_ACT.sem, ML_ACT.after("q0"))
                take_slot(pe, n + 3 + c)
                for k in range(3):
                    m = by_rows([bank(4 + 2 * (c % 2)), bank(5 + 2 * (c % 2))], k, n + 3 + c, k, 512, k == 0, k == 2)
                m.then_inc(weights_used, 1)
            for c in range(2):
                if c == 1:
                    pe.wait_ge(ML_ACT.sem, ML_ACT.after("q2"))
                take_slot(pe, n + 6 + c)
                for k in range(2):
                    for half in range(2):
                        m = by_rows([bank(4 * c + half), bank(4 * c + 2 + half)], 3 + k, n + 6 + c, k, D, k == 0, k == 1,
                                    off=half * 512, cols_n=512)
                m.then_inc(weights_used, 1)

            def turn(src, first_bank):
                for h in range(MH):
                    for tt in range(TT):
                        at = (h % 2) * T + tt * P
                        m = nc.tensor.transpose(ps[:, first_bank + h // 2, at:at + P], src[:, tt, h, 0:NOPE], ident[:, :])
                return m

            def turn_rope(src, first_bank):
                for h in range(MH // 2):
                    for tt in range(TT):
                        at = (h % 2) * T + tt * P
                        m = nc.tensor.transpose(ps[:, first_bank + h // 2, at:at + P],
                                                src[:, tt, 2 * h:2 * h + 2, :].rearrange("p h d -> p (h d)"), ident[:, :])
                return m

            pe.wait_ge(ML_ACT.sem, ML_ACT.after("kv0"))
            ML_PE.done(turn(m_q, 0), "q_turned")
            pe.wait_ge(ML_DVE.sem, ML_DVE.after("k_scaled"))
            ML_PE.done(turn(m_k, 4), "k_turned")
            pe.wait_ge(ML_ACT.sem, ML_ACT.after("q_cols"))
            ML_PE.done(turn_rope(m_qr, 0), "q_rope_turned")
            pe.wait_ge(ML_DVE.sem, ML_DVE.after("k_rope"))
            ML_PE.done(turn_rope(m_krot, 2), "k_rope_turned")
            pe.wait_ge(ML_ACT.sem, ML_ACT.after("q_rope_cols"))
            pe.wait_ge(ML_DVE.sem, ML_DVE.after("k_rope_cols"))
            mla_attn.pe(pe)
            turn_pe(pe, s, 2, xn, KT)
            turned_by(pe, s, 2, 4)
            project_out(pe, n + 8)

        def mla_act(act, s):
            n = base[s]
            norm_act(act, s, GAINS + (5 + 1) * KT)
            act.wait_ge(ML_DVE.sem, ML_DVE.after("angles"))
            ML_ACT.done(nc.scalar.activation(m_ang, m_ang, ACT.Sin), "sin")
            act_ahead.before(act, n + 1)
            act.wait_ge(weights_used, n + 2)
            ML_ACT.done(nc.scalar.activation(m_c[:, :, 0:512], ps[:, 0:2, :], ACT.Copy), "c0")
            act_ahead.before(act, n + 2)
            act.wait_ge(weights_used, n + 3)
            nc.scalar.activation(m_c[:, :, 512:640], ps[:, 2:4, 0:128], ACT.Copy)
            ML_ACT.done(nc.scalar.activation(m_kr, ps[:, 2:4, 128:192], ACT.Copy), "c1")
            act.wait_ge(ML_ACT.sem, ML_ACT.after("c1"))
            for j, (a, b) in enumerate(((0, QL), (QL, QL + KVL))):
                for tt in range(TT):
                    m = nc.scalar.activation(m_sq[j][:, tt * 512:tt * 512 + b - a], m_c[:, tt, a:b], ACT.Square,
                                             scale=1 / math.sqrt(b - a), accum_out=m_css[:, TT * j + tt:TT * j + tt + 1])
            ML_ACT.done(m, "c_sq")
            turn_act(act, s, 1, 5, QA)
            for c in range(3):
                act_ahead.before(act, n + 3 + c)
                act.wait_ge(weights_used, n + 4 + c)
                q = m_q.rearrange("p t h d -> p t (h d)")[:, :, c * 512:(c + 1) * 512]
                ML_ACT.done(nc.scalar.activation(q, ps[:, 4 + 2 * (c % 2):6 + 2 * (c % 2), :], ACT.Copy), f"q{c}")
            act_ahead.before(act, n + 6)
            act.wait_ge(weights_used, n + 7)
            kv = ps[:, 0:4, :].rearrange("p b n -> p (b n)").rearrange("p (t h d) -> p t h d", t=TT, h=4)
            nc.scalar.activation(m_k[:, :, 0:4, :], kv[:, :, :, 0:NOPE], ACT.Copy)
            ML_ACT.done(nc.scalar.activation(m_v[:, :, 0:4, :], kv[:, :, :, NOPE:2 * NOPE], ACT.Copy), "kv0")
            act_ahead.before(act, n + 7)
            act.wait_ge(ML_ACT.sem, ML_ACT.after("kv0"))
            for tt in range(TT):
                m = nc.scalar.activation(m_sq[tt][:, 0:MH * QK], m_q[:, tt, :, :].rearrange("p h d -> p (h d)"), ACT.Square)
            ML_ACT.done(m, "q_sq")
            act.wait_ge(ML_DVE.sem, ML_DVE.after("kv1"))
            ML_ACT.done(nc.scalar.activation(m_ksq, m_k.rearrange("p t h d -> p (t h d)"), ACT.Square), "k_sq")
            act.wait_ge(ML_PE.sem, ML_PE.after("q_turned"))
            act.wait_ge(ML_DVE.sem, ML_DVE.after("squares"))
            ML_ACT.done(nc.scalar.activation(m_qt, ps[:, 0:4, :], ACT.Copy, scale=cols[:, QN:QN + 1]), "q_cols")
            act.wait_ge(ML_PE.sem, ML_PE.after("q_rope_turned"))
            ML_ACT.done(nc.scalar.activation(m_qrt, ps[:, 0:2, :], ACT.Copy), "q_rope_cols")
            mla_attn.act(act)
            turn_act(act, s, 2, KT)
            act_ahead.before(act, n + 11)

        def mla_pool(pool, s):
            ML_POOL.done(make_causal(pool), "causal")
            pool.wait_ge(ML_ACT.sem, ML_ACT.after("c_sq"))
            pool_link(pool, nc.gpsimd.tensor_scalar(m_css, m_css, EPS, None, ALU.add))
            ML_POOL.done(nc.gpsimd.tensor_tensor(m_crs, m_css, minus_half[:, 0:4], ALU.pow), "c_rstd")
            pool.wait_ge(ML_DVE.sem, ML_DVE.after("squares"))
            for a in range(2):
                ss, rs = (v[:, a, :, :].rearrange("p t h -> p (t h)") for v in (m_ss, m_rs))
                pool_link(pool, nc.gpsimd.tensor_scalar(ss, ss, 1.0 / QK, EPS, ALU.mult, ALU.add))
                m = nc.gpsimd.tensor_tensor(rs, ss, minus_half[:, :], ALU.pow)
            ML_POOL.done(m, "rstd")
            pool.wait_ge(ML_POOL.sem, ML_POOL.after("rstd"))
            q = m_rs[:, 0, :, :].rearrange("p t h -> p (t h)")
            ML_POOL.done(nc.gpsimd.tensor_scalar(q, q, QK ** -0.5, None, ALU.mult), "q_scale")

        def mla_dve(dve, s):
            n = base[s]
            norm_dve(dve, s, GAINS + (5 + 1) * KT)
            dve_link(dve, nc.vector.tensor_copy(m_pos, pos_i[:, :]))
            for a in range(2):
                for tt in range(TT):
                    m = nc.vector.tensor_scalar(m_ang[:, a, tt, :], inv_freq[:, :], m_pos[:, tt:tt + 1], None, ALU.mult)
            dve_link(dve, m)
            for a in range(2):
                m = nc.vector.tensor_scalar(m_n[:, a, :, :], m_ang[:, a, :, :], 1 / (2 * math.pi), 0.25 * a, ALU.mult, ALU.add)
            dve_link(dve, m)
            dve_link(dve, nc.vector.tensor_scalar(m_n, m_n, 1.5 * 2 ** 23, None, ALU.add))
            dve_link(dve, nc.vector.tensor_scalar(m_n, m_n, -1.5 * 2 ** 23, None, ALU.add))
            rest, part = 2 * math.pi, 6.28125
            for _ in range(3):
                dve_link(dve, nc.vector.scalar_tensor_tensor(out=m_ang, in0=m_n, scalar=-part, in1=m_ang, op0=ALU.mult, op1=ALU.add))
                rest -= part
                part = math.ldexp(round(math.ldexp(rest, 20)), -20) if _ == 0 else rest
            dve_link(dve, nc.vector.tensor_scalar(m_ang[:, 1, :, :], m_ang[:, 1, :, :], math.pi / 2, None, ALU.add))
            ML_DVE.done(nc.vector.tensor_scalar(m_ang, m_ang, 3.1415925, -3.1415925, ALU.min, ALU.max), "angles")
            dve.wait_ge(ML_ACT.sem, ML_ACT.after("sin"))
            for a in range(2):
                for half in range(2):
                    f = slice(half * 32, half * 32 + 32)
                    other = slice(32 - half * 32, 64 - half * 32)
                    nc.vector.tensor_tensor(m_cos[:, a, :, f], m_ang[:, 1, :, :], repeated(qk_norm[:, a, f], 1, TT), ALU.mult)
                    m = nc.vector.tensor_tensor(m_sin[:, a, :, f], m_ang[:, 0, :, :], repeated(qk_norm[:, a, other], 1, TT), ALU.mult)
            dve_link(dve, m)
            dve_link(dve, nc.vector.tensor_scalar(m_sin[:, :, :, 0:32], m_sin[:, :, :, 0:32], -1.0, None, ALU.mult))
            dve_ahead.before(dve, n + 1)
            dve_ahead.before(dve, n + 2)
            dve.wait_ge(ML_POOL.sem, ML_POOL.after("c_rstd"))
            for j, (a, b) in enumerate(((0, QL), (QL, QL + KVL))):
                for tt in range(TT):
                    m = nc.vector.tensor_scalar(xn[:, tt, a:b], m_c[:, tt, a:b], m_crs[:, TT * j + tt:TT * j + tt + 1], None, ALU.mult)
            m.then_inc(rows_ready, TT)
            turn_dve(dve, s, 1, 5, QA)
            for c in range(3):
                dve_ahead.before(dve, n + 3 + c)
            dve_ahead.before(dve, n + 6)
            dve_ahead.before(dve, n + 7)
            dve.wait_ge(weights_used, n + 8)
            kv = ps[:, 4:8, :].rearrange("p b n -> p (b n)").rearrange("p (t h d) -> p t h d", t=TT, h=4)
            nc.vector.tensor_copy(m_k[:, :, 4:8, :], kv[:, :, :, 0:NOPE])
            ML_DVE.done(nc.vector.tensor_copy(m_v[:, :, 4:8, :], kv[:, :, :, NOPE:2 * NOPE]), "kv1")
            dve_link(dve, nc.vector.tensor_tensor(m_qr[:, :, 0, :], m_kr, m_kr, ALU.mult))
            ML_DVE.done(nc.vector.tensor_reduce(m_krs, m_qr[:, :, 0, :], AX.X, ALU.add), "kr_sq")
            dve.wait_ge(ML_ACT.sem, ML_ACT.after("q_sq"))
            for tt in range(TT):
                nc.vector.tensor_reduce(m_ss[:, 0, tt, :], m_sq[tt][:, 0:MH * QK].rearrange("p (h d) -> p h d", h=MH), AX.X, ALU.add)
            dve.wait_ge(ML_ACT.sem, ML_ACT.after("k_sq"))
            dve_link(dve, nc.vector.tensor_reduce(m_ss[:, 1, :, :].rearrange("p t h -> p (t h)"),
                                                  m_ksq.rearrange("p (n d) -> p n d", d=NOPE), AX.X, ALU.add))
            ML_DVE.done(nc.vector.tensor_tensor(m_ss[:, 1, :, :], m_ss[:, 1, :, :], repeated(m_krs, 2, MH), ALU.add), "squares")

            def rotate(dst, src, a, tmp):
                c, sn = m_cos[:, a, :, :], m_sin[:, a, :, :]
                nh = src.shape[2]
                nc.vector.tensor_tensor(tmp, src, repeated(c, 2, nh), ALU.mult)
                nc.vector.tensor_tensor(dst[:, :, :, 0:32], src[:, :, :, 32:64], repeated(sn[:, :, 0:32], 2, nh), ALU.mult)
                dve_link(dve, nc.vector.tensor_tensor(dst[:, :, :, 32:64], src[:, :, :, 0:32], repeated(sn[:, :, 32:64], 2, nh), ALU.mult))
                return nc.vector.tensor_tensor(dst, dst, tmp, ALU.add)

            tmp = m_tmp[:, 0:TT * MH * ROPE].rearrange("p (t h d) -> p t h d", t=TT, h=MH)
            ML_DVE.done(rotate(m_qr, m_q[:, :, :, NOPE:QK], 0, tmp), "q_rope")
            dve.wait_ge(ML_POOL.sem, ML_POOL.after("rstd"))
            ML_DVE.done(nc.vector.tensor_tensor(m_k, m_k, repeated(m_rs[:, 1, :, :], 3, NOPE), ALU.mult), "k_scaled")
            tmp1 = m_tmp[:, 1024:1024 + TT * ROPE].rearrange("p (t h d) -> p t h d", t=TT, h=1)
            rot = m_tmp[:, 1152:1152 + TT * ROPE].rearrange("p (t h d) -> p t h d", t=TT, h=1)
            dve_link(dve, rotate(rot, m_kr.unsqueeze(2), 1, tmp1))
            ML_DVE.done(nc.vector.tensor_tensor(m_krot, repeated(rot[:, :, 0, :], 2, MH), repeated(m_rs[:, 1, :, :], 3, ROPE), ALU.mult), "k_rope")
            dve.wait_ge(ML_PE.sem, ML_PE.after("k_turned"))
            ML_DVE.done(nc.vector.tensor_scalar(m_kt, ps[:, 4:8, :], cols[:, KN:KN + 1], None, ALU.mult), "k_cols")
            dve.wait_ge(ML_PE.sem, ML_PE.after("k_rope_turned"))
            ML_DVE.done(nc.vector.tensor_copy(m_krt, ps[:, 2:4, :]), "k_rope_cols")
            dve.wait_ge(ML_POOL.sem, ML_POOL.after("q_scale"))
            mla_attn.dve(dve)
            dve.wait_ge(mla_attn.dve_done.sem, mla_attn.dve_done.after(f"rows{MH - 1}"))
            dve.sem_inc(rows_ready, TT)
            turn_dve(dve, s, 2, KT)
            add_result(dve, s, 1.0)

        GH, GD = 6, 64
        SH, SD, SG, SN, CONV = 6, 64, 2, 128, 4
        SR = SH // SG
        XT = 7
        PADC, PADP = 4, 16
        ar = Arena()
        h_u = ar(TT * 1536, "p (t n) -> p t n", t=TT)
        h_x = ar(XT * (T + PADC), "p (k t) -> p k t", k=XT)
        h_c = ar(XT * T, "p (k t) -> p k t", k=XT)
        h_p = ar(2 * (T + PADP), "p (k t) -> p k t", k=2)
        h_sum = [ar(2 * (T + PADP), "p (k t) -> p k t", k=2) for _ in range(2)]
        h_diff = ar(2 * T, "p (k t) -> p k t", k=2)
        h_count = ar(2 * T, "p (k t) -> p k t", k=2)
        h_pw = ar(2 * P, "p (k d) -> p k d", k=2)
        h_tri = ar(P)
        h_neg = ar(P)
        h_decay = ar(TT * SH * P, "p (n l) -> p n l", l=P)
        h_xs = ar(TT * SH * SD, "p (t n) -> p t n", t=TT)
        h_xdt = ar(TT * SH * SD, "p (t n) -> p t n", t=TT)
        h_b = ar(SG * SN, "p (g n) -> p g n", g=SG)
        h_xw = ar(SH * SD)
        h_state = ar(SH * SD)
        h_qkt = ar(6 * T, "p (k t) -> p k t", k=6)
        h_y = ar(TT * SH * SD, "p (t n) -> p t n", t=TT)
        h_ysq = ar(TT * SH * SD, "p (t n) -> p t n", t=TT)
        h_z = ar(TT * SH * SD, "p (t n) -> p t n", t=TT)
        h_probs = [ar(3 * P) for _ in range(2)]
        h_probs_t = [ar(3 * P) for _ in range(2)]
        h_small = [ar(6), ar(6)]
        N12 = TT * SH
        h_raw, h_abs, h_e, h_s, h_s2, h_q, h_dt, h_da, h_acum, h_eacum = (ar(N12) for _ in range(10))
        h_ea = ar(SH)
        h_yss, h_yrs = ar(4), ar(4)
        HY_PE = Steps(sem("hyb_pe"), ["xs_turned", "cumulated", "cb_pool", "qk_turned", "state", "y"])
        HY_ACT = Steps(sem("hyb_act"), ["ea", "xa", "xb", "exp_dt", "conv", "u0", "xs_rows", "u1", "u2", "silu_z", "decay",
                                        "exp_acum", "qk_cols"])
        HY_DVE = Steps(sem("hyb_dve"), ["conv", "tail", "abs", "diff", "da", "xdt", "acum", "decay", "xw", "scores", "state", "y_off", "y_squares"])
        HY_POOL = Steps(sem("hyb_pool"), ["tri", "counts", "causal", "y_rstd"])
        pw_loaded = sem("pool_w_loaded")
        hyb_attn = Attention(
            "hyb", GH, GD,
            lambda h: [(h_qkt[64 * (h % 2):64 * (h % 2) + 64, h // 2, :], h_qkt[64 * (h % 2):64 * (h % 2) + 64, 3 + h // 2, :])],
            lambda h, t: h_u[:, t, 768 + h * GD:768 + (h + 1) * GD], lambda h, t: GD ** -0.5, 2,
            lambda h, t: xn[:, t, h * GD:(h + 1) * GD], h_probs, h_probs_t, h_small)

        def hybrid_load(sp, s):
            n, w = base[s], io["w_in_2"][0]
            load_columns(sp, n, w, 1536, 512)
            load_columns(sp, n + 2, w, 2048, 384)
            load_columns(sp, n + 4, w, 2432, 262)
            for j in range(3):
                load_columns(sp, n + 6 + 2 * j, w, 512 * j, 512)
            load_square(sp, n + 12, io["w_out_2"][0])

        def hybrid_pe(pe, s):
            n = base[s]
            turn_pe(pe, s, 0, xn, KT)
            turned_by(pe, s, 0, 4)
            columns_product(pe, n, [bank(4 + j, T) for j in range(4)], 512)
            columns_product(pe, n + 2, [bank(j, T) for j in range(3)], 384)
            pe.wait_ge(HY_ACT.sem, HY_ACT.after("xa"))
            for half in range(2):
                take_slot(pe, n + 4 + half)
                for kk in range(4):
                    k = 4 * half + kk
                    by_rows([bank(3, 6), bank(6, 6)], k, n + 4 + half, kk, 262, k == 0, k == KT - 1, cols_n=6)
                    for j in range(2):
                        m = by_columns(bank(4 + j, T), k, n + 4 + half, kk, 262, 6 + j * P, k == 0, k == KT - 1)
                m.then_inc(weights_used, 1)
            pe.wait_ge(HY_ACT.sem, HY_ACT.after("xb"))
            rows_product(pe, n + 6, [bank(0), bank(1)])
            pe.wait_ge(HY_ACT.sem, HY_ACT.after("conv"))
            pe.wait_ge(HY_DVE.sem, HY_DVE.after("tail"))
            for tt in range(TT):
                for k in range(3):
                    nc.tensor.transpose(ps[:, 2 + tt, k * P:(k + 1) * P], h_c[:, k, tt * P:(tt + 1) * P], ident[:, :])
            for g in range(SG):
                m = nc.tensor.transpose(ps[:, 2 + g, 3 * P:4 * P], h_c[:, 3 + g, 0:P], ident[:, :])
            HY_PE.done(m, "xs_turned")
            rows_product(pe, n + 8, [bank(4), bank(5)])
            rows_product(pe, n + 10, [bank(6), bank(7)])
            pe.wait_ge(HY_DVE.sem, HY_DVE.after("da"))
            pe.wait_ge(HY_ACT.sem, HY_ACT.after("xs_rows"))
            for tt in range(TT):
                for h in range(SH):
                    j = tt * SH + h
                    nc.tensor.matmul(ps[:, j // 4, (j % 4) * P:(j % 4 + 1) * P], h_da[:, j:j + 1].broadcast_to([P, P]), h_tri,
                                     start=True, stop=True)
            for tt in range(TT):
                m = nc.tensor.matmul(ps[:, 3, tt * SH:(tt + 1) * SH], h_tri, h_da[:, tt * SH:(tt + 1) * SH], start=True, stop=True)
            HY_PE.done(m, "cumulated")
            pe.wait_ge(HY_ACT.sem, HY_ACT.after("u1"))
            pe.wait_ge(HY_DVE.sem, HY_DVE.after("diff"))
            pe.wait_ge(pw_loaded, 32)
            for tt in range(TT):
                for g in range(SG):
                    o = (tt * SG + g) * P
                    nc.tensor.matmul(ps[:, 4, o:o + P], h_c[:, 3 + g, tt * P:(tt + 1) * P], h_c[:, 5 + g, tt * P:(tt + 1) * P],
                                     start=True, stop=True)
            for tt in range(TT):
                for k in range(2):
                    m = nc.tensor.matmul(ps[:, 5, (tt * 2 + k) * P:(tt * 2 + k + 1) * P],
                                         h_diff[:, k, tt * P:(tt + 1) * P], h_pw[:, k, :], start=True, stop=True)
            HY_PE.done(m, "cb_pool")
            pe.wait_ge(HY_ACT.sem, HY_ACT.after("u2"))
            pe.wait_ge(HY_DVE.sem, HY_DVE.after("acum"))
            for k in range(6):
                b = (6, 7, 3)[k // 2]
                for tt in range(TT):
                    at = (k % 2) * T + tt * P
                    m = nc.tensor.transpose(ps[:, b, at:at + P], h_u[:, tt, k * P:(k + 1) * P], ident[:, :])
            HY_PE.done(m, "qk_turned")
            pe.wait_ge(HY_DVE.sem, HY_DVE.after("xw"))
            for g in range(SG):
                c = slice(g * SR * SD, (g + 1) * SR * SD)
                m = nc.tensor.matmul(ps[:, 2, c], h_b[:, g, :], h_xw[:, c], start=True, stop=True)
            HY_PE.done(m, "state")
            pe.wait_ge(HY_DVE.sem, HY_DVE.after("scores"))
            for tt in range(TT):
                for h in range(SH):
                    c = slice(h * SD, (h + 1) * SD)
                    nc.tensor.matmul(ps[:, tt, c], h_decay[:, tt * SH + h, :], h_xdt[:, tt, c], start=True, stop=True)
            pe.wait_ge(HY_DVE.sem, HY_DVE.after("state"))
            pe.wait_ge(HY_ACT.sem, HY_ACT.after("qk_cols"))
            for g in range(SG):
                c = slice(g * SR * SD, (g + 1) * SR * SD)
                m = nc.tensor.matmul(ps[:, 3, c], h_c[:, 5 + g, P:T], h_state[:, c], start=True, stop=True)
            HY_PE.done(m, "y")
            pe.wait_ge(HY_DVE.sem, HY_DVE.after("y_off"))
            hyb_attn.pe(pe)
            turn_pe(pe, s, 1, xn, KT)
            turned_by(pe, s, 1, 4)
            project_out(pe, n + 12)

        def hybrid_act(act, s):
            n = base[s]
            norm_act(act, s, None)
            turn_act(act, s, 0, KT, MIX2)
            HY_ACT.done(nc.scalar.activation(h_ea, a_log[:, :], ACT.Exp), "ea")
            act_ahead.before(act, n + 1)
            act.wait_ge(weights_used, n + 2)
            HY_ACT.done(nc.scalar.activation(h_x[:, 0:4, PADC:PADC + T], ps[:, 4:8, 0:T], ACT.Copy), "xa")
            act_ahead.before(act, n + 3)
            act.wait_ge(weights_used, n + 4)
            HY_ACT.done(nc.scalar.activation(h_x[:, 4:7, PADC:PADC + T], ps[:, 0:3, 0:T], ACT.Copy), "xb")
            act_ahead.before(act, n + 5)
            act.wait_ge(HY_DVE.sem, HY_DVE.after("abs"))
            HY_ACT.done(nc.scalar.activation(h_e, h_abs, ACT.Exp, scale=-1.0), "exp_dt")
            for k in range(XT):
                m = nc.scalar.activation(h_c[:, k, :], h_c[:, k, :], ACT.Silu, bias=conv_cols[:, CONVB + k:CONVB + k + 1])
            HY_ACT.done(m, "conv")
            act_ahead.before(act, n + 7)
            act.wait_ge(weights_used, n + 8)
            HY_ACT.done(nc.scalar.activation(h_u[:, :, 0:512], ps[:, 0:2, :], ACT.Copy), "u0")
            act.wait_ge(HY_PE.sem, HY_PE.after("xs_turned"))
            nc.scalar.activation(h_xs, ps[:, 2:4, 0:3 * P], ACT.Copy)
            HY_ACT.done(nc.scalar.activation(h_b, ps[:, 2:4, 3 * P:4 * P], ACT.Copy), "xs_rows")
            act_ahead.before(act, n + 9)
            act.wait_ge(weights_used, n + 10)
            HY_ACT.done(nc.scalar.activation(h_u[:, :, 512:1024], ps[:, 4:6, :], ACT.Copy), "u1")
            act_ahead.before(act, n + 11)
            act.wait_ge(weights_used, n + 12)
            HY_ACT.done(nc.scalar.activation(h_u[:, :, 1024:1536], ps[:, 6:8, :], ACT.Copy), "u2")
            act.wait_ge(HY_ACT.sem, HY_ACT.after("u2"))
            HY_ACT.done(nc.scalar.activation(h_z, h_u[:, :, 1152:1536], ACT.Silu), "silu_z")
            act.wait_ge(HY_DVE.sem, HY_DVE.after("decay"))
            HY_ACT.done(nc.scalar.activation(h_decay, h_decay, ACT.Exp), "decay")
            HY_ACT.done(nc.scalar.activation(h_eacum, h_acum, ACT.Exp), "exp_acum")
            act.wait_ge(HY_PE.sem, HY_PE.after("qk_turned"))
            nc.scalar.activation(h_qkt[:, 0:4, :], ps[:, 6:8, :], ACT.Copy)
            HY_ACT.done(nc.scalar.activation(h_qkt[:, 4:6, :], ps[:, 3, :], ACT.Copy), "qk_cols")
            hyb_attn.act(act)
            turn_act(act, s, 1, KT)
            act_ahead.before(act, n + 15)

        def hybrid_pool(pool, s):
            pool_link(pool, nc.gpsimd.memset(h_pw, 0.0))
            for b in range(2):
                pool.dma_start(h_pw[64 * b:64 * b + 64, :, 64 * b:64 * b + 64],
                               io["pool_w_2"][0].rearrange("(a b) c d -> b c a d", b=2)[b]).then_inc(pw_loaded, 16)
            nc.gpsimd.memset(h_x[:, :, 0:PADC], 0.0)
            nc.gpsimd.memset(h_p[:, :, 0:PADP], 0.0)
            for j in range(2):
                nc.gpsimd.memset(h_sum[j][:, :, 0:PADP], 0.0)
            nc.gpsimd.memset(h_tri, 1.0)
            pool_link(pool, nc.gpsimd.memset(h_neg, 0.0))
            nc.gpsimd.affine_select(out=h_tri, in_=h_tri, compare_op=ALU.is_ge, fill=0.0, base=0, pattern=[[1, P]],
                                    channel_multiplier=-1)
            HY_POOL.done(nc.gpsimd.affine_select(out=h_neg, in_=h_neg, compare_op=ALU.is_ge, fill=-1e30, base=0,
                                                 pattern=[[1, P]], channel_multiplier=-1), "tri")
            pool_link(pool, nc.gpsimd.iota(h_count, pattern=[[0, 2], [1, T]], base=1, channel_multiplier=0,
                                           allow_small_or_imprecise_dtypes=True))
            for g, w in enumerate((2, 4, 8, 16)):
                v = h_count[64 * (g % 2):64 * (g % 2) + 64, g // 2, :]
                pool_link(pool, nc.gpsimd.tensor_scalar(v, v, float(w), None, ALU.min))
            HY_POOL.done(nc.gpsimd.memset(h_yss, 0.0), "counts")
            HY_POOL.done(make_causal(pool), "causal")
            pool.wait_ge(HY_DVE.sem, HY_DVE.after("y_squares"))
            pool_link(pool, nc.gpsimd.tensor_scalar(h_yss, h_yss, 1.0 / (SR * SD), EPS, ALU.mult, ALU.add))
            HY_POOL.done(nc.gpsimd.tensor_tensor(h_yrs, h_yss, minus_half[:, 0:4], ALU.pow), "y_rstd")

        def hybrid_dve(dve, s):
            n = base[s]
            norm_dve(dve, s, MIX2)
            dve_ahead.before(dve, n + 1)
            dve.wait_ge(HY_POOL.sem, HY_POOL.after("counts"))
            dve_link(dve, nc.vector.reciprocal(h_count, h_count))

            def convolve(k):
                for j in range(CONV):
                    w = conv_cols[:, CONVW + j * XT + k:CONVW + j * XT + k + 1]
                    v = h_x[:, k, PADC - CONV + 1 + j:PADC - CONV + 1 + j + T]
                    if j == 0:
                        m = nc.vector.tensor_scalar(h_c[:, k, :], v, w, None, ALU.mult)
                    else:
                        m = nc.vector.scalar_tensor_tensor(out=h_c[:, k, :], in0=v, scalar=w, in1=h_c[:, k, :], op0=ALU.mult, op1=ALU.add)
                    if j < CONV - 1:
                        dve_link(dve, m)
                return m

            dve.wait_ge(HY_ACT.sem, HY_ACT.after("xa"))
            for k in range(4):
                convolve(k)
            dve_ahead.before(dve, n + 3)
            dve.wait_ge(HY_ACT.sem, HY_ACT.after("xb"))
            for k in range(4, XT):
                m = convolve(k)
            HY_DVE.done(m, "conv")
            dve_ahead.before(dve, n + 5)
            dve.wait_ge(weights_used, n + 6)
            for tt in range(TT):
                nc.vector.tensor_tensor(h_raw[:, tt * SH:(tt + 1) * SH], bank(3 + 3 * tt, SH), dt_bias[:, :], ALU.add)
            HY_DVE.done(nc.vector.tensor_copy(h_p[:, :, PADP:PADP + T], ps[:, 4:6, 0:T]), "tail")
            dve.wait_ge(HY_DVE.sem, HY_DVE.after("tail"))
            HY_DVE.done(nc.vector.scalar_tensor_tensor(out=h_abs, in0=h_raw, scalar=-1.0, in1=h_raw, op0=ALU.mult, op1=ALU.max), "abs")

            src = h_p
            for g in range(4):
                dst, w = h_sum[g % 2], 2 ** g
                dve_link(dve, nc.vector.tensor_tensor(dst[:, :, PADP:PADP + T], src[:, :, PADP:PADP + T], src[:, :, PADP - w:PADP - w + T], ALU.add))
                rows = slice(64 * (g % 2), 64 * (g % 2) + 64)
                d = h_diff[rows, g // 2, :]
                dve_link(dve, nc.vector.tensor_tensor(d, dst[rows, g // 2, PADP:PADP + T], h_count[rows, g // 2, :], ALU.mult))
                m = nc.vector.tensor_tensor(d, d, h_p[rows, g // 2, PADP:PADP + T], ALU.subtract)
                src = dst
            HY_DVE.done(m, "diff")

            dve.wait_ge(HY_ACT.sem, HY_ACT.after("exp_dt"))
            dve_link(dve, nc.vector.tensor_scalar(h_s, h_e, 2.0, None, ALU.add))
            dve_link(dve, nc.vector.reciprocal(h_s, h_s))
            dve_link(dve, nc.vector.tensor_tensor(h_s, h_s, h_e, ALU.mult))
            dve_link(dve, nc.vector.tensor_tensor(h_s2, h_s, h_s, ALU.mult))
            dve_link(dve, nc.vector.tensor_scalar(h_q, h_s2, 1 / 17, None, ALU.mult))
            for d in (15, 13, 11, 9, 7, 5, 3):
                dve_link(dve, nc.vector.scalar_tensor_tensor(out=h_q, in0=h_q, scalar=1 / d, in1=h_s2, op0=ALU.add, op1=ALU.mult))
            dve_link(dve, nc.vector.scalar_tensor_tensor(out=h_q, in0=h_q, scalar=1.0, in1=h_s, op0=ALU.add, op1=ALU.mult))
            dve_link(dve, nc.vector.tensor_scalar(h_raw, h_raw, 0.0, None, ALU.max))
            dve_link(dve, nc.vector.scalar_tensor_tensor(out=h_dt, in0=h_q, scalar=2.0, in1=h_raw, op0=ALU.mult, op1=ALU.add))
            dve.wait_ge(HY_ACT.sem, HY_ACT.after("ea"))
            v2 = h_dt.rearrange("p (t h) -> p t h", t=TT)
            HY_DVE.done(nc.vector.scalar_tensor_tensor(out=h_da.rearrange("p (t h) -> p t h", t=TT), in0=v2, scalar=-1.0,
                                                       in1=repeated(h_ea, 1, TT), op0=ALU.mult, op1=ALU.mult), "da")
            dve_ahead.before(dve, n + 7)
            dve.wait_ge(HY_ACT.sem, HY_ACT.after("xs_rows"))
            xs = h_xs.rearrange("p t n -> p (t n)").rearrange("p (n d) -> p n d", d=SD)
            xdt = h_xdt.rearrange("p t n -> p (t n)").rearrange("p (n d) -> p n d", d=SD)
            HY_DVE.done(nc.vector.tensor_tensor(xdt, xs, repeated(h_dt, 2, SD), ALU.mult), "xdt")
            dve_ahead.before(dve, n + 9)
            dve_ahead.before(dve, n + 11)
            dve.wait_ge(HY_PE.sem, HY_PE.after("cumulated"))
            HY_DVE.done(nc.vector.tensor_copy(h_acum, bank(3, N12)), "acum")
            dve.wait_ge(HY_DVE.sem, HY_DVE.after("acum"))
            acb = ps[:, 0:3, :].rearrange("p b n -> p (b n)").rearrange("p (n l) -> p n l", l=P)
            dve_link(dve, nc.vector.tensor_tensor(h_decay, acb, repeated(h_acum, 2, P), ALU.subtract))
            HY_DVE.done(nc.vector.tensor_tensor(h_decay, h_decay, repeated(h_neg, 1, N12), ALU.add), "decay")
            dve.wait_ge(HY_PE.sem, HY_PE.after("cb_pool"))
            nc.vector.tensor_tensor(xn[:, :, 768:1024], bank(5).rearrange("p (t n) -> p t n", t=TT), repeated(pool_gain[:, :], 1, TT), ALU.mult)
            dve.wait_ge(HY_ACT.sem, HY_ACT.after("decay"))
            xw = h_xw.rearrange("p (h d) -> p h d", d=SD)
            HY_DVE.done(nc.vector.tensor_tensor(xw, xdt[:, 0:SH, :], repeated(h_decay[:, 0:SH, P - 1], 2, SD), ALU.mult), "xw")
            dve.wait_ge(HY_DVE.sem, HY_DVE.after("xw"))
            for tt in range(TT):
                cb = bank(4)[:, tt * SG * P:(tt + 1) * SG * P].rearrange("p (g l) -> p g l", g=SG)
                v = h_decay[:, tt * SH:(tt + 1) * SH, :].rearrange("p (g r) l -> p g r l", g=SG)
                m = nc.vector.tensor_tensor(v, v, repeated(cb, 2, SR), ALU.mult)
            HY_DVE.done(m, "scores")
            dve.wait_ge(HY_PE.sem, HY_PE.after("state"))
            HY_DVE.done(nc.vector.tensor_copy(h_state, bank(2, SH * SD)), "state")
            dve.wait_ge(HY_PE.sem, HY_PE.after("y"))
            dve.wait_ge(HY_ACT.sem, HY_ACT.after("exp_acum"))
            y = h_y.rearrange("p t n -> p (t n)").rearrange("p (n d) -> p n d", d=SD)
            dve_link(dve, skip(y, xs))
            dve_link(dve, nc.vector.tensor_tensor(h_y, h_y, ps[:, 0:2, 0:SH * SD], ALU.add))
            yo = h_ysq[:, 1, :].rearrange("p (h d) -> p h d", d=SD)
            HY_DVE.done(nc.vector.tensor_tensor(yo, bank(3, SH * SD).rearrange("p (h d) -> p h d", d=SD),
                                                repeated(h_eacum[:, SH:N12], 2, SD), ALU.mult), "y_off")
            dve.wait_ge(HY_DVE.sem, HY_DVE.after("y_off"))
            dve_link(dve, nc.vector.tensor_tensor(h_y[:, 1, :], h_y[:, 1, :], h_ysq[:, 1, :], ALU.add))
            dve.wait_ge(HY_ACT.sem, HY_ACT.after("silu_z"))
            dve_link(dve, nc.vector.tensor_tensor(h_y, h_y, h_z, ALU.mult))
            dve_link(dve, nc.vector.tensor_tensor(h_ysq, h_y, h_y, ALU.mult))
            HY_DVE.done(nc.vector.tensor_reduce(h_yss, h_ysq.rearrange("p t n -> p (t n)").rearrange("p (n d) -> p n d", d=SR * SD),
                                                AX.X, ALU.add), "y_squares")
            dve_link(dve, nc.vector.tensor_tensor(h_y, h_y, repeated(ssd_gain[:, :], 1, TT), ALU.mult))
            dve.wait_ge(HY_POOL.sem, HY_POOL.after("y_rstd"))
            nc.vector.tensor_tensor(xn[:, :, 384:768].rearrange("p t (g d) -> p t g d", g=SG),
                                    h_y.rearrange("p t (g d) -> p t g d", g=SG),
                                    repeated(h_yrs.rearrange("p (t g) -> p t g", t=TT), 3, SR * SD), ALU.mult)
            hyb_attn.dve(dve)
            dve.wait_ge(hyb_attn.dve_done.sem, hyb_attn.dve_done.after(f"rows{GH - 1}"))
            dve.sem_inc(rows_ready, TT)
            turn_dve(dve, s, 1, KT)
            add_result(dve, s, 1.0)

        def skip(y, xs):
            for tt in range(TT):
                m = nc.vector.tensor_tensor(y[:, tt * SH:(tt + 1) * SH, :], xs[:, tt * SH:(tt + 1) * SH, :],
                                            repeated(d_skip[:, :], 2, SD), ALU.mult)
            return m

        def load_params(q):
            def rows(dst, at, v):
                q.dma_start(dst[at:at + v.shape[0], :], v).then_inc(rows_loaded, 16)

            q.dma_start(pos_i[:, :], io["positions"].rearrange("o (t p) -> p (o t)", p=P),
                        allow_slow_non_contiguous=True).then_inc(params_loaded, 16)
            rows(rows_a, GAINS, io["norm_gains"].rearrange("l n (k p) -> (l n k) p", p=P))
            rows(rows_a, MIX2, io["norm_mix_2"].rearrange("o (k p) -> (o k) p", p=P))
            rows(rows_a, FFN2, io["norm_ffn_2"].rearrange("o (k p) -> (o k) p", p=P))
            rows(rows_a, QA, io["mla_q_a_norm"].rearrange("o (k p) -> (o k) p", p=P))
            rows(rows_a, KVA, io["mla_kv_a_norm"].rearrange("o (k p) -> (o k) p", p=P))
            rows(rows_a, BS, io["gmlp_b_s"].rearrange("o h p -> (o h) p"))
            rows(rows_a, LB, io["hgrn_lb_raw"].rearrange("o (k p) -> (o k) p", p=P))
            rows(rows_a, QN, io["mla_q_norm"][:, 0:P])
            rows(rows_a, KN, io["mla_k_norm"][:, 0:P])
            rows(rows_b, CONVW, io["conv_w_2"].rearrange("o w (k p) -> (o w k) p", p=P))
            rows(rows_b, CONVB, io["conv_b_2"].rearrange("o (k p) -> (o k) p", p=P))
            for dst, v in ((vnorm[:, :], io["gmlp_v_norm"].rearrange("o h d -> o (h d)")), (onorm[:, :], io["hgrn_out_norm"]),
                           (qk_norm[:, 0, :], io["mla_q_norm"][:, P:]), (qk_norm[:, 1, :], io["mla_k_norm"][:, P:]),
                           (ssd_gain[:, :], io["ssd_norm_2"]), (pool_gain[:, :], io["pool_scale_2"]), (dt_bias[:, :], io["dt_bias_2"]),
                           (a_log[:, :], io["a_log_2"]), (d_skip[:, :], io["d_skip_2"])):
                q.dma_start(dst, v.partition_broadcast(P)).then_inc(params_loaded, 16)
        ROWS_DMAS, PARAM_DMAS = 11, 10

        def final_dve(dve):
            last = len(PLAN)
            dve.wait_ge(gain_loaded, 16 * (PLAN.count("ple") + 1))
            for tt in range(TT):
                if last < 10:
                    nc.vector.tensor_copy(xn[:, tt, :], x[:, tt, :]).then_inc(rows_ready, 1)
                    continue
                dve.wait_ge(rstd_ready, TT * last + tt + 1)
                nc.vector.scalar_tensor_tensor(out=xn[:, tt, :], in0=x[:, tt, :], scalar=rstd[:, tt:tt + 1],
                                               in1=gain_row[:, :], op0=ALU.mult, op1=ALU.mult).then_inc(rows_ready, 1)

        block = stack.enter_context(nc.Block())

        @block.sync
        def _(sp):
            for tt in range(TT):
                sp.dma_start(x[:, tt, :], io["x"][0, tt * P:(tt + 1) * P, :]).then_inc(x_loaded, 16)
            for s, name in enumerate(PLAN):
                n, f = base[s], fs[s]
                if name == "even":
                    even_load(sp, s)
                if name == "mla":
                    mla_load(sp, s)
                if name == "hybrid":
                    hybrid_load(sp, s)
                if name == "ple":
                    ple_load(sp, s, ples[s])
                if name == "ffn":
                    if f < 4:
                        l, j = divmod(f, 2)
                        ffn_load(sp, n, io["ffn_w_gate"][l, j], io["ffn_w_up"][l, j], io["ffn_w_down"][l, j])
                    else:
                        gu = io["w_gate_up_2"][0]
                        ffn_load(sp, n, gu[:, 0:FF], gu[:, FF:2 * FF], io["w_down_2"][0])
            for tt in range(TT):
                sp.wait_ge(rows_ready, TT * calls_so_far + tt + 1)
                sp.dma_start(out[0, tt * P:(tt + 1) * P, :], xn[:, tt, :]).then_inc(stored, 16)
            sp.wait_ge(stored, 16 * TT)

        @block.gpsimd
        def _(pool):
            pool_link(pool, nc.gpsimd.memset(ident[:, :], 0.0))
            nc.gpsimd.affine_select(out=ident[:, :], in_=ident[:, :], compare_op=ALU.not_equal, fill=1.0, base=0,
                                    pattern=[[-1, P]], channel_multiplier=1).then_inc(ident_ready, 1)
            pool_link(pool, nc.gpsimd.memset(minus_half[:, :], -0.5))
            for j in range(32):
                m = nc.gpsimd.memset(inv_freq[:, j:j + 1], 10000.0 ** (-2 * j / 64))
            m.then_inc(consts_ready, 1)
            for s, name in enumerate(PLAN):
                norm_pool(pool, s)
                if name == "even":
                    even_pool(pool, s)
                if name == "mla":
                    mla_pool(pool, s)
                if name == "hybrid":
                    hybrid_pool(pool, s)
                if name == "ple":
                    ple_pool(pool, s, ples[s])
            norm_pool(pool, len(PLAN))

        @block.scalar
        def _(act):
            load_params(act)
            act.wait_ge(cols_turned, 1)
            nc.scalar.activation(cols[:, :], ps[:, 3, 0:ROWS_A], ACT.Copy).then_inc(cols_ready, 1)
            nc.scalar.activation(conv_cols[:, :], ps[:, 3, P:P + ROWS_B], ACT.Copy).then_inc(cols_ready, 1)
            act.wait_ge(cols_ready, 2)
            act.wait_ge(lb_steps, 1)
            nc.scalar.activation(lb[:, 1, :], lb[:, 0, :], ACT.Exp).then_inc(lb_steps, 1)
            for s, name in enumerate(PLAN):
                if name == "even":
                    even_act(act, s)
                if name == "mla":
                    mla_act(act, s)
                if name == "hybrid":
                    hybrid_act(act, s)
                if name == "ple":
                    ple_act(act, s, ples[s])
                if name == "ffn":
                    if s == len(PLAN) - 1:
                        act.wait_ge(x_ready, TT * s)
                        act.dma_start(gain_row[:, :], io["norm_final_2"].rearrange("(o n) -> o n", o=1).partition_broadcast(P))\
                           .then_inc(gain_loaded, 16)
                    ffn_act(act, base[s], s, fs[s])
            norm_act(act, len(PLAN), None)

        @block.vector
        def _(dve):
            dve.wait_ge(cols_ready, 2)
            dve.wait_ge(params_loaded, 16 * PARAM_DMAS)
            dve.wait_ge(consts_ready, 1)
            nc.vector.tensor_tensor(lb[:, 0, :], cols[:, LB:LB + 4], cols[:, LB:LB + 4], ALU.subtract).then_inc(lb_steps, 1)
            dve.wait_ge(lb_steps, 2)
            dve_link(dve, nc.vector.reciprocal(lb[:, 2, :], lb[:, 1, :]))
            dve_link(dve, nc.vector.tensor_tensor(lb[:, 2, :], lb[:, 2, :], lb[:, 1, :], ALU.mult))
            dve_link(dve, nc.vector.tensor_tensor(lb[:, 0, :], lb[:, 2, :], lb[:, 2, :], ALU.subtract))
            dve_link(dve, nc.vector.tensor_scalar(lb[:, 0, :], lb[:, 0, :], 0.0, 0.999, ALU.max, ALU.min))
            dve_link(dve, nc.vector.tensor_scalar(lb[:, 1, :], lb[:, 0, :], -1.0, 1.0, ALU.mult, ALU.add))
            for s, name in enumerate(PLAN):
                if name == "even":
                    even_dve(dve, s)
                if name == "mla":
                    mla_dve(dve, s)
                if name == "hybrid":
                    hybrid_dve(dve, s)
                if name == "ple":
                    ple_dve(dve, s, ples[s])
                if name == "ffn":
                    ffn_dve(dve, base[s], s, fs[s])
            final_dve(dve)

        @block.tensor
        def _(pe):
            pe.wait_ge(rows_loaded, 16 * ROWS_DMAS)
            pe.wait_ge(ident_ready, 1)
            nc.tensor.transpose(ps[:, 3, 0:ROWS_A], rows_a[0:ROWS_A, :], ident[0:ROWS_A, 0:ROWS_A])
            nc.tensor.transpose(ps[:, 3, P:P + ROWS_B], rows_b[0:ROWS_B, :], ident[0:ROWS_B, 0:ROWS_B]).then_inc(cols_turned, 1)
            pe.wait_ge(cols_ready, 2)
            for s, name in enumerate(PLAN):
                if name == "even":
                    even_pe(pe, s)
                if name == "mla":
                    mla_pe(pe, s)
                if name == "hybrid":
                    hybrid_pe(pe, s)
                if name == "ple":
                    ple_pe(pe, s, ples[s])
                if name == "ffn":
                    turn_pe(pe, s, 0, xn, KT)
                    ffn_pe(pe, base[s], s, fs[s])


INPUTS = ["x", "p", "positions", "norm_gains", "ffn_w_gate", "ffn_w_up", "ffn_w_down", "ple_w_gate", "ple_w_proj",
          "even_w_in", "gmlp_v_norm", "gmlp_w_s", "gmlp_b_s", "hgrn_lb_raw", "hgrn_out_norm", "even_w_out",
          "mla_w_in", "mla_q_a_norm", "mla_kv_a_norm", "mla_w_q_b", "mla_w_kv_b", "mla_q_norm", "mla_k_norm",
          "mla_w_out", "norm_mix_2", "w_in_2", "conv_w_2", "conv_b_2", "dt_bias_2", "a_log_2", "d_skip_2",
          "ssd_norm_2", "pool_w_2", "pool_scale_2", "w_out_2", "norm_ffn_2", "w_gate_up_2", "w_down_2", "norm_final_2"]


def kernel(**inputs):
    import numpy as np
    import concourse.bacc as bacc
    from concourse.bass_utils import run_bass_kernel_spmd

    nc = bacc.Bacc("TRN2", target_bir_lowering=False, num_devices=1)
    arrays, io = {}, {}
    for name in INPUTS:
        a = np.ascontiguousarray(inputs[name])
        arrays["in_" + name] = a
        io[name] = nc.dram_tensor("in_" + name, a.shape, mybir.dt.from_np(a.dtype), kind="ExternalInput").ap()
    out = nc.dram_tensor("out", inputs["x"].shape, mybir.dt.float32, kind="ExternalOutput").ap()
    build_block(nc, io, out)
    r = run_bass_kernel_spmd(nc, [arrays], core_ids=[0])
    return r.results[0]["out"]
```

```python
import math
from contextlib import ExitStack

import concourse.bass as bass
from concourse import mybir


class Steps:

    def __init__(self, sem, names, calls=1):
        self.sem, self.names, self.calls, self.said = sem, names, calls, 0

    def after(self, name, call=0):
        return call * len(self.names) + self.names.index(name) + 1

    def done(self, instruction, name, call=0):
        self.said += 1
        assert self.said == self.after(name, call), (name, self.names[(self.said - 1) % len(self.names)])
        instruction.then_inc(self.sem, 1)


def build_block(nc, io, out, stages=99, dump=None):
    f32, f32r, i32 = mybir.dt.float32, mybir.dt.float32r, mybir.dt.int32
    ALU, ACT, AX = mybir.AluOpType, mybir.ActivationFunctionType, mybir.AxisListType

    P = 128
    T, D = io["x"].shape[1:]
    TT = T // P
    KT = D // P
    FF = io["ffn_w_gate"].shape[3]
    HC = 256
    NCH = FF // HC
    EPS = 1e-6
    assert T == 256 and D == 1024 and FF % HC == 0

    SLOT = 2048
    RING = 3
    FFN_SLOTS = 3 * NCH
    PLAN = ["ffn", "even", "ffn", "ple", "ffn", "mla", "ffn", "ple", "hybrid", "ffn"][:stages]
    SLOTS_OF = {"ffn": FFN_SLOTS, "even": 16, "ple": 5, "mla": 12, "hybrid": 16}
    base, total = [], 0
    for name in PLAN:
        base.append(total)
        total += SLOTS_OF[name]

    FEATURES_OF = {"ffn": [KT], "even": [KT, KT], "ple": [KT, 2], "mla": [KT, 5, KT], "hybrid": [KT, KT]}
    features_base, banks_so_far, calls_so_far = [], 0, 0
    call_base, bank_base = [], []
    for name in PLAN:
        call_base.append([])
        bank_base.append([])
        for c, n in enumerate(FEATURES_OF[name]):
            call_base[-1].append(calls_so_far)
            bank_base[-1].append(banks_so_far)
            banks_so_far += (n + 1) // 2
            calls_so_far += c > 0 and name != "ple"

    GAINS, MIX2, FFN2, QA, KVA, BS, LB, QN, KN = 0, 80, 88, 96, 99, 101, 109, 113, 114
    ROWS_A = 115
    CONVW, CONVB, ROWS_B = 0, 28, 35

    with ExitStack() as stack:
        def sb(name, shape, dt=f32):
            return stack.enter_context(nc.sbuf_tensor(name, shape, dt))

        def sem(name):
            return stack.enter_context(nc.semaphore(name))

        raw = sb("raw", [P, RING, SLOT])
        wh = sb("wh", [P, RING, SLOT], f32r)
        wl = sb("wl", [P, RING, SLOT], f32r)
        x = sb("x_rows", [P, TT, D])
        xn = sb("xn", [P, TT, D])
        hth = sb("hth", [P, KT, T], f32r)
        htl = sb("htl", [P, KT, T], f32r)
        silu_g = sb("silu_g", [P, TT, HC])
        prod = sb("prod", [P, TT, HC])
        prod_h = sb("prod_h", [P, 2, T], f32r)
        prod_l = sb("prod_l", [P, 2, T], f32r)
        r_diag = silu_g[:, 0, :].rearrange("p (t n) -> p t n", t=TT)
        ident = sb("ident", [P, P])
        rows_a = sb("rows_a", [P, P])
        rows_b = sb("rows_b", [P, P])
        cols = sb("cols", [P, ROWS_A])
        conv_cols = sb("conv_cols", [P, ROWS_B])
        r_row = sb("r_row", [P, T])
        ones = sb("ones", [P, P])
        mean_sq = sb("mean_sq", [P, TT])
        rstd = sb("rstd", [P, TT])
        minus_half = sb("minus_half", [P, 16])
        gain_row = sb("gain_row", [P, D])
        vnorm = sb("vnorm", [P, 512])
        onorm = sb("onorm", [P, 128])
        qk_norm = sb("qk_norm", [P, 2, 64])
        ssd_gain = sb("ssd_gain", [P, 384])
        pool_gain = sb("pool_gain", [P, 256])
        dt_bias = sb("dt_bias", [P, 6])
        a_log = sb("a_log", [P, 6])
        d_skip = sb("d_skip", [P, 6])
        inv_freq = sb("inv_freq", [P, 32])
        pos_i = sb("pos_i", [P, TT], i32)
        lb = sb("lb", [P, 3, 4])
        arena = sb("arena", [P, 20040])
        ps = stack.enter_context(nc.psum_tensor("ps", [P, 8, 512], f32))

        def bank(b, w=512):
            return ps[:, b, 0:w]

        raw_loaded = [sem(f"raw_loaded{r}") for r in range(RING)]
        high_ready = sem("high_ready")
        split_ready = sem("split_ready")
        weights_used = sem("weights_used")
        x_loaded = sem("x_loaded")
        params_loaded = sem("params_loaded")
        rows_loaded = sem("rows_loaded")
        ident_ready = sem("ident_ready")
        consts_ready = sem("consts_ready")
        cols_turned = sem("cols_turned")
        cols_ready = sem("cols_ready")
        x_ready = sem("x_ready")
        half_ready = sem("half_ready")
        r_steps = sem("r_steps")
        sq_ready = sem("sq_ready")
        rstd_ready = sem("rstd_ready")
        rows_ready = sem("rows_ready")
        turned = sem("turned")
        cols_high = sem("cols_high")
        cols_low = sem("cols_low")
        silu_ready = sem("silu_ready")
        prod_ready = sem("prod_ready")
        prod_turned = sem("prod_turned")
        prod_high = sem("prod_high")
        prod_low = sem("prod_low")
        gain_loaded = sem("gain_loaded")
        stored = sem("stored")
        lb_steps = sem("lb_steps")
        act_chain, dve_chain, pool_chain = sem("act_chain"), sem("dve_chain"), sem("pool_chain")

        class Chain:

            def __init__(self, s):
                self.sem, self.n = s, 0

            def __call__(self, eng, instruction):
                self.n += 1
                instruction.then_inc(self.sem, 1)
                eng.wait_ge(self.sem, self.n)

        act_link, dve_link, pool_link = Chain(act_chain), Chain(dve_chain), Chain(pool_chain)

        def load_slot(sp, n, pieces):
            if n >= RING:
                sp.wait_ge(split_ready, n - RING + 1)
            assert len(pieces) == 2
            for dst, src in pieces:
                sp.dma_start(dst, src).then_inc(raw_loaded[n % RING], 16)

        def raw_view(n, k, w):
            return raw[:, n % RING, 0:k * w].rearrange("p (k n) -> p k n", k=k)

        width = [SLOT] * total
        for s, name in enumerate(PLAN):
            if name == "mla":
                width[base[s] + 2] = 8 * 192
                for j in range(3):
                    width[base[s] + 3 + j] = 3 * 512
            if name == "hybrid":
                for j in range(2):
                    width[base[s] + 2 + j] = 4 * 384
                    width[base[s] + 4 + j] = 4 * 262

        def split_high(act, n):
            act.wait_ge(raw_loaded[n % RING], 32 * (n // RING + 1))
            if n >= RING:
                act.wait_ge(weights_used, n - RING + 1)
            nc.scalar.activation(wh[:, n % RING, 0:width[n]], raw[:, n % RING, 0:width[n]], ACT.Copy)\
              .then_inc(high_ready, 1)

        def split_low(dve, n):
            dve.wait_ge(high_ready, n + 1)
            nc.vector.tensor_tensor(wl[:, n % RING, 0:width[n]], raw[:, n % RING, 0:width[n]],
                                    wh[:, n % RING, 0:width[n]].bitcast(f32), ALU.subtract)\
              .then_inc(split_ready, 1)

        class Ahead:

            def __init__(self, split):
                self.split, self.n = split, 0

            def through(self, eng, n):
                while self.n <= min(n, total - 1):
                    self.split(eng, self.n)
                    self.n += 1

            def before(self, eng, n):
                self.through(eng, n + RING - 1)

        act_ahead, dve_ahead = Ahead(split_high), Ahead(split_low)

        def take_slot(pe, n):
            pe.wait_ge(split_ready, n + 1)

        def product(o, xh, xl, a, b, first, last):
            nc.tensor.matmul(o, xh, b, start=first, stop=False)
            nc.tensor.matmul(o, xh, a, start=False, stop=False)
            return nc.tensor.matmul(o, xl, a, start=False, stop=last)

        def by_rows(outs, k, n, kk, w, first, last, off=0, cols_n=None):
            c = cols_n or w
            a, b = wh[:, n % RING, kk * w + off:kk * w + off + c], wl[:, n % RING, kk * w + off:kk * w + off + c]
            for tt in range(TT):
                m = product(outs[tt], hth[:, k, tt * P:(tt + 1) * P], htl[:, k, tt * P:(tt + 1) * P], a, b, first, last)
            return m

        def by_columns(o, k, n, kk, w, off, first, last):
            c = kk * w + off
            a, b = wh[:, n % RING, c:c + P], wl[:, n % RING, c:c + P]
            nc.tensor.matmul(o, b, hth[:, k, :], start=first, stop=False)
            nc.tensor.matmul(o, a, hth[:, k, :], start=False, stop=False)
            return nc.tensor.matmul(o, a, htl[:, k, :], start=False, stop=last)

        def project_out(pe, s, c, n, by_halves=True, rest=None):
            for j in range(4):
                take_slot(pe, n + j)
                turned_by(pe, s, c, j + 1)
                pieces = [(kk, half, tt) for kk in range(2) for half in range(2) for tt in range(TT)]
                if j == 3:
                    pieces.sort(key=lambda v: v[1] if by_halves else v[2])
                for i, (kk, half, tt) in enumerate(pieces):
                    k, at = 2 * j + kk, kk * D + half * 512
                    m = product(bank(4 + 2 * tt + half), hth[:, k, tt * P:(tt + 1) * P], htl[:, k, tt * P:(tt + 1) * P],
                                wh[:, (n + j) % RING, at:at + 512], wl[:, (n + j) % RING, at:at + 512], k == 0, k == KT - 1)
                    if j == 3 and i == 3:
                        m.then_inc(half_ready if by_halves else tile_ready, 1)
                    if j == 1 and i == 3 and rest is not None:
                        rest()
                m.then_inc(weights_used, 1)

        def load_square(sp, n, w):
            v = w.rearrange("(k p) n -> p k n", p=P)
            for s in range(4):
                load_slot(sp, n + s, [(raw_view(n + s, 2, D)[:, j:j + 1, :], v[:, 2 * s + j:2 * s + j + 1, :])
                                      for j in range(2)])

        def load_columns(sp, n, w, c0, c):
            v = w.rearrange("(k p) n -> p k n", p=P)
            for s in range(2):
                load_slot(sp, n + s, [(raw_view(n + s, 4, c)[:, 2 * j:2 * j + 2, :],
                                       v[:, 4 * s + 2 * j:4 * s + 2 * j + 2, c0:c0 + c]) for j in range(2)])

        def rows_product(pe, n, outs, first_of=None):
            for half in range(2):
                take_slot(pe, n + half)
                for kk in range(4):
                    if first_of is not None and kk % 2 == 0:
                        turned_by(pe, first_of, 0, 2 * half + kk // 2 + 1)
                    m = by_rows(outs, 4 * half + kk, n + half, kk, 512, half + kk == 0, half + kk == 4)
                m.then_inc(weights_used, 1)

        def columns_product(pe, n, outs, w, first_of=None):
            for half in range(2):
                take_slot(pe, n + half)
                for kk in range(4):
                    if first_of is not None and kk % 2 == 0:
                        turned_by(pe, first_of, 0, 2 * half + kk // 2 + 1)
                    for j, o in enumerate(outs):
                        m = by_columns(o, 4 * half + kk, n + half, kk, w, j * P, half + kk == 0, half + kk == 4)
                m.then_inc(weights_used, 1)

        def turn_bank(b, n_k, src, to):
            for k in range(2 * b, min(2 * b + 2, n_k)):
                for tt in range(TT):
                    at = (k % 2) * T + tt * P
                    m = nc.tensor.transpose(ps[:, to, at:at + P], src[:, tt, k * P:(k + 1) * P], ident[:, :])
            m.then_inc(turned, 1)

        def turn_pe(pe, s, c, src, n_k, loaded=False):
            if not loaded:
                pe.wait_ge(rows_ready, TT * (call_base[s][c] + 1))
            for b in range((n_k + 1) // 2):
                turn_bank(b, n_k, src, b)

        def turn_x(pe, s, b, to):
            if s == 0:
                pe.wait_ge(x_loaded, 16 * TT)
            else:
                pe.wait_ge(x_ready, 4 * (s - 1) + (4 if PLAN[s - 1] == "ple" else 2 * (b // 2 + 1)))
            turn_bank(b, KT, x, to)

        def turn_act(act, s, c, n_k, gain=None, banks=(0, 1, 2, 3), dst=None, part=None):
            dst = hth if dst is None else dst
            for b in range(*(part or (0, (n_k + 1) // 2))):
                act.wait_ge(turned, bank_base[s][c] + b + 1)
                for k in range(2 * b, min(2 * b + 2, n_k)):
                    o = (k % 2) * T
                    g = 1.0 if gain is None else cols[:, gain + k:gain + k + 1]
                    m = nc.scalar.activation(dst[:, k, :], ps[:, banks[b], o:o + T], ACT.Copy, scale=g)
                m.then_inc(cols_high, 1)

        def turn_dve(dve, s, c, n_k, gain=None, banks=(0, 1, 2, 3), dst=None, dst_h=None, part=None):
            dst = htl if dst is None else dst
            dst_h = hth if dst_h is None else dst_h
            for b in range(*(part or (0, (n_k + 1) // 2))):
                dve.wait_ge(cols_high, bank_base[s][c] + b + 1)
                for k in range(2 * b, min(2 * b + 2, n_k)):
                    o = (k % 2) * T
                    g = 1.0 if gain is None else cols[:, gain + k:gain + k + 1]
                    m = nc.vector.scalar_tensor_tensor(out=dst[:, k, :], in0=ps[:, banks[b], o:o + T], scalar=g,
                                                       in1=dst_h[:, k, :].bitcast(f32), op0=ALU.mult, op1=ALU.subtract)
                m.then_inc(cols_low, 1)

        def turned_by(pe, s, c, banks_n):
            pe.wait_ge(cols_low, bank_base[s][c] + banks_n)

        def norm_act(act, s, gain, banks=(0, 1, 2, 3)):
            if gain is not None:
                turn_act(act, s, 0, KT, gain, banks, part=(0, 2))
                act_ahead.through(act, base[s] + 1)
                turn_act(act, s, 0, KT, gain, banks, part=(2, 4))
            if s == 0:
                act.wait_ge(x_loaded, 16 * TT)
            else:
                act.wait_ge(x_ready, 4 * s)
            for tt in range(TT):
                nc.scalar.activation(xn[:, tt, :], x[:, tt, :], ACT.Square, scale=1 / math.sqrt(D),
                                     accum_out=mean_sq[:, tt:tt + 1]).then_inc(sq_ready, 1)

        def norm_pool(pool, s):
            for tt in range(TT):
                pool.wait_ge(sq_ready, TT * s + tt + 1)
                pool_link(pool, nc.gpsimd.tensor_scalar(mean_sq[:, tt:tt + 1], mean_sq[:, tt:tt + 1], EPS, None, ALU.add))
                nc.gpsimd.tensor_tensor(rstd[:, tt:tt + 1], mean_sq[:, tt:tt + 1], minus_half[:, 0:1], ALU.pow)\
                  .then_inc(rstd_ready, 1)

        def norm_dve(dve, s, gain, banks=(0, 1, 2, 3)):
            turn_dve(dve, s, 0, KT, gain, banks, part=(0, 2))
            dve_ahead.through(dve, base[s] + 1)
            turn_dve(dve, s, 0, KT, gain, banks, part=(2, 4))

        def rms(eng, s):
            eng.wait_ge(rstd_ready, TT * (s + 1))

        def rms_diagonals(dve, s, r):
            rms(dve, s)
            for tt in range(TT):
                m = nc.vector.tensor_scalar(r_diag[:, tt, :], ident[:, :], rstd[:, tt:tt + 1], None, ALU.mult)
            m.then_inc(r_steps, 1)

        def rms_row_pe(pe, r, b):
            pe.wait_ge(r_steps, 3 * r + 1)
            for tt in range(TT):
                m = nc.tensor.matmul(ps[:, b, tt * P:(tt + 1) * P], ones[:, :], r_diag[:, tt, :], start=True, stop=True)
            m.then_inc(r_steps, 1)

        def rms_row(dve, r, b):
            dve.wait_ge(r_steps, 3 * r + 2)
            nc.vector.tensor_copy(r_row[:, :], bank(b, T)).then_inc(r_steps, 1)
            dve.wait_ge(r_steps, 3 * r + 3)

        def add_result(dve, s, scale):
            dve_ahead.before(dve, base[s] + SLOTS_OF[PLAN[s]] - 1)
            for half in range(2):
                if half == 0:
                    dve.wait_ge(half_ready, len([p for p in PLAN[:s] if p != "ple"]) + 1)
                else:
                    dve.wait_ge(weights_used, base[s] + SLOTS_OF[PLAN[s]])
                for tt in range(TT):
                    a = x[:, tt, half * 512:(half + 1) * 512]
                    nc.vector.scalar_tensor_tensor(out=a, in0=bank(4 + 2 * tt + half), scalar=scale, in1=a,
                                                   op0=ALU.mult, op1=ALU.add).then_inc(x_ready, 1)

        def ffn_load(sp, n, w_gate, w_up, w_down):
            g = w_gate.rearrange("(k p) n -> p k n", p=P)
            u = w_up.rearrange("(k p) n -> p k n", p=P)
            d = w_down.rearrange("(k p) n -> p k n", p=P)

            def gate_up(slot, half, c0):
                v = raw_view(slot, 4, 2 * HC)
                return [(v[:, :, 0:HC], g[:, 4 * half:4 * half + 4, bass.ds(c0, HC)]),
                        (v[:, :, HC:2 * HC], u[:, 4 * half:4 * half + 4, bass.ds(c0, HC)])]

            def down(slot, k0):
                v = raw_view(slot, 2, D)
                return [(v[:, j:j + 1, :], d[:, bass.ds(k0 + j, 1), :]) for j in range(2)]

            for j in range(2):
                load_slot(sp, n + j, gate_up(n + j, j, 0))
            with sp.Fori(0, NCH - 1) as i:
                for j in range(3):
                    sp.wait_ge(split_ready, i * 3 + (n + 2 + j - RING + 1))
                    pieces = gate_up(n + 2 + j, j, i * HC + HC) if j < 2 else down(n + 4, i * 2)
                    for dst, src in pieces:
                        sp.dma_start(dst, src).then_inc(raw_loaded[(n + 2 + j) % RING], 16)
            load_slot(sp, n + FFN_SLOTS - 1, down(n + FFN_SLOTS - 1, 2 * (NCH - 1)))

        def ffn_pe(pe, n, s, f):
            def gate_up(place, k, b=0):
                m = by_rows([bank(b), bank(b + 1)], k, place, k % 4, 2 * HC, k == 0, k == KT - 1)
                if k % 4 == 3:
                    m.then_inc(weights_used, 1)

            def down(place, first, last, halfway=None):
                h, l = (last_h, last_l) if last else (prod_h, prod_l)
                pieces = [(kk, tt, half) for kk in range(2) for tt in range(TT) for half in range(2)]
                if last:
                    pieces.sort(key=lambda v: v[2])
                for i, (kk, tt, half) in enumerate(pieces):
                    at = kk * D + half * 512
                    m = product(bank(4 + 2 * tt + half), h[:, kk, tt * P:(tt + 1) * P], l[:, kk, tt * P:(tt + 1) * P],
                                wh[:, place % RING, at:at + 512], wl[:, place % RING, at:at + 512],
                                first and kk == 0, last and kk == 1)
                    if last and i == 3:
                        m.then_inc(half_ready, 1)
                    if halfway is not None and i == 3:
                        halfway()
                m.then_inc(weights_used, 1)

            def turn_product(b=2):
                for kk in range(2):
                    for tt in range(TT):
                        at = kk * T + tt * P
                        m = nc.tensor.transpose(ps[:, b, at:at + P], prod[:, tt, kk * P:(kk + 1) * P], ident[:, :])
                m.then_inc(prod_turned, 1)

            def chunk(c, first):
                for half in range(2):
                    pe.wait_ge(split_ready, c * 3 + (n + half))
                    for kk in range(4):
                        gate_up(n + 2 + half, 4 * half + kk)
                pe.wait_ge(prod_low, c + f * NCH)
                pe.wait_ge(split_ready, c * 3 + (n + 2))
                down(n + 4, first, False)
                pe.wait_ge(prod_ready, c + (f * NCH + 1))
                turn_product()

            turn_x(pe, s, 0, FFN_BANKS[0])
            turn_x(pe, s, 1, FFN_BANKS[1])
            take_slot(pe, n)
            for b in range(4):
                turned_by(pe, s, 0, b + 1)
                if b == 2:
                    take_slot(pe, n + 1)
                for k in (2 * b, 2 * b + 1):
                    gate_up(n + b // 2, k)
                if b == 0:
                    turn_x(pe, s, 2, FFN_BANKS[2])
                    turn_x(pe, s, 3, FFN_BANKS[3])
            for half in range(2):
                take_slot(pe, n + 2 + half)
                for kk in range(4):
                    gate_up(n + 2 + half, 4 * half + kk, 2)
                if half == 0:
                    pe.wait_ge(prod_ready, f * NCH + 1)
                    turn_product(0)
            pe.wait_ge(prod_low, f * NCH + 1)
            take_slot(pe, n + 4)
            down(n + 4, True, False)
            pe.wait_ge(prod_ready, f * NCH + 2)
            turn_product()
            with pe.Fori(2, NCH - 1) as c:
                chunk(c, False)

            def turn_last():
                pe.wait_ge(prod_ready, (f + 1) * NCH)
                turn_product()

            c = NCH - 1
            for half in range(2):
                take_slot(pe, n + 3 * c - 1 + half)
                for kk in range(4):
                    gate_up(n + 3 * c - 1 + half, 4 * half + kk)
            pe.wait_ge(prod_low, c + f * NCH)
            take_slot(pe, n + 3 * c + 1)
            down(n + 3 * c + 1, False, False, turn_last)
            pe.wait_ge(prod_low, (f + 1) * NCH)
            take_slot(pe, n + FFN_SLOTS - 1)
            down(n + FFN_SLOTS - 1, False, True)

        def ffn_act(act, n, s, f):
            def silu(used, b=0):
                act.wait_ge(weights_used, used)
                for tt in range(TT):
                    nc.scalar.activation(silu_g[:, tt, :], ps[:, b + tt, 0:HC], ACT.Silu, scale=rstd[:, tt:tt + 1]).then_inc(silu_ready, 1)

            def high(c, b=2, to=prod_h):
                act.wait_ge(prod_turned, c + (f * NCH + 1))
                nc.scalar.activation(to[:, :, :], bank(b).rearrange("p (k t) -> p k t", k=2), ACT.Copy)\
                  .then_inc(prod_high, 1)

            def split(c, j):
                r = (n + j) % RING
                act.wait_ge(raw_loaded[r], c * 32 + 32 * ((n + j) // RING + 1))
                act.wait_ge(weights_used, c * 3 + (n + j - RING + 1))
                nc.scalar.activation(wh[:, r, :], raw[:, r, :], ACT.Copy).then_inc(high_ready, 1)

            norm_act(act, s, FFN_GAIN[f], FFN_BANKS)
            act_ahead.through(act, n + 3)
            rms(act, s)
            silu(n + 2)
            act_ahead.through(act, n + 4)
            high(0, 0)
            act_ahead.through(act, n + 5)
            silu(n + 4, 2)
            act_ahead.through(act, n + 6)
            high(1)
            with act.Fori(2, NCH - 1) as c:
                split(c, 1)
                split(c, 2)
                silu(c * 3 + (n + 1))
                split(c, 3)
                high(c)
            act_ahead.n += 3 * (NCH - 3)
            act_ahead.through(act, n + FFN_SLOTS - 1)
            silu(n + 3 * (NCH - 1) + 1)
            act_ahead.through(act, n + FFN_SLOTS)
            high(NCH - 1, to=last_h)
            act_ahead.before(act, n + FFN_SLOTS - 1)

        def ffn_dve(dve, n, s, f):
            def multiply(c, b=0):
                for tt in range(TT):
                    dve.wait_ge(silu_ready, c * TT + (f * NCH * TT + tt + 1))
                    m = nc.vector.scalar_tensor_tensor(out=prod[:, tt, :], in0=ps[:, b + tt, HC:2 * HC], scalar=rstd[:, tt:tt + 1],
                                                       in1=silu_g[:, tt, :], op0=ALU.mult, op1=ALU.mult)
                m.then_inc(prod_ready, 1)

            def low(c, b=2, to=prod_l, high=prod_h):
                dve.wait_ge(prod_high, c + (f * NCH + 1))
                nc.vector.tensor_tensor(to[:, :, :], bank(b).rearrange("p (k t) -> p k t", k=2),
                                        high[:, :, :].bitcast(f32), ALU.subtract).then_inc(prod_low, 1)

            def split(c, j):
                r = (n + j) % RING
                dve.wait_ge(high_ready, c * 3 + (n + j + 1))
                nc.vector.tensor_tensor(wl[:, r, :], raw[:, r, :], wh[:, r, :].bitcast(f32), ALU.subtract)\
                  .then_inc(split_ready, 1)

            norm_dve(dve, s, FFN_GAIN[f], FFN_BANKS)
            dve_ahead.through(dve, n + 3)
            multiply(0)
            dve_ahead.through(dve, n + 4)
            low(0, 0)
            dve_ahead.through(dve, n + 5)
            multiply(1, 2)
            dve_ahead.through(dve, n + 6)
            low(1)
            with dve.Fori(2, NCH - 1) as c:
                split(c, 1)
                split(c, 2)
                multiply(c)
                split(c, 3)
                low(c)
            dve_ahead.n += 3 * (NCH - 3)
            dve_ahead.through(dve, n + FFN_SLOTS - 1)
            multiply(NCH - 1)
            dve_ahead.through(dve, n + FFN_SLOTS)
            low(NCH - 1, to=last_l, high=last_h)
            add_result(dve, s, 0.5 if f < 4 else 1.0)

        FFN_BANKS = (2, 3, 4, 6)
        last_h, last_l = hth[:, KT - 2:KT, :], htl[:, KT - 2:KT, :]
        FFN_GAIN = [GAINS, GAINS + 2 * KT, GAINS + 5 * KT, GAINS + 7 * KT, FFN2]
        fs = {s: PLAN[:s].count("ffn") for s in range(len(PLAN))}

        ple_gate = Steps(sem("ple_act"), ["sigmoid0", "squares0", "sigmoid1", "squares1"], 2)
        ple_vector = Steps(sem("ple_dve"), ["product0", "product1"], 2)
        ple_rstd = Steps(sem("ple_pool"), ["rstd0", "rstd1"], 2)
        p_loaded = sem("p_loaded")
        tile_ready = sem("tile_ready")
        p_rows = arena[:, 0:TT * HC].rearrange("p (t n) -> p t n", t=TT)
        ple_sq = arena[:, 1024:1024 + TT * D].rearrange("p (t n) -> p t n", t=TT)
        gained = arena[:, 5120:5120 + TT * D].rearrange("p (t n) -> p t n", t=TT)
        ple_ms = arena[:, 4096:4096 + TT]
        ple_rs = arena[:, 4100:4100 + TT]
        ples = {s: PLAN[:s].count("ple") for s in range(len(PLAN))}

        def ple_load(sp, s, l):
            n = base[s]
            v = io["ple_w_proj"][l].rearrange("(k p) n -> p k n", p=P)
            load_slot(sp, n, [(raw_view(n, 2, D)[:, j:j + 1, :], v[:, j:j + 1, :]) for j in range(2)])
            load_square(sp, n + 1, io["ple_w_gate"][l])

        def ple_pe(pe, s, l):
            n = base[s]
            for b in range(2):
                turn_x(pe, s, b, b)
            pe.wait_ge(p_loaded, 16 * (l + 1))
            for b in (2, 3):
                turn_x(pe, s, b, b)
            turn_bank(0, 2, p_rows, 4)
            turned_by(pe, s, 1, 1)
            take_slot(pe, n)
            for kk in range(2):
                for tt in range(TT):
                    for half in range(2):
                        c = kk * D + half * 512
                        m = product(bank(2 * tt + half), prod_h[:, kk, tt * P:(tt + 1) * P], prod_l[:, kk, tt * P:(tt + 1) * P],
                                    wh[:, n % RING, c:c + 512], wl[:, n % RING, c:c + 512], kk == 0, kk == 1)
            m.then_inc(weights_used, 1)
            project_out(pe, s, 0, n + 1, by_halves=False)

        def ple_act(act, s, l):
            n = base[s]
            act.wait_ge(x_ready, 4 * (s - 1))
            act.dma_start(gain_row[:, :], io["norm_gains"][l, 4:5, :].partition_broadcast(P)).then_inc(gain_loaded, 16)
            act.dma_start(p_rows, io["p"][l, 0].rearrange("(t p) n -> p t n", p=P)).then_inc(p_loaded, 16)
            turn_act(act, s, 0, KT, GAINS + (5 * l + 3) * KT)
            turn_act(act, s, 1, 2, banks=(4,), dst=prod_h)
            norm_act(act, s, None)
            rms(act, s)
            act_ahead.before(act, n + 4)
            for tt in range(TT):
                if tt == 0:
                    act.wait_ge(tile_ready, l + 1)
                else:
                    act.wait_ge(weights_used, n + 5)
                ple_gate.done(nc.scalar.activation(xn[:, tt, :], ps[:, 4 + 2 * tt:6 + 2 * tt, :], ACT.Sigmoid,
                                                   scale=rstd[:, tt:tt + 1]), f"sigmoid{tt}", l)
                act.wait_ge(ple_vector.sem, ple_vector.after(f"product{tt}", l))
                ple_gate.done(nc.scalar.activation(ple_sq[:, tt, :], xn[:, tt, :], ACT.Square, scale=1 / math.sqrt(D),
                                                   accum_out=ple_ms[:, tt:tt + 1]), f"squares{tt}", l)

        def ple_pool(pool, s, l):
            pool.wait_ge(gain_loaded, 16 * (l + 1))
            for tt in range(TT):
                pool.wait_ge(ple_gate.sem, ple_gate.after(f"squares{tt}", l))
                pool_link(pool, nc.gpsimd.tensor_scalar(ple_ms[:, tt:tt + 1], ple_ms[:, tt:tt + 1], EPS, None, ALU.add))
                ple_rstd.done(nc.gpsimd.tensor_tensor(ple_rs[:, tt:tt + 1], ple_ms[:, tt:tt + 1], minus_half[:, 0:1],
                                                      ALU.pow), f"rstd{tt}", l)

        def ple_dve(dve, s, l):
            n = base[s]
            norm_dve(dve, s, GAINS + (5 * l + 3) * KT)
            turn_dve(dve, s, 1, 2, banks=(4,), dst=prod_l, dst_h=prod_h)
            dve_ahead.before(dve, n + 4)
            dve.wait_ge(gain_loaded, 16 * (l + 1))
            for tt in range(TT):
                dve.wait_ge(ple_gate.sem, ple_gate.after(f"sigmoid{tt}", l))
                ple_vector.done(nc.vector.tensor_tensor(xn[:, tt, :], xn[:, tt, :], ps[:, 2 * tt:2 * tt + 2, :], ALU.mult),
                                f"product{tt}", l)
                dve.wait_ge(ple_vector.sem, ple_vector.after(f"product{tt}", l))
                nc.vector.tensor_tensor(gained[:, tt, :], xn[:, tt, :], gain_row[:, :], ALU.mult).then_inc(dve_chain, 1)
                dve_link.n += 1
            for tt in range(TT):
                dve.wait_ge(ple_rstd.sem, ple_rstd.after(f"rstd{tt}", l))
                dve.wait_ge(dve_chain, dve_link.n - 1 + tt)
                nc.vector.scalar_tensor_tensor(out=x[:, tt, :], in0=gained[:, tt, :], scalar=ple_rs[:, tt:tt + 1],
                                               in1=x[:, tt, :], op0=ALU.mult, op1=ALU.add).then_inc(x_ready, 2)

        class Arena:
            def __init__(self):
                self.at = 0

            def __call__(self, n, pattern=None, **sizes):
                v = arena[:, self.at:self.at + n]
                self.at += n
                assert self.at <= arena.shape[1], self.at
                return v.rearrange(pattern, **sizes) if pattern else v

        def repeated(v, axis, n):
            v = v.unsqueeze(axis)
            return v.broadcast_to([n if i == axis else d for i, d in enumerate(v.shape)])

        def scaled_rows(dst, b, func, w=512):
            for tt in range(TT):
                m = nc.scalar.activation(dst[:, tt, :], bank(b + tt, w), func, scale=rstd[:, tt:tt + 1])
            return m

        H, BC, SB = 4, 64, 8
        NC, NB = T // BC, BC // SB
        AH, AD = 8, 64
        ar = Arena()
        e_f = ar(H * T, "p (h t) -> p h t", h=H)
        e_k = ar(H * T, "p (h t) -> p h t", h=H)
        e_b = ar(H * T, "p (h t) -> p h t", h=H)
        e_mid = ar(H * T, "p (h t) -> p h t", h=H)
        e_exp = ar(H * T, "p (h t) -> p h t", h=H)
        e_last = ar(H * T, "p (h t) -> p h t", h=H)
        e_qm = ar(H * T, "p (h t) -> p h t", h=H)
        e_q0 = ar(H * T, "p (h t) -> p h t", h=H)
        e_kd = [ar(NC * NB * BC, "p (c i s) -> p c i s", c=NC, i=NB) for _ in range(2)]
        e_reset = ar(H * T)
        e_v = ar(TT * 512, "p (t n) -> p t n", t=TT)
        e_keys = ar(TT * 512, "p (t n) -> p t n", t=TT)
        e_mask = silu_g[:, :, :].rearrange("p a b -> p (a b)").rearrange("p (n t) -> p n t", t=BC)
        e_scores = prod[:, :, :].rearrange("p a b -> p (a b)").rearrange("p (n t) -> p n t", t=BC)
        e_state = ar(3 * 512, "p (c h e) -> p c h e", c=3, h=H)
        e_u = ar(TT * 512, "p (t n) -> p t n", t=TT)
        e_av = ar(TT * 512, "p (t n) -> p t n", t=TT)
        e_g = ar(TT * 512, "p (t n) -> p t n", t=TT)
        e_ss = ar(16)
        e_decay = ar(16)
        e_rs = ar(16)
        e_os = ar(8)
        e_or = ar(8)
        e_w = e_keys.rearrange("p h t -> p (h t)").rearrange("p (h s) -> p h s", h=AH)
        e_wt = e_f.rearrange("p h t -> p (h t)").rearrange("p (h s) -> p h s", h=AH)
        e_sq = e_mid.rearrange("p h t -> p (h t)")
        e_o = e_reset.rearrange("p (t n) -> p t n", t=TT)
        EV_PE = Steps(sem("even_pe"), ["w_turned", "scores0", "scores1", "keys_turned", "scores2", "scores3", "deltas", "mixed", "o"])
        EV_ACT = Steps(sem("even_act"), ["sigmoid", "log", "exp_mid", "exp_b", "exp_last", "exp0", "v", "w_cols", "exp1", "av",
                                         "exp2", "u", "keys", "exp3", "g", "o_copied", "o_squared"])
        EV_DVE = Steps(sem("even_dve"), ["f", "floor", "cum", "diff_mid", "diff_last", "decayed", "queries", "keys0", "keys1",
                                         "v_squares", "v_normed", "keys2", "keys3", "states", "masked", "o_squares"])
        EV_POOL = Steps(sem("even_pool"), ["reset", "w_masked", "diff0", "diff1", "zeros", "v_rstd", "diff2", "diff3", "gate", "o_rstd"])
        w_loaded = sem("gmlp_w_loaded")

        def even_load(sp, s):
            n, w = base[s], io["even_w_in"][0]
            for j, c0 in enumerate((1536, 1024, 2048, 512, 0, 2560)):
                load_columns(sp, n + 2 * j, w, c0, 512)
            load_square(sp, n + 12, io["even_w_out"][0])

        def flat(v):
            return v.rearrange("p h t -> p (h t)")

        middles = flat(e_b).rearrange("p (c i s) -> p c i s", i=NB, s=SB)[:, :, :, SB // 2 - 1]
        lasts = flat(e_b).rearrange("p (c s) -> p c s", s=BC)[:, :, BC - 1]

        def even_pe(pe, s):
            n = base[s]

            def scores(h):
                pe.wait_ge(EV_DVE.sem, EV_DVE.after(f"keys{h}"))
                for c in range(NC):
                    p0 = (c % 2) * BC
                    for i in range(NB):
                        o = (h * TT + c // 2) * BC + i * SB
                        m = nc.tensor.matmul(ps[p0:p0 + BC, 0, o:o + SB], e_kd[h % 2][:, c, i, :],
                                             e_qm[:, h, c * BC + i * SB:c * BC + (i + 1) * SB], start=True, stop=True)
                EV_PE.done(m, f"scores{h}")

            for b in range(4):
                turn_x(pe, s, b, b)
            columns_product(pe, n, [bank(4 + h, T) for h in range(H)], 512, first_of=s)
            rms_row_pe(pe, 0, 0)
            pe.wait_ge(r_steps, 3)
            columns_product(pe, n + 2, [bank(h, T) for h in range(H)], 512)
            pe.wait_ge(EV_DVE.sem, EV_DVE.after("f"))
            rows_product(pe, n + 4, [bank(4), bank(5)])
            pe.wait_ge(EV_POOL.sem, EV_POOL.after("w_masked"))
            pe.wait_ge(EV_DVE.sem, EV_DVE.after("queries"))
            for h in range(AH):
                m = nc.tensor.transpose(ps[:, 2 + h // 4, (h % 4) * P:(h % 4 + 1) * P], e_w[:, h, :], ident[:, :])
            EV_PE.done(m, "w_turned")
            scores(0)
            rows_product(pe, n + 6, [bank(6), bank(7)])
            scores(1)
            pe.wait_ge(EV_ACT.sem, EV_ACT.after("w_cols"))
            for tt in range(TT):
                for h in range(H):
                    m = nc.tensor.transpose(ps[:, 1 + tt, h * P:(h + 1) * P], e_last[:, h, tt * P:(tt + 1) * P], ident[:, :])
            EV_PE.done(m, "keys_turned")
            pe.wait_ge(EV_ACT.sem, EV_ACT.after("v"))
            rows_product(pe, n + 8, [bank(4), bank(5)])
            scores(2)
            pe.wait_ge(EV_ACT.sem, EV_ACT.after("av"))
            rows_product(pe, n + 10, [bank(6), bank(7)])
            scores(3)
            pe.wait_ge(EV_ACT.sem, EV_ACT.after("keys"))
            for c, b in ((0, 3), (1, 1), (2, 2)):
                p0 = (c % 2) * BC
                for h in range(H):
                    m = nc.tensor.matmul(ps[:, b, h * P:(h + 1) * P], e_keys[p0:p0 + BC, c // 2, h * P:(h + 1) * P],
                                         e_v[p0:p0 + BC, c // 2, h * P:(h + 1) * P], start=True, stop=True)
            EV_PE.done(m, "deltas")
            pe.wait_ge(EV_DVE.sem, EV_DVE.after("v_normed"))
            pe.wait_ge(EV_ACT.sem, EV_ACT.after("u"))
            for h in range(AH):
                m = nc.tensor.matmul(ps[:, 4 + h // 4, (h % 4) * P:(h % 4 + 1) * P].rearrange("p (t d) -> p t d", t=TT),
                                     e_wt[:, h, :], e_av[:, :, h * AD:(h + 1) * AD], start=True, stop=True)
            EV_PE.done(m, "mixed")
            pe.wait_ge(EV_DVE.sem, EV_DVE.after("masked"))
            pe.wait_ge(EV_ACT.sem, EV_ACT.after("g"))
            for c in range(NC):
                p0, tt = (c % 2) * BC, c // 2
                for h in range(H):
                    o = ps[p0:p0 + BC, 6 + tt, h * P:(h + 1) * P]
                    m = nc.tensor.matmul(o, e_scores[p0:p0 + BC, h * TT + tt, :], e_v[p0:p0 + BC, tt, h * P:(h + 1) * P],
                                         start=True, stop=c == 0)
                    if c:
                        m = nc.tensor.matmul(o, e_q0[:, h, c * BC:(c + 1) * BC], e_state[:, c - 1, h, :], start=False, stop=True)
            EV_PE.done(m, "o")
            pe.wait_ge(rows_ready, TT * call_base[s][1] + 1)
            turn_bank(0, KT, xn, 0)
            turn_bank(1, KT, xn, 1)
            pe.wait_ge(EV_ACT.sem, EV_ACT.after("o_copied"))

            def turn_rest():
                pe.wait_ge(rows_ready, TT * (call_base[s][1] + 1))
                turn_bank(2, KT, xn, 2)
                turn_bank(3, KT, xn, 3)

            project_out(pe, s, 1, n + 12, rest=turn_rest)

        def even_act(act, s):
            n = base[s]
            act.wait_ge(x_ready, 4 * (s - 1))
            act.dma_start(e_w, io["gmlp_w_s"][0].rearrange("h t s -> t h s")).then_inc(w_loaded, 16)
            norm_act(act, s, GAINS + KT)
            act_ahead.before(act, n + 1)
            act.wait_ge(EV_DVE.sem, EV_DVE.after("f"))
            EV_ACT.done(nc.scalar.activation(e_f, e_f, ACT.Sigmoid), "sigmoid")
            act_ahead.before(act, n + 2)
            act.wait_ge(EV_DVE.sem, EV_DVE.after("floor"))
            EV_ACT.done(nc.scalar.activation(e_last, e_f, ACT.Ln), "log")
            act.wait_ge(EV_DVE.sem, EV_DVE.after("diff_mid"))
            EV_ACT.done(nc.scalar.activation(e_mid, e_mid, ACT.Exp), "exp_mid")
            EV_ACT.done(nc.scalar.activation(e_exp, e_b, ACT.Exp), "exp_b")
            act.wait_ge(EV_DVE.sem, EV_DVE.after("diff_last"))
            EV_ACT.done(nc.scalar.activation(e_last, e_last, ACT.Exp), "exp_last")

            def exp(h):
                act.wait_ge(EV_POOL.sem, EV_POOL.after(f"diff{h}"))
                EV_ACT.done(nc.scalar.activation(e_kd[h % 2], e_kd[h % 2], ACT.Exp), f"exp{h}")

            act_ahead.before(act, n + 3)
            exp(0)
            act_ahead.before(act, n + 5)
            rms(act, s)
            act.wait_ge(weights_used, n + 6)
            EV_ACT.done(scaled_rows(e_v, 4, ACT.Copy), "v")
            act.wait_ge(EV_PE.sem, EV_PE.after("w_turned"))
            EV_ACT.done(nc.scalar.activation(e_wt, ps[:, 2:4, :], ACT.Copy), "w_cols")
            exp(1)
            act_ahead.before(act, n + 7)
            act.wait_ge(weights_used, n + 8)
            EV_ACT.done(scaled_rows(e_av, 6, ACT.Gelu_apprx_tanh), "av")
            exp(2)
            act_ahead.before(act, n + 9)
            act.wait_ge(weights_used, n + 10)
            EV_ACT.done(scaled_rows(e_u, 4, ACT.Gelu_apprx_tanh), "u")
            act.wait_ge(EV_PE.sem, EV_PE.after("keys_turned"))
            EV_ACT.done(nc.scalar.activation(e_keys, ps[:, 1:3, :], ACT.Copy), "keys")
            exp(3)
            act_ahead.before(act, n + 11)
            act.wait_ge(weights_used, n + 12)
            EV_ACT.done(scaled_rows(e_g, 6, ACT.Silu), "g")
            act.wait_ge(EV_PE.sem, EV_PE.after("o"))
            EV_ACT.done(nc.scalar.activation(e_o, ps[:, 6:8, :], ACT.Copy), "o_copied")
            act.wait_ge(EV_DVE.sem, EV_DVE.after("v_squares"))
            act.wait_ge(EV_ACT.sem, EV_ACT.after("o_copied"))
            EV_ACT.done(nc.scalar.activation(e_sq, e_o.rearrange("p t n -> p (t n)"), ACT.Square), "o_squared")
            turn_act(act, s, 1, KT, part=(0, 2))
            act_ahead.before(act, n + 12)
            turn_act(act, s, 1, KT, part=(2, 4))
            act_ahead.before(act, n + 15)

        def even_pool(pool, s):
            pool_link(pool, nc.gpsimd.memset(e_reset, 1.0))
            EV_POOL.done(nc.gpsimd.memset(e_reset.rearrange("p (c s) -> p c s", s=BC)[:, :, 0:1], 0.0), "reset")
            pool.wait_ge(w_loaded, 16)
            EV_POOL.done(nc.gpsimd.affine_select(out=e_w, in_=e_w, compare_op=ALU.is_ge, fill=0.0, base=0,
                                                 pattern=[[0, AH], [-1, P]], channel_multiplier=1), "w_masked")

            def diff(h):
                if h == 0:
                    pool.wait_ge(EV_DVE.sem, EV_DVE.after("cum"))
                if h >= 2:
                    pool.wait_ge(EV_PE.sem, EV_PE.after(f"scores{h - 2}"))
                mid = repeated(middles[:, h * NC:(h + 1) * NC, :], 3, BC)
                b = repeated(e_b[:, h, :].rearrange("p (c s) -> p c s", c=NC), 2, NB)
                EV_POOL.done(nc.gpsimd.tensor_tensor(e_kd[h % 2], mid, b, ALU.subtract), f"diff{h}")

            diff(0)
            diff(1)
            pool_link(pool, nc.gpsimd.memset(e_mask, 1.0))
            for p0 in (0, BC):
                v = e_mask[p0:p0 + BC, :, :]
                pool_link(pool, nc.gpsimd.affine_select(out=v, in_=v, compare_op=ALU.is_ge, fill=0.0, base=0,
                                                        pattern=[[0, H * TT], [1, BC]], channel_multiplier=-1))
            EV_POOL.done(nc.gpsimd.memset(e_scores, 0.0), "zeros")
            pool.wait_ge(EV_DVE.sem, EV_DVE.after("v_squares"))
            pool_link(pool, nc.gpsimd.tensor_scalar(e_ss, e_ss, 1.0 / AD, EPS, ALU.mult, ALU.add))
            EV_POOL.done(nc.gpsimd.tensor_tensor(e_rs, e_ss, minus_half[:, 0:16], ALU.pow), "v_rstd")
            diff(2)
            diff(3)
            pool.wait_ge(EV_ACT.sem, EV_ACT.after("g"))
            g8 = e_g.rearrange("p t n -> p (t n)").rearrange("p (n d) -> p n d", d=P)
            EV_POOL.done(nc.gpsimd.tensor_tensor(g8, g8, repeated(onorm[:, :], 1, 8), ALU.mult), "gate")
            pool.wait_ge(EV_DVE.sem, EV_DVE.after("o_squares"))
            pool_link(pool, nc.gpsimd.tensor_scalar(e_os, e_os, 1.0 / P, EPS, ALU.mult, ALU.add))
            EV_POOL.done(nc.gpsimd.tensor_tensor(e_or, e_os, minus_half[:, 0:8], ALU.pow), "o_rstd")

        def even_dve(dve, s):
            n = base[s]
            norm_dve(dve, s, GAINS + KT)
            rms_diagonals(dve, s, 0)
            dve_ahead.before(dve, n + 1)
            rms_row(dve, 0, 0)
            dve.wait_ge(weights_used, n + 2)
            EV_DVE.done(nc.vector.tensor_tensor(e_f, ps[:, 4:8, 0:T], repeated(r_row[:, :], 1, H), ALU.mult), "f")
            dve.wait_ge(EV_ACT.sem, EV_ACT.after("sigmoid"))
            for h in range(H):
                m = nc.vector.tensor_scalar(e_f[:, h, :], e_f[:, h, :], lb[:, 1, h:h + 1], lb[:, 0, h:h + 1], ALU.mult, ALU.add)
            dve_link(dve, m)
            nc.vector.tensor_scalar(e_k, e_f, -1.0, 1.0, ALU.mult, ALU.add)
            EV_DVE.done(nc.vector.tensor_scalar(e_f, e_f, 1e-6, None, ALU.max), "floor")
            dve_ahead.before(dve, n + 2)
            dve.wait_ge(EV_ACT.sem, EV_ACT.after("log"))
            dve.wait_ge(EV_POOL.sem, EV_POOL.after("reset"))
            EV_DVE.done(nc.vector.tensor_tensor_scan(flat(e_b), e_reset, flat(e_last), 0.0, ALU.mult, ALU.add), "cum")
            dve.wait_ge(EV_DVE.sem, EV_DVE.after("cum"))
            b8 = flat(e_b).rearrange("p (c s) -> p c s", s=SB)
            mid = repeated(b8[:, :, SB // 2 - 1], 2, SB)
            EV_DVE.done(nc.vector.tensor_tensor(flat(e_mid).rearrange("p (c s) -> p c s", s=SB), b8, mid, ALU.subtract), "diff_mid")
            b64 = flat(e_b).rearrange("p (c s) -> p c s", s=BC)
            EV_DVE.done(nc.vector.tensor_tensor(flat(e_last).rearrange("p (c s) -> p c s", s=BC), repeated(lasts, 2, BC), b64,
                                                ALU.subtract), "diff_last")
            dve.wait_ge(EV_ACT.sem, EV_ACT.after("exp_last"))
            EV_DVE.done(nc.vector.tensor_tensor(e_last, e_last, e_k, ALU.mult), "decayed")
            nc.vector.tensor_copy(e_decay, flat(e_exp).rearrange("p (c s) -> p c s", s=BC)[:, :, BC - 1])
            nc.vector.tensor_tensor(e_q0, e_exp, repeated(r_row[:, :], 1, H), ALU.mult)
            dve_link(dve, nc.vector.tensor_tensor(e_mid, e_mid, repeated(r_row[:, :], 1, H), ALU.mult))
            dve_ahead.before(dve, n + 3)
            dve.wait_ge(weights_used, n + 4)
            nc.vector.tensor_tensor(e_q0, e_q0, ps[:, 0:4, 0:T], ALU.mult)
            EV_DVE.done(nc.vector.tensor_tensor(e_qm, e_mid, ps[:, 0:4, 0:T], ALU.mult), "queries")

            def keys(h):
                dve.wait_ge(EV_ACT.sem, EV_ACT.after(f"exp{h}"))
                k = repeated(e_k[:, h, :].rearrange("p (c s) -> p c s", c=NC), 2, NB)
                EV_DVE.done(nc.vector.tensor_tensor(e_kd[h % 2], e_kd[h % 2], k, ALU.mult), f"keys{h}")

            keys(0)
            dve_ahead.before(dve, n + 5)
            keys(1)
            dve_ahead.before(dve, n + 7)
            dve.wait_ge(EV_ACT.sem, EV_ACT.after("av"))
            dve_link(dve, nc.vector.tensor_tensor(e_sq, e_av.rearrange("p t n -> p (t n)"), e_av.rearrange("p t n -> p (t n)"), ALU.mult))
            EV_DVE.done(nc.vector.tensor_reduce(e_ss, e_sq.rearrange("p (n d) -> p n d", d=AD), AX.X, ALU.add), "v_squares")
            dve.wait_ge(EV_POOL.sem, EV_POOL.after("v_rstd"))
            av = e_av.rearrange("p t n -> p (t n)").rearrange("p (n d) -> p n d", d=AD)
            dve_link(dve, nc.vector.tensor_tensor(av, av, repeated(e_rs, 2, AD), ALU.mult))
            EV_DVE.done(nc.vector.tensor_tensor(e_av, e_av, repeated(vnorm[:, :], 1, TT), ALU.mult), "v_normed")
            keys(2)
            dve_ahead.before(dve, n + 9)
            keys(3)
            dve_ahead.before(dve, n + 11)
            dve.wait_ge(EV_PE.sem, EV_PE.after("deltas"))
            dve_link(dve, nc.vector.tensor_copy(e_state[:, 0, :, :], bank(3).rearrange("p (h e) -> p h e", h=H)))
            for c in (1, 2):
                for h in range(H):
                    m = nc.vector.scalar_tensor_tensor(out=e_state[:, c, h, :], in0=e_state[:, c - 1, h, :],
                                                       scalar=e_decay[:, h * NC + c:h * NC + c + 1],
                                                       in1=ps[:, c, h * P:(h + 1) * P], op0=ALU.mult, op1=ALU.add)
                if c == 1:
                    dve_link(dve, m)
            EV_DVE.done(m, "states")
            dve.wait_ge(EV_POOL.sem, EV_POOL.after("zeros"))
            EV_DVE.done(nc.vector.copy_predicated(e_scores, e_mask.bitcast(i32), bank(0).rearrange("p (n t) -> p n t", t=BC)), "masked")
            dve.wait_ge(EV_PE.sem, EV_PE.after("mixed"))
            for h in range(AH):
                o = slice(h * AD, (h + 1) * AD)
                m = nc.vector.scalar_tensor_tensor(out=xn[:, :, o], in0=ps[:, 4 + h // 4, (h % 4) * P:(h % 4 + 1) * P].rearrange("p (t d) -> p t d", t=TT),
                                               scalar=cols[:, BS + h:BS + h + 1], in1=e_u[:, :, o], op0=ALU.add, op1=ALU.mult)
            m.then_inc(rows_ready, 1)
            turn_dve(dve, s, 1, KT, part=(0, 2))
            dve_ahead.before(dve, n + 12)
            dve.wait_ge(EV_ACT.sem, EV_ACT.after("o_copied"))
            dve.wait_ge(EV_POOL.sem, EV_POOL.after("gate"))
            dve_link(dve, nc.vector.tensor_tensor(e_o, e_o, e_g, ALU.mult))
            dve.wait_ge(EV_ACT.sem, EV_ACT.after("o_squared"))
            EV_DVE.done(nc.vector.tensor_reduce(e_os, e_sq.rearrange("p (n d) -> p n d", d=P), AX.X, ALU.add), "o_squares")
            dve.wait_ge(EV_POOL.sem, EV_POOL.after("o_rstd"))
            o4 = e_o.rearrange("p t (h d) -> p t h d", h=H)
            rs4 = repeated(e_or.rearrange("p (t h) -> p t h", t=TT), 3, P)
            nc.vector.tensor_tensor(xn[:, :, 512:1024].rearrange("p t (h d) -> p t h d", h=H), o4, rs4, ALU.mult)\
              .then_inc(rows_ready, 1)
            turn_dve(dve, s, 1, KT, part=(2, 4))
            add_result(dve, s, 1.0)

        class Attention:

            def __init__(self, name, heads, dv, parts, value, scale, o_bank, rows, probs, probs_t, small):
                self.heads, self.dv, self.parts, self.value, self.scale = heads, dv, parts, value, scale
                self.o_bank, self.rows, self.probs, self.probs_t, self.small = o_bank, rows, probs, probs_t, small
                names = ["scores0", "scores1"]
                for h in range(heads):
                    names += [f"turned{h}"] + [f"scores{h + 2}"] * (h + 2 < heads) + [f"output{h}"]
                self.pe_done = Steps(sem(name + "_attn_pe"), names)
                names = ["probs0"]
                for h in range(heads):
                    names += [f"columns{h}"] + [f"probs{h + 1}"] * (h + 1 < heads)
                self.act_done = Steps(sem(name + "_attn_act"), names)
                names = ["max0", "max1"]
                for h in range(heads):
                    names += [f"max{h + 2}"] * (h + 2 < heads) + [f"rows{h}"]
                self.dve_done = Steps(sem(name + "_attn_dve"), names)

            def pe(self, pe):
                def scores(h):
                    for qt in range(TT):
                        c0, w = qt * P, (qt + 1) * P
                        parts = self.parts(h)
                        for j, (q, k) in enumerate(parts):
                            m = nc.tensor.matmul(ps[:, 4 + h % 2, c0:c0 + w], q[:, qt * P:(qt + 1) * P], k[:, 0:w],
                                                 start=j == 0, stop=j == len(parts) - 1)
                    self.pe_done.done(m, f"scores{h}")

                scores(0)
                scores(1)
                for h in range(self.heads):
                    pe.wait_ge(self.act_done.sem, self.act_done.after(f"probs{h}"))
                    for j in range(3):
                        m = nc.tensor.transpose(ps[:, 6 + h % 2, j * P:(j + 1) * P], self.probs[h % 2][:, j * P:(j + 1) * P],
                                                ident[:, :])
                    self.pe_done.done(m, f"turned{h}")
                    if h + 2 < self.heads:
                        scores(h + 2)
                    pe.wait_ge(self.act_done.sem, self.act_done.after(f"columns{h}"))
                    if h >= 2:
                        pe.wait_ge(self.dve_done.sem, self.dve_done.after(f"rows{h - 2}"))
                    o = [ps[:, self.o_bank + h % 2, qt * self.dv:(qt + 1) * self.dv] for qt in range(TT)]
                    pt = self.probs_t[h % 2]
                    nc.tensor.matmul(o[0], pt[:, 0:P], self.value(h, 0), start=True, stop=True)
                    nc.tensor.matmul(o[1], pt[:, P:2 * P], self.value(h, 0), start=True, stop=False)
                    m = nc.tensor.matmul(o[1], pt[:, 2 * P:3 * P], self.value(h, 1), start=False, stop=True)
                    self.pe_done.done(m, f"output{h}")

            def act(self, act):
                def probs(h):
                    act.wait_ge(self.dve_done.sem, self.dve_done.after(f"max{h}"))
                    pr, sm = self.probs[h % 2], self.small[h % 4]
                    nc.scalar.activation(pr[:, 0:P], pr[:, 0:P], ACT.Exp, bias=sm[:, 0:1], accum_out=sm[:, 2:3])
                    m = nc.scalar.activation(pr[:, P:3 * P], pr[:, P:3 * P], ACT.Exp, bias=sm[:, 1:2], accum_out=sm[:, 3:4])
                    self.act_done.done(m, f"probs{h}")

                probs(0)
                for h in range(self.heads):
                    act.wait_ge(self.pe_done.sem, self.pe_done.after(f"turned{h}"))
                    self.act_done.done(nc.scalar.activation(self.probs_t[h % 2], bank(6 + h % 2, 3 * P), ACT.Copy), f"columns{h}")
                    if h + 1 < self.heads:
                        probs(h + 1)

            def dve(self, dve):
                def maxima(h):
                    dve.wait_ge(self.pe_done.sem, self.pe_done.after(f"scores{h}"))
                    pr, sm = self.probs[h % 2], self.small[h % 4]
                    nc.vector.scalar_tensor_tensor(out=pr[:, 0:P], in0=ps[:, 4 + h % 2, 0:P], scalar=self.scale(h, 0),
                                                   in1=causal[:, 0:P], op0=ALU.mult, op1=ALU.add)
                    dve_link(dve, nc.vector.scalar_tensor_tensor(out=pr[:, P:3 * P], in0=ps[:, 4 + h % 2, P:3 * P],
                                                                 scalar=self.scale(h, 1), in1=causal[:, P:3 * P],
                                                                 op0=ALU.mult, op1=ALU.add))
                    nc.vector.tensor_reduce(sm[:, 0:1], pr[:, 0:P], AX.X, ALU.max, negate=True)
                    self.dve_done.done(nc.vector.tensor_reduce(sm[:, 1:2], pr[:, P:3 * P], AX.X, ALU.max, negate=True), f"max{h}")

                maxima(0)
                maxima(1)
                for h in range(self.heads):
                    if h + 2 < self.heads:
                        maxima(h + 2)
                    dve.wait_ge(self.pe_done.sem, self.pe_done.after(f"output{h}"))
                    sm = self.small[h % 4]
                    dve_link(dve, nc.vector.reciprocal(sm[:, 4:6], sm[:, 2:4]))
                    for qt in range(TT):
                        m = nc.vector.tensor_scalar(self.rows(h, qt), ps[:, self.o_bank + h % 2, qt * self.dv:(qt + 1) * self.dv],
                                                    sm[:, 4 + qt:5 + qt], None, ALU.mult)
                    self.dve_done.done(m, f"rows{h}")

        causal = silu_g[:, :, :].rearrange("p a b -> p (a b)")[:, 0:3 * P]

        def make_causal(pool):
            pool_link(pool, nc.gpsimd.memset(causal, 0.0))
            nc.gpsimd.affine_select(out=causal[:, 0:P], in_=causal[:, 0:P], compare_op=ALU.is_ge, fill=-1e30, base=0,
                                    pattern=[[-1, P]], channel_multiplier=1)
            return nc.gpsimd.affine_select(out=causal[:, 2 * P:3 * P], in_=causal[:, 2 * P:3 * P], compare_op=ALU.is_ge,
                                           fill=-1e30, base=0, pattern=[[-1, P]], channel_multiplier=1)

        MH, NOPE, ROPE, QL, KVL = 8, 128, 64, 384, 256
        QK = NOPE + ROPE
        ar = Arena()
        m_c = ar(TT * (QL + KVL), "p (t n) -> p t n", t=TT)
        m_kr = ar(TT * ROPE, "p (t n) -> p t n", t=TT)
        m_q = ar(TT * MH * QK, "p (t h d) -> p t h d", t=TT, h=MH)
        m_qr = ar(TT * MH * ROPE, "p (t h d) -> p t h d", t=TT, h=MH)
        m_k = ar(TT * MH * NOPE, "p (t h d) -> p t h d", t=TT, h=MH)
        m_krot = ar(TT * MH * ROPE, "p (t h d) -> p t h d", t=TT, h=MH)
        m_v = ar(TT * MH * NOPE, "p (t h d) -> p t h d", t=TT, h=MH)
        m_qt = ar(MH * T, "p (h t) -> p h t", h=MH)
        m_kt = ar(MH * T, "p (h t) -> p h t", h=MH)
        m_qrt = ar(MH // 2 * T, "p (h t) -> p h t", h=MH // 2)
        m_krt = ar(MH // 2 * T, "p (h t) -> p h t", h=MH // 2)
        m_pos = ar(TT)
        m_ang = ar(4 * 32, "p (a t f) -> p a t f", a=2, t=TT)
        m_n = ar(4 * 32, "p (a t f) -> p a t f", a=2, t=TT)
        m_cos = ar(4 * ROPE, "p (a t f) -> p a t f", a=2, t=TT)
        m_sin = ar(4 * ROPE, "p (a t f) -> p a t f", a=2, t=TT)
        m_css = ar(4)
        m_crs = ar(4)
        m_ss = ar(2 * TT * MH, "p (a t h) -> p a t h", a=2, t=TT)
        m_rs = ar(2 * TT * MH, "p (a t h) -> p a t h", a=2, t=TT)
        m_krs = ar(TT)
        m_small = [ar(6) for _ in range(4)]
        m_sq = [m_qt.rearrange("p h t -> p (h t)"), m_kt.rearrange("p h t -> p (h t)")]
        m_tmp = xn[:, :, :].rearrange("p t n -> p (t n)")
        m_probs = [m_q.rearrange("p t h d -> p (t h d)")[:, j * 384:(j + 1) * 384] for j in range(2)]
        m_probs_t = [m_q.rearrange("p t h d -> p (t h d)")[:, (2 + j) * 384:(3 + j) * 384] for j in range(2)]
        m_ksq = m_tmp
        ML_PE = Steps(sem("mla_pe"), ["q_turned", "k_turned", "q_rope_turned", "k_rope_turned"])
        ML_ACT = Steps(sem("mla_act"), ["sin", "c0", "c1", "c_sq", "q0", "q1", "q2", "kv0", "q_sq", "k_sq", "q_cols", "q_rope_cols"])
        ML_DVE = Steps(sem("mla_dve"), ["angles", "kv1", "kr_sq", "squares", "q_rope", "k_scaled", "k_rope", "k_cols", "k_rope_cols"])
        ML_POOL = Steps(sem("mla_pool"), ["causal", "c_rstd", "rstd", "q_scale"])

        mla_attn = Attention(
            "mla", MH, NOPE,
            lambda h: [(m_qt[:, h, :], m_kt[:, h, :]),
                       (m_qrt[64 * (h % 2):64 * (h % 2) + 64, h // 2, :], m_krt[64 * (h % 2):64 * (h % 2) + 64, h // 2, :])],
            lambda h, t: m_v[:, t, h, :], lambda h, t: m_rs[:, 0, t, h:h + 1], 0,
            lambda h, t: xn[:, t, h * NOPE:(h + 1) * NOPE], m_probs, m_probs_t, m_small)

        def mla_load(sp, s):
            n = base[s]
            load_columns(sp, n, io["mla_w_in"][0], 0, 512)
            v = io["mla_w_in"][0].rearrange("(k p) n -> p k n", p=P)
            load_slot(sp, n + 2, [(raw_view(n + 2, 8, 192)[:, 4 * j:4 * j + 4, :], v[:, 4 * j:4 * j + 4, 512:704]) for j in range(2)])
            v = io["mla_w_q_b"][0].rearrange("(k p) n -> p k n", p=P)
            for c in range(3):
                load_slot(sp, n + 3 + c, [(raw_view(n + 3 + c, 3, 512)[:, a:b, :], v[:, a:b, c * 512:(c + 1) * 512])
                                          for a, b in ((0, 2), (2, 3))])
            v = io["mla_w_kv_b"][0].rearrange("(k p) n -> p k n", p=P)
            for c in range(2):
                load_slot(sp, n + 6 + c, [(raw_view(n + 6 + c, 2, D)[:, j:j + 1, :], v[:, j:j + 1, c * D:(c + 1) * D])
                                          for j in range(2)])
            load_square(sp, n + 8, io["mla_w_out"][0])

        def mla_pe(pe, s):
            n = base[s]
            for b in range(4):
                turn_x(pe, s, b, b)
            rows_product(pe, n, [bank(4), bank(5)], first_of=s)
            take_slot(pe, n + 2)
            for k in range(KT):
                m = by_rows([bank(6, 192), bank(7, 192)], k, n + 2, k, 192, k == 0, k == KT - 1)
            m.then_inc(weights_used, 1)
            turn_pe(pe, s, 1, xn, 5)
            turned_by(pe, s, 1, 3)
            for c in range(3):
                if c == 2:
                    pe.wait_ge(ML_ACT.sem, ML_ACT.after("q0"))
                take_slot(pe, n + 3 + c)
                for k in range(3):
                    m = by_rows([bank(4 + 2 * (c % 2)), bank(5 + 2 * (c % 2))], k, n + 3 + c, k, 512, k == 0, k == 2)
                m.then_inc(weights_used, 1)
            for c in range(2):
                if c == 1:
                    pe.wait_ge(ML_ACT.sem, ML_ACT.after("q2"))
                take_slot(pe, n + 6 + c)
                for k in range(2):
                    for half in range(2):
                        m = by_rows([bank(4 * c + half), bank(4 * c + 2 + half)], 3 + k, n + 6 + c, k, D, k == 0, k == 1,
                                    off=half * 512, cols_n=512)
                m.then_inc(weights_used, 1)

            def turn(src, first_bank):
                for h in range(MH):
                    for tt in range(TT):
                        at = (h % 2) * T + tt * P
                        m = nc.tensor.transpose(ps[:, first_bank + h // 2, at:at + P], src[:, tt, h, 0:NOPE], ident[:, :])
                return m

            def turn_rope(src, first_bank):
                for h in range(MH // 2):
                    for tt in range(TT):
                        at = (h % 2) * T + tt * P
                        m = nc.tensor.transpose(ps[:, first_bank + h // 2, at:at + P],
                                                src[:, tt, 2 * h:2 * h + 2, :].rearrange("p h d -> p (h d)"), ident[:, :])
                return m

            pe.wait_ge(ML_ACT.sem, ML_ACT.after("kv0"))
            ML_PE.done(turn(m_q, 0), "q_turned")
            pe.wait_ge(ML_DVE.sem, ML_DVE.after("k_scaled"))
            ML_PE.done(turn(m_k, 4), "k_turned")
            pe.wait_ge(ML_ACT.sem, ML_ACT.after("q_cols"))
            ML_PE.done(turn_rope(m_qr, 0), "q_rope_turned")
            pe.wait_ge(ML_DVE.sem, ML_DVE.after("k_rope"))
            ML_PE.done(turn_rope(m_krot, 2), "k_rope_turned")
            pe.wait_ge(ML_ACT.sem, ML_ACT.after("q_rope_cols"))
            pe.wait_ge(ML_DVE.sem, ML_DVE.after("k_rope_cols"))
            mla_attn.pe(pe)
            turn_pe(pe, s, 2, xn, KT)
            project_out(pe, s, 2, n + 8)

        def mla_act(act, s):
            n = base[s]
            norm_act(act, s, GAINS + (5 + 1) * KT)
            rms(act, s)
            act.wait_ge(ML_DVE.sem, ML_DVE.after("angles"))
            ML_ACT.done(nc.scalar.activation(m_ang, m_ang, ACT.Sin), "sin")
            act_ahead.before(act, n + 1)
            act.wait_ge(weights_used, n + 2)
            ML_ACT.done(scaled_rows(m_c[:, :, 0:512], 4, ACT.Copy), "c0")
            act_ahead.before(act, n + 2)
            act.wait_ge(weights_used, n + 3)
            scaled_rows(m_c[:, :, 512:640], 6, ACT.Copy, 128)
            for tt in range(TT):
                m = nc.scalar.activation(m_kr[:, tt, :], ps[:, 6 + tt, 128:192], ACT.Copy, scale=rstd[:, tt:tt + 1])
            ML_ACT.done(m, "c1")
            act.wait_ge(ML_ACT.sem, ML_ACT.after("c1"))
            for j, (a, b) in enumerate(((0, QL), (QL, QL + KVL))):
                for tt in range(TT):
                    m = nc.scalar.activation(m_sq[j][:, tt * 512:tt * 512 + b - a], m_c[:, tt, a:b], ACT.Square,
                                             scale=1 / math.sqrt(b - a), accum_out=m_css[:, TT * j + tt:TT * j + tt + 1])
            ML_ACT.done(m, "c_sq")
            turn_act(act, s, 1, 5, QA)
            for c in range(3):
                act_ahead.before(act, n + 3 + c)
                act.wait_ge(weights_used, n + 4 + c)
                q = m_q.rearrange("p t h d -> p t (h d)")[:, :, c * 512:(c + 1) * 512]
                ML_ACT.done(nc.scalar.activation(q, ps[:, 4 + 2 * (c % 2):6 + 2 * (c % 2), :], ACT.Copy), f"q{c}")
            act_ahead.before(act, n + 6)
            act.wait_ge(weights_used, n + 7)
            kv = ps[:, 0:4, :].rearrange("p b n -> p (b n)").rearrange("p (t h d) -> p t h d", t=TT, h=4)
            nc.scalar.activation(m_k[:, :, 0:4, :], kv[:, :, :, 0:NOPE], ACT.Copy)
            ML_ACT.done(nc.scalar.activation(m_v[:, :, 0:4, :], kv[:, :, :, NOPE:2 * NOPE], ACT.Copy), "kv0")
            act_ahead.before(act, n + 7)
            act.wait_ge(ML_ACT.sem, ML_ACT.after("kv0"))
            for tt in range(TT):
                m = nc.scalar.activation(m_sq[tt][:, 0:MH * QK], m_q[:, tt, :, :].rearrange("p h d -> p (h d)"), ACT.Square)
            ML_ACT.done(m, "q_sq")
            act.wait_ge(ML_DVE.sem, ML_DVE.after("kv1"))
            ML_ACT.done(nc.scalar.activation(m_ksq, m_k.rearrange("p t h d -> p (t h d)"), ACT.Square), "k_sq")
            act.wait_ge(ML_PE.sem, ML_PE.after("q_turned"))
            act.wait_ge(ML_DVE.sem, ML_DVE.after("squares"))
            ML_ACT.done(nc.scalar.activation(m_qt, ps[:, 0:4, :], ACT.Copy, scale=cols[:, QN:QN + 1]), "q_cols")
            act.wait_ge(ML_PE.sem, ML_PE.after("q_rope_turned"))
            ML_ACT.done(nc.scalar.activation(m_qrt, ps[:, 0:2, :], ACT.Copy), "q_rope_cols")
            mla_attn.act(act)
            turn_act(act, s, 2, KT)
            act_ahead.before(act, n + 11)

        def mla_pool(pool, s):
            ML_POOL.done(make_causal(pool), "causal")
            pool.wait_ge(ML_ACT.sem, ML_ACT.after("c_sq"))
            pool_link(pool, nc.gpsimd.tensor_scalar(m_css, m_css, EPS, None, ALU.add))
            ML_POOL.done(nc.gpsimd.tensor_tensor(m_crs, m_css, minus_half[:, 0:4], ALU.pow), "c_rstd")
            pool.wait_ge(ML_DVE.sem, ML_DVE.after("squares"))
            for a in range(2):
                ss, rs = (v[:, a, :, :].rearrange("p t h -> p (t h)") for v in (m_ss, m_rs))
                pool_link(pool, nc.gpsimd.tensor_scalar(ss, ss, 1.0 / QK, EPS, ALU.mult, ALU.add))
                m = nc.gpsimd.tensor_tensor(rs, ss, minus_half[:, :], ALU.pow)
            ML_POOL.done(m, "rstd")
            pool.wait_ge(ML_POOL.sem, ML_POOL.after("rstd"))
            q = m_rs[:, 0, :, :].rearrange("p t h -> p (t h)")
            ML_POOL.done(nc.gpsimd.tensor_scalar(q, q, QK ** -0.5, None, ALU.mult), "q_scale")

        def mla_dve(dve, s):
            n = base[s]
            norm_dve(dve, s, GAINS + (5 + 1) * KT)
            dve_link(dve, nc.vector.tensor_copy(m_pos, pos_i[:, :]))
            for a in range(2):
                for tt in range(TT):
                    m = nc.vector.tensor_scalar(m_ang[:, a, tt, :], inv_freq[:, :], m_pos[:, tt:tt + 1], None, ALU.mult)
            dve_link(dve, m)
            for a in range(2):
                m = nc.vector.tensor_scalar(m_n[:, a, :, :], m_ang[:, a, :, :], 1 / (2 * math.pi), 0.25 * a, ALU.mult, ALU.add)
            dve_link(dve, m)
            dve_link(dve, nc.vector.tensor_scalar(m_n, m_n, 1.5 * 2 ** 23, None, ALU.add))
            dve_link(dve, nc.vector.tensor_scalar(m_n, m_n, -1.5 * 2 ** 23, None, ALU.add))
            rest, part = 2 * math.pi, 6.28125
            for _ in range(3):
                dve_link(dve, nc.vector.scalar_tensor_tensor(out=m_ang, in0=m_n, scalar=-part, in1=m_ang, op0=ALU.mult, op1=ALU.add))
                rest -= part
                part = math.ldexp(round(math.ldexp(rest, 20)), -20) if _ == 0 else rest
            dve_link(dve, nc.vector.tensor_scalar(m_ang[:, 1, :, :], m_ang[:, 1, :, :], math.pi / 2, None, ALU.add))
            ML_DVE.done(nc.vector.tensor_scalar(m_ang, m_ang, 3.1415925, -3.1415925, ALU.min, ALU.max), "angles")
            dve.wait_ge(ML_ACT.sem, ML_ACT.after("sin"))
            for a in range(2):
                for half in range(2):
                    f = slice(half * 32, half * 32 + 32)
                    other = slice(32 - half * 32, 64 - half * 32)
                    nc.vector.tensor_tensor(m_cos[:, a, :, f], m_ang[:, 1, :, :], repeated(qk_norm[:, a, f], 1, TT), ALU.mult)
                    m = nc.vector.tensor_tensor(m_sin[:, a, :, f], m_ang[:, 0, :, :], repeated(qk_norm[:, a, other], 1, TT), ALU.mult)
            dve_link(dve, m)
            dve_link(dve, nc.vector.tensor_scalar(m_sin[:, :, :, 0:32], m_sin[:, :, :, 0:32], -1.0, None, ALU.mult))
            dve_ahead.before(dve, n + 1)
            dve_ahead.before(dve, n + 2)
            dve.wait_ge(ML_POOL.sem, ML_POOL.after("c_rstd"))
            for j, (a, b) in enumerate(((0, QL), (QL, QL + KVL))):
                for tt in range(TT):
                    m = nc.vector.tensor_scalar(xn[:, tt, a:b], m_c[:, tt, a:b], m_crs[:, TT * j + tt:TT * j + tt + 1], None, ALU.mult)
            m.then_inc(rows_ready, TT)
            turn_dve(dve, s, 1, 5, QA)
            for c in range(3):
                dve_ahead.before(dve, n + 3 + c)
            dve_ahead.before(dve, n + 6)
            dve_ahead.before(dve, n + 7)
            dve.wait_ge(weights_used, n + 8)
            kv = ps[:, 4:8, :].rearrange("p b n -> p (b n)").rearrange("p (t h d) -> p t h d", t=TT, h=4)
            nc.vector.tensor_copy(m_k[:, :, 4:8, :], kv[:, :, :, 0:NOPE])
            ML_DVE.done(nc.vector.tensor_copy(m_v[:, :, 4:8, :], kv[:, :, :, NOPE:2 * NOPE]), "kv1")
            dve_link(dve, nc.vector.tensor_tensor(m_qr[:, :, 0, :], m_kr, m_kr, ALU.mult))
            ML_DVE.done(nc.vector.tensor_reduce(m_krs, m_qr[:, :, 0, :], AX.X, ALU.add), "kr_sq")
            dve.wait_ge(ML_ACT.sem, ML_ACT.after("q_sq"))
            for tt in range(TT):
                nc.vector.tensor_reduce(m_ss[:, 0, tt, :], m_sq[tt][:, 0:MH * QK].rearrange("p (h d) -> p h d", h=MH), AX.X, ALU.add)
            dve.wait_ge(ML_ACT.sem, ML_ACT.after("k_sq"))
            dve_link(dve, nc.vector.tensor_reduce(m_ss[:, 1, :, :].rearrange("p t h -> p (t h)"),
                                                  m_ksq.rearrange("p (n d) -> p n d", d=NOPE), AX.X, ALU.add))
            ML_DVE.done(nc.vector.tensor_tensor(m_ss[:, 1, :, :], m_ss[:, 1, :, :], repeated(m_krs, 2, MH), ALU.add), "squares")

            def rotate(dst, src, a, tmp):
                c, sn = m_cos[:, a, :, :], m_sin[:, a, :, :]
                nh = src.shape[2]
                nc.vector.tensor_tensor(tmp, src, repeated(c, 2, nh), ALU.mult)
                nc.vector.tensor_tensor(dst[:, :, :, 0:32], src[:, :, :, 32:64], repeated(sn[:, :, 0:32], 2, nh), ALU.mult)
                dve_link(dve, nc.vector.tensor_tensor(dst[:, :, :, 32:64], src[:, :, :, 0:32], repeated(sn[:, :, 32:64], 2, nh), ALU.mult))
                return nc.vector.tensor_tensor(dst, dst, tmp, ALU.add)

            tmp = m_tmp[:, 0:TT * MH * ROPE].rearrange("p (t h d) -> p t h d", t=TT, h=MH)
            ML_DVE.done(rotate(m_qr, m_q[:, :, :, NOPE:QK], 0, tmp), "q_rope")
            dve.wait_ge(ML_POOL.sem, ML_POOL.after("rstd"))
            ML_DVE.done(nc.vector.tensor_tensor(m_k, m_k, repeated(m_rs[:, 1, :, :], 3, NOPE), ALU.mult), "k_scaled")
            tmp1 = m_tmp[:, 1024:1024 + TT * ROPE].rearrange("p (t h d) -> p t h d", t=TT, h=1)
            rot = m_tmp[:, 1152:1152 + TT * ROPE].rearrange("p (t h d) -> p t h d", t=TT, h=1)
            dve_link(dve, rotate(rot, m_kr.unsqueeze(2), 1, tmp1))
            ML_DVE.done(nc.vector.tensor_tensor(m_krot, repeated(rot[:, :, 0, :], 2, MH), repeated(m_rs[:, 1, :, :], 3, ROPE), ALU.mult), "k_rope")
            dve.wait_ge(ML_PE.sem, ML_PE.after("k_turned"))
            ML_DVE.done(nc.vector.tensor_scalar(m_kt, ps[:, 4:8, :], cols[:, KN:KN + 1], None, ALU.mult), "k_cols")
            dve.wait_ge(ML_PE.sem, ML_PE.after("k_rope_turned"))
            ML_DVE.done(nc.vector.tensor_copy(m_krt, ps[:, 2:4, :]), "k_rope_cols")
            dve.wait_ge(ML_POOL.sem, ML_POOL.after("q_scale"))
            mla_attn.dve(dve)
            dve.wait_ge(mla_attn.dve_done.sem, mla_attn.dve_done.after(f"rows{MH - 1}"))
            dve.sem_inc(rows_ready, TT)
            turn_dve(dve, s, 2, KT)
            add_result(dve, s, 1.0)

        GH, GD = 6, 64
        SH, SD, SG, SN, CONV = 6, 64, 2, 128, 4
        SR = SH // SG
        XT = 7
        PADC, PADP = 4, 16
        ar = Arena()
        h_u = ar(TT * 1536, "p (t n) -> p t n", t=TT)
        h_x = ar(XT * (T + PADC), "p (k t) -> p k t", k=XT)
        h_c = ar(XT * T, "p (k t) -> p k t", k=XT)
        h_p = ar(2 * (T + PADP), "p (k t) -> p k t", k=2)
        h_sum = [ar(2 * (T + PADP), "p (k t) -> p k t", k=2) for _ in range(2)]
        h_diff = ar(2 * T, "p (k t) -> p k t", k=2)
        h_count = ar(2 * T, "p (k t) -> p k t", k=2)
        h_pw = ar(2 * P, "p (k d) -> p k d", k=2)
        h_tri = ar(P)
        h_neg = ar(P)
        h_decay = ar(TT * SH * P, "p (n l) -> p n l", l=P)
        h_xs = ar(TT * SH * SD, "p (t n) -> p t n", t=TT)
        h_xdt = ar(TT * SH * SD, "p (t n) -> p t n", t=TT)
        h_b = ar(SG * SN, "p (g n) -> p g n", g=SG)
        h_xw = ar(SH * SD)
        h_state = ar(SH * SD)
        h_qkt = ar(6 * T, "p (k t) -> p k t", k=6)
        h_y = ar(TT * SH * SD, "p (t n) -> p t n", t=TT)
        h_ysq = ar(TT * SH * SD, "p (t n) -> p t n", t=TT)
        h_z = ar(TT * SH * SD, "p (t n) -> p t n", t=TT)
        h_probs = [ar(3 * P) for _ in range(2)]
        h_probs_t = [ar(3 * P) for _ in range(2)]
        h_small = [ar(6) for _ in range(4)]
        N12 = TT * SH
        h_raw, h_abs, h_e, h_s, h_s2, h_q, h_dt, h_da, h_acum, h_eacum = (ar(N12) for _ in range(10))
        h_ea = ar(SH)
        h_yss, h_yrs = ar(4), ar(4)
        HY_PE = Steps(sem("hyb_pe"), ["xs_turned", "cumulated", "cb_pool", "qk_turned", "state", "y"])
        HY_ACT = Steps(sem("hyb_act"), ["ea", "exp_dt", "conv", "u0", "xs_rows", "u1", "u2", "silu_z", "decay",
                                        "exp_acum", "qk_cols"])
        HY_DVE = Steps(sem("hyb_dve"), ["xa", "xb", "conv", "tail", "abs", "diff", "da", "xdt", "acum", "decay", "xw", "scores", "state", "y_off", "y_squares"])
        HY_POOL = Steps(sem("hyb_pool"), ["tri", "counts", "causal", "y_rstd"])
        pw_loaded = sem("pool_w_loaded")
        hyb_attn = Attention(
            "hyb", GH, GD,
            lambda h: [(h_qkt[64 * (h % 2):64 * (h % 2) + 64, h // 2, :], h_qkt[64 * (h % 2):64 * (h % 2) + 64, 3 + h // 2, :])],
            lambda h, t: h_u[:, t, 768 + h * GD:768 + (h + 1) * GD], lambda h, t: GD ** -0.5, 2,
            lambda h, t: xn[:, t, h * GD:(h + 1) * GD], h_probs, h_probs_t, h_small)

        def hybrid_load(sp, s):
            n, w = base[s], io["w_in_2"][0]
            load_columns(sp, n, w, 1536, 512)
            load_columns(sp, n + 2, w, 2048, 384)
            load_columns(sp, n + 4, w, 2432, 262)
            for j in range(3):
                load_columns(sp, n + 6 + 2 * j, w, 512 * j, 512)
            load_square(sp, n + 12, io["w_out_2"][0])

        def hybrid_pe(pe, s):
            n = base[s]
            for b in range(4):
                turn_x(pe, s, b, b)
            columns_product(pe, n, [bank(4 + j, T) for j in range(4)], 512, first_of=s)
            rms_row_pe(pe, 1, 3)
            columns_product(pe, n + 2, [bank(j, T) for j in range(3)], 384)
            pe.wait_ge(HY_DVE.sem, HY_DVE.after("xa"))
            for half in range(2):
                take_slot(pe, n + 4 + half)
                for kk in range(4):
                    k = 4 * half + kk
                    by_rows([bank(3, 6), bank(6, 6)], k, n + 4 + half, kk, 262, k == 0, k == KT - 1, cols_n=6)
                    for j in range(2):
                        m = by_columns(bank(4 + j, T), k, n + 4 + half, kk, 262, 6 + j * P, k == 0, k == KT - 1)
                m.then_inc(weights_used, 1)
            pe.wait_ge(HY_DVE.sem, HY_DVE.after("xb"))
            rows_product(pe, n + 6, [bank(0), bank(1)])
            pe.wait_ge(HY_ACT.sem, HY_ACT.after("conv"))
            pe.wait_ge(HY_DVE.sem, HY_DVE.after("tail"))
            for tt in range(TT):
                for k in range(3):
                    nc.tensor.transpose(ps[:, 2 + tt, k * P:(k + 1) * P], h_c[:, k, tt * P:(tt + 1) * P], ident[:, :])
            for g in range(SG):
                m = nc.tensor.transpose(ps[:, 2 + g, 3 * P:4 * P], h_c[:, 3 + g, 0:P], ident[:, :])
            HY_PE.done(m, "xs_turned")
            rows_product(pe, n + 8, [bank(4), bank(5)])
            rows_product(pe, n + 10, [bank(6), bank(7)])
            pe.wait_ge(HY_DVE.sem, HY_DVE.after("da"))
            pe.wait_ge(HY_ACT.sem, HY_ACT.after("xs_rows"))
            for tt in range(TT):
                for h in range(SH):
                    j = tt * SH + h
                    nc.tensor.matmul(ps[:, j // 4, (j % 4) * P:(j % 4 + 1) * P], h_da[:, j:j + 1].broadcast_to([P, P]), h_tri,
                                     start=True, stop=True)
            for tt in range(TT):
                m = nc.tensor.matmul(ps[:, 3, tt * SH:(tt + 1) * SH], h_tri, h_da[:, tt * SH:(tt + 1) * SH], start=True, stop=True)
            HY_PE.done(m, "cumulated")
            pe.wait_ge(HY_ACT.sem, HY_ACT.after("u1"))
            pe.wait_ge(HY_DVE.sem, HY_DVE.after("diff"))
            pe.wait_ge(pw_loaded, 32)
            for tt in range(TT):
                for g in range(SG):
                    o = (tt * SG + g) * P
                    nc.tensor.matmul(ps[:, 4, o:o + P], h_c[:, 3 + g, tt * P:(tt + 1) * P], h_c[:, 5 + g, tt * P:(tt + 1) * P],
                                     start=True, stop=True)
            for tt in range(TT):
                for k in range(2):
                    m = nc.tensor.matmul(ps[:, 5, (tt * 2 + k) * P:(tt * 2 + k + 1) * P],
                                         h_diff[:, k, tt * P:(tt + 1) * P], h_pw[:, k, :], start=True, stop=True)
            HY_PE.done(m, "cb_pool")
            pe.wait_ge(HY_ACT.sem, HY_ACT.after("u2"))
            pe.wait_ge(HY_DVE.sem, HY_DVE.after("acum"))
            for k in range(6):
                b = (6, 7, 3)[k // 2]
                for tt in range(TT):
                    at = (k % 2) * T + tt * P
                    m = nc.tensor.transpose(ps[:, b, at:at + P], h_u[:, tt, k * P:(k + 1) * P], ident[:, :])
            HY_PE.done(m, "qk_turned")
            pe.wait_ge(HY_DVE.sem, HY_DVE.after("xw"))
            for g in range(SG):
                c = slice(g * SR * SD, (g + 1) * SR * SD)
                m = nc.tensor.matmul(ps[:, 2, c], h_b[:, g, :], h_xw[:, c], start=True, stop=True)
            HY_PE.done(m, "state")
            pe.wait_ge(HY_DVE.sem, HY_DVE.after("scores"))
            for tt in range(TT):
                for h in range(SH):
                    c = slice(h * SD, (h + 1) * SD)
                    nc.tensor.matmul(ps[:, tt, c], h_decay[:, tt * SH + h, :], h_xdt[:, tt, c], start=True, stop=True)
            pe.wait_ge(HY_DVE.sem, HY_DVE.after("state"))
            pe.wait_ge(HY_ACT.sem, HY_ACT.after("qk_cols"))
            for g in range(SG):
                c = slice(g * SR * SD, (g + 1) * SR * SD)
                m = nc.tensor.matmul(ps[:, 3, c], h_c[:, 5 + g, P:T], h_state[:, c], start=True, stop=True)
            HY_PE.done(m, "y")
            pe.wait_ge(HY_DVE.sem, HY_DVE.after("y_off"))
            hyb_attn.pe(pe)
            turn_pe(pe, s, 1, xn, KT)
            project_out(pe, s, 1, n + 12)

        def hybrid_act(act, s):
            n = base[s]
            norm_act(act, s, MIX2)
            HY_ACT.done(nc.scalar.activation(h_ea, a_log[:, :], ACT.Exp), "ea")
            rms(act, s)
            act_ahead.before(act, n + 5)
            act.wait_ge(HY_DVE.sem, HY_DVE.after("abs"))
            HY_ACT.done(nc.scalar.activation(h_e, h_abs, ACT.Exp, scale=-1.0), "exp_dt")
            for k in range(XT):
                m = nc.scalar.activation(h_c[:, k, :], h_c[:, k, :], ACT.Silu, bias=conv_cols[:, CONVB + k:CONVB + k + 1])
            HY_ACT.done(m, "conv")
            act_ahead.before(act, n + 7)
            act.wait_ge(weights_used, n + 8)
            HY_ACT.done(scaled_rows(h_u[:, :, 0:512], 0, ACT.Copy), "u0")
            act.wait_ge(HY_PE.sem, HY_PE.after("xs_turned"))
            nc.scalar.activation(h_xs, ps[:, 2:4, 0:3 * P], ACT.Copy)
            HY_ACT.done(nc.scalar.activation(h_b, ps[:, 2:4, 3 * P:4 * P], ACT.Copy), "xs_rows")
            act_ahead.before(act, n + 9)
            act.wait_ge(weights_used, n + 10)
            HY_ACT.done(scaled_rows(h_u[:, :, 512:1024], 4, ACT.Copy), "u1")
            act_ahead.before(act, n + 11)
            act.wait_ge(weights_used, n + 12)
            HY_ACT.done(scaled_rows(h_u[:, :, 1024:1536], 6, ACT.Copy), "u2")
            act.wait_ge(HY_ACT.sem, HY_ACT.after("u2"))
            HY_ACT.done(nc.scalar.activation(h_z, h_u[:, :, 1152:1536], ACT.Silu), "silu_z")
            act.wait_ge(HY_DVE.sem, HY_DVE.after("decay"))
            HY_ACT.done(nc.scalar.activation(h_decay, h_decay, ACT.Exp), "decay")
            HY_ACT.done(nc.scalar.activation(h_eacum, h_acum, ACT.Exp), "exp_acum")
            act.wait_ge(HY_PE.sem, HY_PE.after("qk_turned"))
            nc.scalar.activation(h_qkt[:, 0:4, :], ps[:, 6:8, :], ACT.Copy)
            HY_ACT.done(nc.scalar.activation(h_qkt[:, 4:6, :], ps[:, 3, :], ACT.Copy), "qk_cols")
            hyb_attn.act(act)
            turn_act(act, s, 1, KT)
            act_ahead.before(act, n + 15)

        def hybrid_pool(pool, s):
            pool_link(pool, nc.gpsimd.memset(h_pw, 0.0))
            for b in range(2):
                pool.dma_start(h_pw[64 * b:64 * b + 64, :, 64 * b:64 * b + 64],
                               io["pool_w_2"][0].rearrange("(a b) c d -> b c a d", b=2)[b]).then_inc(pw_loaded, 16)
            nc.gpsimd.memset(h_x[:, :, 0:PADC], 0.0)
            nc.gpsimd.memset(h_p[:, :, 0:PADP], 0.0)
            for j in range(2):
                nc.gpsimd.memset(h_sum[j][:, :, 0:PADP], 0.0)
            nc.gpsimd.memset(h_tri, 1.0)
            pool_link(pool, nc.gpsimd.memset(h_neg, 0.0))
            nc.gpsimd.affine_select(out=h_tri, in_=h_tri, compare_op=ALU.is_ge, fill=0.0, base=0, pattern=[[1, P]],
                                    channel_multiplier=-1)
            HY_POOL.done(nc.gpsimd.affine_select(out=h_neg, in_=h_neg, compare_op=ALU.is_ge, fill=-1e30, base=0,
                                                 pattern=[[1, P]], channel_multiplier=-1), "tri")
            pool_link(pool, nc.gpsimd.iota(h_count, pattern=[[0, 2], [1, T]], base=1, channel_multiplier=0,
                                           allow_small_or_imprecise_dtypes=True))
            for g, w in enumerate((2, 4, 8, 16)):
                v = h_count[64 * (g % 2):64 * (g % 2) + 64, g // 2, :]
                pool_link(pool, nc.gpsimd.tensor_scalar(v, v, float(w), None, ALU.min))
            HY_POOL.done(nc.gpsimd.memset(h_yss, 0.0), "counts")
            pool.wait_ge(r_steps, 3 + 2)
            HY_POOL.done(make_causal(pool), "causal")
            pool.wait_ge(HY_DVE.sem, HY_DVE.after("y_squares"))
            pool_link(pool, nc.gpsimd.tensor_scalar(h_yss, h_yss, 1.0 / (SR * SD), EPS, ALU.mult, ALU.add))
            HY_POOL.done(nc.gpsimd.tensor_tensor(h_yrs, h_yss, minus_half[:, 0:4], ALU.pow), "y_rstd")

        def hybrid_dve(dve, s):
            n = base[s]
            norm_dve(dve, s, MIX2)
            rms_diagonals(dve, s, 1)
            dve_ahead.before(dve, n + 1)
            rms_row(dve, 1, 3)
            dve.wait_ge(HY_POOL.sem, HY_POOL.after("counts"))
            dve_link(dve, nc.vector.reciprocal(h_count, h_count))

            def convolve(k):
                for j in range(CONV):
                    w = conv_cols[:, CONVW + j * XT + k:CONVW + j * XT + k + 1]
                    v = h_x[:, k, PADC - CONV + 1 + j:PADC - CONV + 1 + j + T]
                    if j == 0:
                        m = nc.vector.tensor_scalar(h_c[:, k, :], v, w, None, ALU.mult)
                    else:
                        m = nc.vector.scalar_tensor_tensor(out=h_c[:, k, :], in0=v, scalar=w, in1=h_c[:, k, :], op0=ALU.mult, op1=ALU.add)
                    if j < CONV - 1:
                        dve_link(dve, m)
                return m

            dve.wait_ge(weights_used, n + 2)
            HY_DVE.done(nc.vector.tensor_tensor(h_x[:, 0:4, PADC:PADC + T], ps[:, 4:8, 0:T], repeated(r_row[:, :], 1, 4), ALU.mult), "xa")
            dve.wait_ge(HY_DVE.sem, HY_DVE.after("xa"))
            for k in range(4):
                convolve(k)
            dve_ahead.before(dve, n + 3)
            dve.wait_ge(weights_used, n + 4)
            HY_DVE.done(nc.vector.tensor_tensor(h_x[:, 4:7, PADC:PADC + T], ps[:, 0:3, 0:T], repeated(r_row[:, :], 1, 3), ALU.mult), "xb")
            dve.wait_ge(HY_DVE.sem, HY_DVE.after("xb"))
            for k in range(4, XT):
                m = convolve(k)
            HY_DVE.done(m, "conv")
            dve_ahead.before(dve, n + 5)
            dve.wait_ge(weights_used, n + 6)
            for tt in range(TT):
                nc.vector.scalar_tensor_tensor(out=h_raw[:, tt * SH:(tt + 1) * SH], in0=bank(3 + 3 * tt, SH),
                                               scalar=rstd[:, tt:tt + 1], in1=dt_bias[:, :], op0=ALU.mult, op1=ALU.add)
            HY_DVE.done(nc.vector.tensor_tensor(h_p[:, :, PADP:PADP + T], ps[:, 4:6, 0:T], repeated(r_row[:, :], 1, 2), ALU.mult), "tail")
            dve.wait_ge(HY_DVE.sem, HY_DVE.after("tail"))
            HY_DVE.done(nc.vector.scalar_tensor_tensor(out=h_abs, in0=h_raw, scalar=-1.0, in1=h_raw, op0=ALU.mult, op1=ALU.max), "abs")

            src = h_p
            for g in range(4):
                dst, w = h_sum[g % 2], 2 ** g
                dve_link(dve, nc.vector.tensor_tensor(dst[:, :, PADP:PADP + T], src[:, :, PADP:PADP + T], src[:, :, PADP - w:PADP - w + T], ALU.add))
                rows = slice(64 * (g % 2), 64 * (g % 2) + 64)
                d = h_diff[rows, g // 2, :]
                dve_link(dve, nc.vector.tensor_tensor(d, dst[rows, g // 2, PADP:PADP + T], h_count[rows, g // 2, :], ALU.mult))
                m = nc.vector.tensor_tensor(d, d, h_p[rows, g // 2, PADP:PADP + T], ALU.subtract)
                src = dst
            HY_DVE.done(m, "diff")

            dve.wait_ge(HY_ACT.sem, HY_ACT.after("exp_dt"))
            dve_link(dve, nc.vector.tensor_scalar(h_s, h_e, 2.0, None, ALU.add))
            dve_link(dve, nc.vector.reciprocal(h_s, h_s))
            dve_link(dve, nc.vector.tensor_tensor(h_s, h_s, h_e, ALU.mult))
            dve_link(dve, nc.vector.tensor_tensor(h_s2, h_s, h_s, ALU.mult))
            dve_link(dve, nc.vector.tensor_scalar(h_q, h_s2, 1 / 17, None, ALU.mult))
            for d in (15, 13, 11, 9, 7, 5, 3):
                dve_link(dve, nc.vector.scalar_tensor_tensor(out=h_q, in0=h_q, scalar=1 / d, in1=h_s2, op0=ALU.add, op1=ALU.mult))
            dve_link(dve, nc.vector.scalar_tensor_tensor(out=h_q, in0=h_q, scalar=1.0, in1=h_s, op0=ALU.add, op1=ALU.mult))
            dve_link(dve, nc.vector.tensor_scalar(h_raw, h_raw, 0.0, None, ALU.max))
            dve_link(dve, nc.vector.scalar_tensor_tensor(out=h_dt, in0=h_q, scalar=2.0, in1=h_raw, op0=ALU.mult, op1=ALU.add))
            dve.wait_ge(HY_ACT.sem, HY_ACT.after("ea"))
            v2 = h_dt.rearrange("p (t h) -> p t h", t=TT)
            HY_DVE.done(nc.vector.scalar_tensor_tensor(out=h_da.rearrange("p (t h) -> p t h", t=TT), in0=v2, scalar=-1.0,
                                                       in1=repeated(h_ea, 1, TT), op0=ALU.mult, op1=ALU.mult), "da")
            dve_ahead.before(dve, n + 7)
            dve.wait_ge(HY_ACT.sem, HY_ACT.after("xs_rows"))
            xs = h_xs.rearrange("p t n -> p (t n)").rearrange("p (n d) -> p n d", d=SD)
            xdt = h_xdt.rearrange("p t n -> p (t n)").rearrange("p (n d) -> p n d", d=SD)
            HY_DVE.done(nc.vector.tensor_tensor(xdt, xs, repeated(h_dt, 2, SD), ALU.mult), "xdt")
            dve_ahead.before(dve, n + 9)
            dve_ahead.before(dve, n + 11)
            dve.wait_ge(HY_PE.sem, HY_PE.after("cumulated"))
            HY_DVE.done(nc.vector.tensor_copy(h_acum, bank(3, N12)), "acum")
            dve.wait_ge(HY_DVE.sem, HY_DVE.after("acum"))
            acb = ps[:, 0:3, :].rearrange("p b n -> p (b n)").rearrange("p (n l) -> p n l", l=P)
            dve_link(dve, nc.vector.tensor_tensor(h_decay, acb, repeated(h_acum, 2, P), ALU.subtract))
            HY_DVE.done(nc.vector.tensor_tensor(h_decay, h_decay, repeated(h_neg, 1, N12), ALU.add), "decay")
            dve.wait_ge(HY_PE.sem, HY_PE.after("cb_pool"))
            nc.vector.tensor_tensor(xn[:, :, 768:1024], bank(5).rearrange("p (t n) -> p t n", t=TT), repeated(pool_gain[:, :], 1, TT), ALU.mult)
            dve.wait_ge(HY_ACT.sem, HY_ACT.after("decay"))
            xw = h_xw.rearrange("p (h d) -> p h d", d=SD)
            HY_DVE.done(nc.vector.tensor_tensor(xw, xdt[:, 0:SH, :], repeated(h_decay[:, 0:SH, P - 1], 2, SD), ALU.mult), "xw")
            dve.wait_ge(HY_DVE.sem, HY_DVE.after("xw"))
            for tt in range(TT):
                cb = bank(4)[:, tt * SG * P:(tt + 1) * SG * P].rearrange("p (g l) -> p g l", g=SG)
                v = h_decay[:, tt * SH:(tt + 1) * SH, :].rearrange("p (g r) l -> p g r l", g=SG)
                m = nc.vector.tensor_tensor(v, v, repeated(cb, 2, SR), ALU.mult)
            HY_DVE.done(m, "scores")
            dve.wait_ge(HY_PE.sem, HY_PE.after("state"))
            HY_DVE.done(nc.vector.tensor_copy(h_state, bank(2, SH * SD)), "state")
            dve.wait_ge(HY_PE.sem, HY_PE.after("y"))
            dve.wait_ge(HY_ACT.sem, HY_ACT.after("exp_acum"))
            y = h_y.rearrange("p t n -> p (t n)").rearrange("p (n d) -> p n d", d=SD)
            dve_link(dve, skip(y, xs))
            dve_link(dve, nc.vector.tensor_tensor(h_y, h_y, ps[:, 0:2, 0:SH * SD], ALU.add))
            yo = h_ysq[:, 1, :].rearrange("p (h d) -> p h d", d=SD)
            HY_DVE.done(nc.vector.tensor_tensor(yo, bank(3, SH * SD).rearrange("p (h d) -> p h d", d=SD),
                                                repeated(h_eacum[:, SH:N12], 2, SD), ALU.mult), "y_off")
            dve.wait_ge(HY_DVE.sem, HY_DVE.after("y_off"))
            dve_link(dve, nc.vector.tensor_tensor(h_y[:, 1, :], h_y[:, 1, :], h_ysq[:, 1, :], ALU.add))
            dve.wait_ge(HY_ACT.sem, HY_ACT.after("silu_z"))
            dve_link(dve, nc.vector.tensor_tensor(h_y, h_y, h_z, ALU.mult))
            dve_link(dve, nc.vector.tensor_tensor(h_ysq, h_y, h_y, ALU.mult))
            HY_DVE.done(nc.vector.tensor_reduce(h_yss, h_ysq.rearrange("p t n -> p (t n)").rearrange("p (n d) -> p n d", d=SR * SD),
                                                AX.X, ALU.add), "y_squares")
            dve_link(dve, nc.vector.tensor_tensor(h_y, h_y, repeated(ssd_gain[:, :], 1, TT), ALU.mult))
            dve.wait_ge(HY_POOL.sem, HY_POOL.after("y_rstd"))
            nc.vector.tensor_tensor(xn[:, :, 384:768].rearrange("p t (g d) -> p t g d", g=SG),
                                    h_y.rearrange("p t (g d) -> p t g d", g=SG),
                                    repeated(h_yrs.rearrange("p (t g) -> p t g", t=TT), 3, SR * SD), ALU.mult)
            hyb_attn.dve(dve)
            dve.wait_ge(hyb_attn.dve_done.sem, hyb_attn.dve_done.after(f"rows{GH - 1}"))
            dve.sem_inc(rows_ready, TT)
            turn_dve(dve, s, 1, KT)
            add_result(dve, s, 1.0)

        def skip(y, xs):
            for tt in range(TT):
                m = nc.vector.tensor_tensor(y[:, tt * SH:(tt + 1) * SH, :], xs[:, tt * SH:(tt + 1) * SH, :],
                                            repeated(d_skip[:, :], 2, SD), ALU.mult)
            return m

        PARAM_ROWS = [(rows_a, GAINS, io["norm_gains"].rearrange("l n (k p) -> (l n k) p", p=P)),
                      (rows_a, MIX2, io["norm_mix_2"].rearrange("o (k p) -> (o k) p", p=P)),
                      (rows_a, FFN2, io["norm_ffn_2"].rearrange("o (k p) -> (o k) p", p=P)),
                      (rows_a, QA, io["mla_q_a_norm"].rearrange("o (k p) -> (o k) p", p=P)),
                      (rows_a, KVA, io["mla_kv_a_norm"].rearrange("o (k p) -> (o k) p", p=P)),
                      (rows_a, BS, io["gmlp_b_s"].rearrange("o h p -> (o h) p")),
                      (rows_a, LB, io["hgrn_lb_raw"].rearrange("o (k p) -> (o k) p", p=P)),
                      (rows_a, QN, io["mla_q_norm"][:, 0:P]),
                      (rows_a, KN, io["mla_k_norm"][:, 0:P]),
                      (rows_b, CONVW, io["conv_w_2"].rearrange("o w (k p) -> (o w k) p", p=P)),
                      (rows_b, CONVB, io["conv_b_2"].rearrange("o (k p) -> (o k) p", p=P))]

        def load_rows(q, which):
            for dst, at, v in which:
                q.dma_start(dst[at:at + v.shape[0], :], v).then_inc(rows_loaded, 16)

        def load_repeated(q):
            q.dma_start(pos_i[:, :], io["positions"].rearrange("o (t p) -> p (o t)", p=P),
                        allow_slow_non_contiguous=True).then_inc(params_loaded, 16)
            for dst, v in ((vnorm[:, :], io["gmlp_v_norm"].rearrange("o h d -> o (h d)")), (onorm[:, :], io["hgrn_out_norm"]),
                           (qk_norm[:, 0, :], io["mla_q_norm"][:, P:]), (qk_norm[:, 1, :], io["mla_k_norm"][:, P:]),
                           (ssd_gain[:, :], io["ssd_norm_2"]), (pool_gain[:, :], io["pool_scale_2"]), (dt_bias[:, :], io["dt_bias_2"]),
                           (a_log[:, :], io["a_log_2"]), (d_skip[:, :], io["d_skip_2"])):
                q.dma_start(dst, v.partition_broadcast(P)).then_inc(params_loaded, 16)
        ROWS_DMAS, PARAM_DMAS = len(PARAM_ROWS), 10

        def final_dve(dve):
            last = len(PLAN)
            if last == 10:
                dve.wait_ge(gain_loaded, 16 * (PLAN.count("ple") + 1))
            for tt in range(TT):
                if last < 10:
                    dve.wait_ge(rstd_ready, TT * last + tt + 1)
                    nc.vector.tensor_copy(xn[:, tt, :], x[:, tt, :]).then_inc(rows_ready, 1)
                    continue
                dve.wait_ge(rstd_ready, TT * last + tt + 1)
                nc.vector.scalar_tensor_tensor(out=xn[:, tt, :], in0=x[:, tt, :], scalar=rstd[:, tt:tt + 1],
                                               in1=gain_row[:, :], op0=ALU.mult, op1=ALU.mult).then_inc(rows_ready, 1)

        block = stack.enter_context(nc.Block())

        @block.sync
        def _(sp):
            for tt in range(TT):
                sp.dma_start(x[:, tt, :], io["x"][0, tt * P:(tt + 1) * P, :]).then_inc(x_loaded, 16)
            load_rows(sp, PARAM_ROWS[6:])
            for s, name in enumerate(PLAN):
                n, f = base[s], fs[s]
                if name == "even":
                    even_load(sp, s)
                if name == "mla":
                    mla_load(sp, s)
                if name == "hybrid":
                    hybrid_load(sp, s)
                if name == "ple":
                    ple_load(sp, s, ples[s])
                if name == "ffn":
                    if f < 4:
                        l, j = divmod(f, 2)
                        ffn_load(sp, n, io["ffn_w_gate"][l, j], io["ffn_w_up"][l, j], io["ffn_w_down"][l, j])
                    else:
                        gu = io["w_gate_up_2"][0]
                        ffn_load(sp, n, gu[:, 0:FF], gu[:, FF:2 * FF], io["w_down_2"][0])
            for tt in range(TT):
                sp.wait_ge(rows_ready, TT * calls_so_far + tt + 1)
                sp.dma_start(out[0, tt * P:(tt + 1) * P, :], xn[:, tt, :]).then_inc(stored, 16)
            sp.wait_ge(stored, 16 * TT)

        @block.gpsimd
        def _(pool):
            pool_link(pool, nc.gpsimd.memset(ident[:, :], 0.0))
            nc.gpsimd.affine_select(out=ident[:, :], in_=ident[:, :], compare_op=ALU.not_equal, fill=1.0, base=0,
                                    pattern=[[-1, P]], channel_multiplier=1).then_inc(ident_ready, 1)
            pool_link(pool, nc.gpsimd.memset(minus_half[:, :], -0.5))
            for j in range(32):
                m = nc.gpsimd.memset(inv_freq[:, j:j + 1], 10000.0 ** (-2 * j / 64))
            m.then_inc(consts_ready, 1)
            nc.gpsimd.memset(ones[:, :], 1.0).then_inc(consts_ready, 1)
            load_repeated(pool)
            for s, name in enumerate(PLAN):
                norm_pool(pool, s)
                if name == "even":
                    even_pool(pool, s)
                if name == "mla":
                    mla_pool(pool, s)
                if name == "hybrid":
                    hybrid_pool(pool, s)
                if name == "ple":
                    ple_pool(pool, s, ples[s])
            norm_pool(pool, len(PLAN))

        @block.scalar
        def _(act):
            load_rows(act, PARAM_ROWS[0:6])
            act.wait_ge(cols_turned, 1)
            nc.scalar.activation(cols[:, :], ps[:, 3, 0:ROWS_A], ACT.Copy).then_inc(cols_ready, 1)
            nc.scalar.activation(conv_cols[:, :], ps[:, 3, P:P + ROWS_B], ACT.Copy).then_inc(cols_ready, 1)
            act.wait_ge(cols_ready, 2)
            act.wait_ge(lb_steps, 1)
            nc.scalar.activation(lb[:, 1, :], lb[:, 0, :], ACT.Exp).then_inc(lb_steps, 1)
            act_ahead.through(act, 0)
            for s, name in enumerate(PLAN):
                if name == "even":
                    even_act(act, s)
                if name == "mla":
                    mla_act(act, s)
                if name == "hybrid":
                    hybrid_act(act, s)
                if name == "ple":
                    ple_act(act, s, ples[s])
                if name == "ffn":
                    if s == len(PLAN) - 1:
                        act.wait_ge(x_ready, 4 * s)
                        act.dma_start(gain_row[:, :], io["norm_final_2"].rearrange("(o n) -> o n", o=1).partition_broadcast(P))\
                           .then_inc(gain_loaded, 16)
                    ffn_act(act, base[s], s, fs[s])
            norm_act(act, len(PLAN), None)

        @block.vector
        def _(dve):
            dve.wait_ge(cols_ready, 2)
            dve.wait_ge(consts_ready, 2)
            nc.vector.tensor_tensor(lb[:, 0, :], cols[:, LB:LB + 4], cols[:, LB:LB + 4], ALU.subtract).then_inc(lb_steps, 1)
            dve.wait_ge(lb_steps, 2)
            dve_link(dve, nc.vector.reciprocal(lb[:, 2, :], lb[:, 1, :]))
            dve_link(dve, nc.vector.tensor_tensor(lb[:, 2, :], lb[:, 2, :], lb[:, 1, :], ALU.mult))
            dve_link(dve, nc.vector.tensor_tensor(lb[:, 0, :], lb[:, 2, :], lb[:, 2, :], ALU.subtract))
            dve_link(dve, nc.vector.tensor_scalar(lb[:, 0, :], lb[:, 0, :], 0.0, 0.999, ALU.max, ALU.min))
            dve_link(dve, nc.vector.tensor_scalar(lb[:, 1, :], lb[:, 0, :], -1.0, 1.0, ALU.mult, ALU.add))
            dve_ahead.through(dve, 0)
            for s, name in enumerate(PLAN):
                if s == 1:
                    dve.wait_ge(params_loaded, 16 * PARAM_DMAS)
                if name == "even":
                    even_dve(dve, s)
                if name == "mla":
                    mla_dve(dve, s)
                if name == "hybrid":
                    hybrid_dve(dve, s)
                if name == "ple":
                    ple_dve(dve, s, ples[s])
                if name == "ffn":
                    ffn_dve(dve, base[s], s, fs[s])
            final_dve(dve)

        @block.tensor
        def _(pe):
            pe.wait_ge(rows_loaded, 16 * ROWS_DMAS)
            pe.wait_ge(ident_ready, 1)
            nc.tensor.transpose(ps[:, 3, 0:ROWS_A], rows_a[0:ROWS_A, :], ident[0:ROWS_A, 0:ROWS_A])
            nc.tensor.transpose(ps[:, 3, P:P + ROWS_B], rows_b[0:ROWS_B, :], ident[0:ROWS_B, 0:ROWS_B]).then_inc(cols_turned, 1)
            pe.wait_ge(cols_ready, 2)
            for s, name in enumerate(PLAN):
                if name == "even":
                    even_pe(pe, s)
                if name == "mla":
                    mla_pe(pe, s)
                if name == "hybrid":
                    hybrid_pe(pe, s)
                if name == "ple":
                    ple_pe(pe, s, ples[s])
                if name == "ffn":
                    ffn_pe(pe, base[s], s, fs[s])


INPUTS = ["x", "p", "positions", "norm_gains", "ffn_w_gate", "ffn_w_up", "ffn_w_down", "ple_w_gate", "ple_w_proj",
          "even_w_in", "gmlp_v_norm", "gmlp_w_s", "gmlp_b_s", "hgrn_lb_raw", "hgrn_out_norm", "even_w_out",
          "mla_w_in", "mla_q_a_norm", "mla_kv_a_norm", "mla_w_q_b", "mla_w_kv_b", "mla_q_norm", "mla_k_norm",
          "mla_w_out", "norm_mix_2", "w_in_2", "conv_w_2", "conv_b_2", "dt_bias_2", "a_log_2", "d_skip_2",
          "ssd_norm_2", "pool_w_2", "pool_scale_2", "w_out_2", "norm_ffn_2", "w_gate_up_2", "w_down_2", "norm_final_2"]


def kernel(**inputs):
    import numpy as np
    import concourse.bacc as bacc
    from concourse.bass_utils import run_bass_kernel_spmd

    nc = bacc.Bacc("TRN2", target_bir_lowering=False, num_devices=1)
    arrays, io = {}, {}
    for name in INPUTS:
        a = np.ascontiguousarray(inputs[name])
        arrays["in_" + name] = a
        io[name] = nc.dram_tensor("in_" + name, a.shape, mybir.dt.from_np(a.dtype), kind="ExternalInput").ap()
    out = nc.dram_tensor("out", inputs["x"].shape, mybir.dt.float32, kind="ExternalOutput").ap()
    build_block(nc, io, out)
    r = run_bass_kernel_spmd(nc, [arrays], core_ids=[0])
    return r.results[0]["out"]
```

```python
import math
from contextlib import ExitStack

import concourse.bass as bass
from concourse import mybir


class Steps:

    def __init__(self, sem, names, calls=1):
        self.sem, self.names, self.calls, self.said = sem, names, calls, 0

    def after(self, name, call=0):
        return call * len(self.names) + self.names.index(name) + 1

    def done(self, instruction, name, call=0):
        self.said += 1
        assert self.said == self.after(name, call), (name, self.names[(self.said - 1) % len(self.names)])
        instruction.then_inc(self.sem, 1)


def build_block(nc, io, out):
    f32, f32r, i32 = mybir.dt.float32, mybir.dt.float32r, mybir.dt.int32
    ALU, ACT, AX = mybir.AluOpType, mybir.ActivationFunctionType, mybir.AxisListType

    P = 128
    T, D = io["x"].shape[1:]
    TT = T // P
    KT = D // P
    FF = io["ffn_w_gate"].shape[3]
    HC = 256
    NCH = FF // HC
    EPS = 1e-6
    assert T == 256 and D == 1024 and FF % HC == 0

    SLOT = 2048
    RING = 3
    FFN_SLOTS = 3 * NCH
    PLAN = ["ffn", "even", "ffn", "ple", "ffn", "mla", "ffn", "ple", "hybrid", "ffn"]
    SLOTS_OF = {"ffn": FFN_SLOTS, "even": 16, "ple": 5, "mla": 12, "hybrid": 16}
    base, total = [], 0
    for name in PLAN:
        base.append(total)
        total += SLOTS_OF[name]

    FEATURES_OF = {"ffn": [KT], "even": [KT, KT], "ple": [2, KT], "mla": [KT, 5, KT], "hybrid": [KT, KT]}
    features_base, banks_so_far, calls_so_far = [], 0, 0
    call_base, bank_base = [], []
    for name in PLAN:
        call_base.append([])
        bank_base.append([])
        for c, n in enumerate(FEATURES_OF[name]):
            call_base[-1].append(calls_so_far)
            bank_base[-1].append(banks_so_far)
            banks_so_far += (n + 1) // 2
            calls_so_far += c > 0 and name == "even"

    GAINS, MIX2, FFN2, QA, KVA, BS, LB, QN, KN = 0, 80, 88, 96, 99, 101, 109, 113, 114
    ROWS_A = 115
    CONVW, CONVB, ROWS_B = 0, 28, 35

    with ExitStack() as stack:
        def sb(name, shape, dt=f32):
            return stack.enter_context(nc.sbuf_tensor(name, shape, dt))

        def sem(name):
            return stack.enter_context(nc.semaphore(name))

        raw = sb("raw", [P, RING, SLOT])
        wh = sb("wh", [P, RING, SLOT], f32r)
        wl = sb("wl", [P, RING, SLOT], f32r)
        x = sb("x_rows", [P, TT, D])
        xn = sb("xn", [P, TT, D])
        hth = sb("hth", [P, KT, T], f32r)
        htl = sb("htl", [P, KT, T], f32r)
        silu_g = sb("silu_g", [P, TT, HC])
        prod = sb("prod", [P, TT, HC])
        prod_h = sb("prod_h", [P, 2, T], f32r)
        prod_l = sb("prod_l", [P, 2, T], f32r)
        r_diag = silu_g[:, 0, :].rearrange("p (t n) -> p t n", t=TT)
        ident = sb("ident", [P, P])
        rows_a = sb("rows_a", [P, P])
        rows_b = sb("rows_b", [P, P])
        cols = sb("cols", [P, ROWS_A])
        conv_cols = sb("conv_cols", [P, ROWS_B])
        r_row = sb("r_row", [P, T])
        ones = sb("ones", [P, P])
        mean_sq = sb("mean_sq", [P, TT])
        rstd = sb("rstd", [P, TT])
        minus_half = sb("minus_half", [P, 16])
        gain_row = sb("gain_row", [P, D])
        vnorm = sb("vnorm", [P, 512])
        onorm = sb("onorm", [P, 128])
        qk_norm = sb("qk_norm", [P, 2, 64])
        ssd_gain = sb("ssd_gain", [P, 384])
        pool_gain = sb("pool_gain", [P, 256])
        dt_bias = sb("dt_bias", [P, 6])
        a_log = sb("a_log", [P, 6])
        d_skip = sb("d_skip", [P, 6])
        inv_freq = sb("inv_freq", [P, 32])
        pos_i = sb("pos_i", [P, TT], i32)
        lb = sb("lb", [P, 3, 4])
        arena = sb("arena", [P, 20040])
        ps = stack.enter_context(nc.psum_tensor("ps", [P, 8, 512], f32))

        def bank(b, w=512):
            return ps[:, b, 0:w]

        raw_loaded = [sem(f"raw_loaded{r}") for r in range(RING)]
        high_ready = sem("high_ready")
        split_ready = sem("split_ready")
        weights_used = sem("weights_used")
        x_loaded = sem("x_loaded")
        params_loaded = sem("params_loaded")
        rows_loaded = sem("rows_loaded")
        ident_ready = sem("ident_ready")
        consts_ready = sem("consts_ready")
        cols_turned = sem("cols_turned")
        cols_ready = sem("cols_ready")
        x_ready = sem("x_ready")
        half_ready = sem("half_ready")
        r_steps = sem("r_steps")
        sq_ready = sem("sq_ready")
        rstd_ready = sem("rstd_ready")
        rows_ready = sem("rows_ready")
        turned = sem("turned")
        cols_high = sem("cols_high")
        cols_low = sem("cols_low")
        silu_ready = sem("silu_ready")
        prod_ready = sem("prod_ready")
        prod_turned = sem("prod_turned")
        prod_high = sem("prod_high")
        prod_low = sem("prod_low")
        gain_loaded = sem("gain_loaded")
        stored = sem("stored")
        lb_steps = sem("lb_steps")
        act_chain, dve_chain, pool_chain = sem("act_chain"), sem("dve_chain"), sem("pool_chain")

        class Chain:

            def __init__(self, s):
                self.sem, self.n = s, 0

            def __call__(self, eng, instruction):
                self.n += 1
                instruction.then_inc(self.sem, 1)
                eng.wait_ge(self.sem, self.n)

        act_link, dve_link, pool_link = Chain(act_chain), Chain(dve_chain), Chain(pool_chain)

        def load_slot(sp, n, pieces):
            if n >= RING:
                sp.wait_ge(split_ready, n - RING + 1)
            assert len(pieces) == 2
            for dst, src in pieces:
                sp.dma_start(dst, src).then_inc(raw_loaded[n % RING], 16)

        def raw_view(n, k, w):
            return raw[:, n % RING, 0:k * w].rearrange("p (k n) -> p k n", k=k)

        width = [SLOT] * total
        for s, name in enumerate(PLAN):
            if name == "mla":
                width[base[s] + 2] = 8 * 192
                for j in range(3):
                    width[base[s] + 5 + j] = 3 * 512
            if name == "hybrid":
                for j in range(2):
                    width[base[s] + 2 + j] = 4 * 384
                    width[base[s] + 4 + j] = 4 * 262

        def split_high(act, n):
            act.wait_ge(raw_loaded[n % RING], 32 * (n // RING + 1))
            if n >= RING:
                act.wait_ge(weights_used, n - RING + 1)
            nc.scalar.activation(wh[:, n % RING, 0:width[n]], raw[:, n % RING, 0:width[n]], ACT.Copy)\
              .then_inc(high_ready, 1)

        def split_low(dve, n):
            dve.wait_ge(high_ready, n + 1)
            nc.vector.tensor_tensor(wl[:, n % RING, 0:width[n]], raw[:, n % RING, 0:width[n]],
                                    wh[:, n % RING, 0:width[n]].bitcast(f32), ALU.subtract)\
              .then_inc(split_ready, 1)

        class Ahead:

            def __init__(self, split):
                self.split, self.n = split, 0

            def through(self, eng, n):
                while self.n <= min(n, total - 1):
                    self.split(eng, self.n)
                    self.n += 1

            def before(self, eng, n):
                self.through(eng, n + RING - 1)

        act_ahead, dve_ahead = Ahead(split_high), Ahead(split_low)

        def take_slot(pe, n):
            pe.wait_ge(split_ready, n + 1)

        def product(o, xh, xl, a, b, first, last):
            nc.tensor.matmul(o, xh, b, start=first, stop=False)
            nc.tensor.matmul(o, xh, a, start=False, stop=False)
            return nc.tensor.matmul(o, xl, a, start=False, stop=last)

        def by_rows(outs, k, n, kk, w, first, last, off=0, cols_n=None):
            c = cols_n or w
            a, b = wh[:, n % RING, kk * w + off:kk * w + off + c], wl[:, n % RING, kk * w + off:kk * w + off + c]
            for tt in range(TT):
                m = product(outs[tt], hth[:, k, tt * P:(tt + 1) * P], htl[:, k, tt * P:(tt + 1) * P], a, b, first, last)
            return m

        def by_columns(o, k, n, kk, w, off, first, last):
            c = kk * w + off
            a, b = wh[:, n % RING, c:c + P], wl[:, n % RING, c:c + P]
            nc.tensor.matmul(o, b, hth[:, k, :], start=first, stop=False)
            nc.tensor.matmul(o, a, hth[:, k, :], start=False, stop=False)
            return nc.tensor.matmul(o, a, htl[:, k, :], start=False, stop=last)

        def project_out(pe, s, c, n, by_halves=True, rest=None, order=(0, 1, 2, 3)):
            for j in range(4):
                take_slot(pe, n + j)
                turned_by(pe, s, c, j + 1)
                pieces = [(kk, half, tt) for kk in range(2) for half in range(2) for tt in range(TT)]
                if j == 3:
                    pieces.sort(key=lambda v: v[1] if by_halves else v[2])
                for i, (kk, half, tt) in enumerate(pieces):
                    k, at = 2 * order[j] + kk, kk * D + half * 512
                    m = product(bank(4 + 2 * tt + half), hth[:, k, tt * P:(tt + 1) * P], htl[:, k, tt * P:(tt + 1) * P],
                                wh[:, (n + j) % RING, at:at + 512], wl[:, (n + j) % RING, at:at + 512], j + kk == 0, j + kk == 4)
                    if j == 3 and i == 3:
                        m.then_inc(half_ready if by_halves else tile_ready, 1)
                    if j == 1 and i == 3 and rest is not None:
                        rest()
                m.then_inc(weights_used, 1)

        def load_square(sp, n, w, order=(0, 1, 2, 3)):
            v = w.rearrange("(k p) n -> p k n", p=P)
            for s, b in enumerate(order):
                load_slot(sp, n + s, [(raw_view(n + s, 2, D)[:, j:j + 1, :], v[:, 2 * b + j:2 * b + j + 1, :])
                                      for j in range(2)])

        def load_columns(sp, n, w, c0, c):
            v = w.rearrange("(k p) n -> p k n", p=P)
            for s in range(2):
                load_slot(sp, n + s, [(raw_view(n + s, 4, c)[:, 2 * j:2 * j + 2, :],
                                       v[:, 4 * s + 2 * j:4 * s + 2 * j + 2, c0:c0 + c]) for j in range(2)])

        def rows_product(pe, n, outs, first_of=None, halfway=None):
            for half in range(2):
                take_slot(pe, n + half)
                for kk in range(4):
                    if first_of is not None and kk % 2 == 0:
                        turned_by(pe, first_of, 0, 2 * half + kk // 2 + 1)
                    m = by_rows(outs, 4 * half + kk, n + half, kk, 512, half + kk == 0, half + kk == 4)
                m.then_inc(weights_used, 1)
                if half == 0 and halfway is not None:
                    halfway()

        def columns_product(pe, n, outs, w, first_of=None):
            for half in range(2):
                take_slot(pe, n + half)
                for kk in range(4):
                    if first_of is not None and kk % 2 == 0:
                        turned_by(pe, first_of, 0, 2 * half + kk // 2 + 1)
                    for j, o in enumerate(outs):
                        m = by_columns(o, 4 * half + kk, n + half, kk, w, j * P, half + kk == 0, half + kk == 4)
                m.then_inc(weights_used, 1)

        def turn_bank(b, n_k, src, to):
            for k in range(2 * b, min(2 * b + 2, n_k)):
                for tt in range(TT):
                    at = (k % 2) * T + tt * P
                    m = nc.tensor.transpose(ps[:, to, at:at + P], src[:, tt, k * P:(k + 1) * P], ident[:, :])
            m.then_inc(turned, 1)

        def turn_x(pe, s, b, to):
            if s == 0:
                pe.wait_ge(x_loaded, 16 * TT)
            else:
                pe.wait_ge(x_ready, 4 * (s - 1) + 2 * (b // 2 + 1))
            turn_bank(b, KT, x, to)

        def turn_act(act, s, c, n_k, gain=None, banks=(0, 1, 2, 3), dst=None, part=None, order=(0, 1, 2, 3)):
            dst = hth if dst is None else dst
            for i in range(*(part or (0, (n_k + 1) // 2))):
                b = order[i]
                act.wait_ge(turned, bank_base[s][c] + i + 1)
                for k in range(2 * b, min(2 * b + 2, n_k)):
                    o = (k % 2) * T
                    g = 1.0 if gain is None else cols[:, gain + k:gain + k + 1]
                    m = nc.scalar.activation(dst[:, k, :], ps[:, banks[b], o:o + T], ACT.Copy, scale=g)
                m.then_inc(cols_high, 1)

        def turn_dve(dve, s, c, n_k, gain=None, banks=(0, 1, 2, 3), dst=None, dst_h=None, part=None, order=(0, 1, 2, 3)):
            dst = htl if dst is None else dst
            dst_h = hth if dst_h is None else dst_h
            for i in range(*(part or (0, (n_k + 1) // 2))):
                b = order[i]
                dve.wait_ge(cols_high, bank_base[s][c] + i + 1)
                for k in range(2 * b, min(2 * b + 2, n_k)):
                    o = (k % 2) * T
                    g = 1.0 if gain is None else cols[:, gain + k:gain + k + 1]
                    m = nc.vector.scalar_tensor_tensor(out=dst[:, k, :], in0=ps[:, banks[b], o:o + T], scalar=g,
                                                       in1=dst_h[:, k, :].bitcast(f32), op0=ALU.mult, op1=ALU.subtract)
                m.then_inc(cols_low, 1)

        def turned_by(pe, s, c, banks_n):
            pe.wait_ge(cols_low, bank_base[s][c] + banks_n)

        def norm_act(act, s, gain, banks=(0, 1, 2, 3)):
            if gain is not None:
                turn_act(act, s, 0, KT, gain, banks, part=(0, 2))
                act_ahead.through(act, base[s] + 1)
                turn_act(act, s, 0, KT, gain, banks, part=(2, 4))
            if s == 0:
                act.wait_ge(x_loaded, 16 * TT)
            else:
                act.wait_ge(x_ready, 4 * s)
            for tt in range(TT):
                nc.scalar.activation(xn[:, tt, :], x[:, tt, :], ACT.Square, scale=1 / math.sqrt(D),
                                     accum_out=mean_sq[:, tt:tt + 1]).then_inc(sq_ready, 1)

        def norm_pool(pool, s):
            for tt in range(TT):
                pool.wait_ge(sq_ready, TT * s + tt + 1)
                pool_link(pool, nc.gpsimd.tensor_scalar(mean_sq[:, tt:tt + 1], mean_sq[:, tt:tt + 1], EPS, None, ALU.add))
                nc.gpsimd.tensor_tensor(rstd[:, tt:tt + 1], mean_sq[:, tt:tt + 1], minus_half[:, 0:1], ALU.pow)\
                  .then_inc(rstd_ready, 1)

        def norm_dve(dve, s, gain, banks=(0, 1, 2, 3)):
            turn_dve(dve, s, 0, KT, gain, banks, part=(0, 2))
            dve_ahead.through(dve, base[s] + 1)
            turn_dve(dve, s, 0, KT, gain, banks, part=(2, 4))

        def rms(eng, s):
            eng.wait_ge(rstd_ready, TT * (s + 1))

        def rms_diagonals(dve, s, r):
            rms(dve, s)
            for tt in range(TT):
                m = nc.vector.tensor_scalar(r_diag[:, tt, :], ident[:, :], rstd[:, tt:tt + 1], None, ALU.mult)
            m.then_inc(r_steps, 1)

        def rms_row_pe(pe, r, b):
            pe.wait_ge(r_steps, 3 * r + 1)
            for tt in range(TT):
                m = nc.tensor.matmul(ps[:, b, tt * P:(tt + 1) * P], ones[:, :], r_diag[:, tt, :], start=True, stop=True)
            m.then_inc(r_steps, 1)

        def rms_row(dve, r, b):
            dve.wait_ge(r_steps, 3 * r + 2)
            nc.vector.tensor_copy(r_row[:, :], bank(b, T)).then_inc(r_steps, 1)
            dve.wait_ge(r_steps, 3 * r + 3)

        def add_result(dve, s, scale):
            dve_ahead.before(dve, base[s] + SLOTS_OF[PLAN[s]] - 1)
            for half in range(2):
                if half == 0:
                    dve.wait_ge(half_ready, len([p for p in PLAN[:s] if p != "ple"]) + 1)
                else:
                    dve.wait_ge(weights_used, base[s] + SLOTS_OF[PLAN[s]])
                for tt in range(TT):
                    a = x[:, tt, half * 512:(half + 1) * 512]
                    nc.vector.scalar_tensor_tensor(out=a, in0=bank(4 + 2 * tt + half), scalar=scale, in1=a,
                                                   op0=ALU.mult, op1=ALU.add).then_inc(x_ready, 1)

        def ffn_load(sp, n, w_gate, w_up, w_down):
            g = w_gate.rearrange("(k p) n -> p k n", p=P)
            u = w_up.rearrange("(k p) n -> p k n", p=P)
            d = w_down.rearrange("(k p) n -> p k n", p=P)

            def gate_up(slot, half, c0):
                v = raw_view(slot, 4, 2 * HC)
                return [(v[:, :, 0:HC], g[:, 4 * half:4 * half + 4, bass.ds(c0, HC)]),
                        (v[:, :, HC:2 * HC], u[:, 4 * half:4 * half + 4, bass.ds(c0, HC)])]

            def down(slot, k0):
                v = raw_view(slot, 2, D)
                return [(v[:, j:j + 1, :], d[:, bass.ds(k0 + j, 1), :]) for j in range(2)]

            for j in range(2):
                load_slot(sp, n + j, gate_up(n + j, j, 0))
            with sp.Fori(0, NCH - 1) as i:
                for j in range(3):
                    sp.wait_ge(split_ready, i * 3 + (n + 2 + j - RING + 1))
                    pieces = gate_up(n + 2 + j, j, i * HC + HC) if j < 2 else down(n + 4, i * 2)
                    for dst, src in pieces:
                        sp.dma_start(dst, src).then_inc(raw_loaded[(n + 2 + j) % RING], 16)
            load_slot(sp, n + FFN_SLOTS - 1, down(n + FFN_SLOTS - 1, 2 * (NCH - 1)))

        def ffn_pe(pe, n, s, f):
            def gate_up(place, k, b=0):
                m = by_rows([bank(b), bank(b + 1)], k, place, k % 4, 2 * HC, k == 0, k == KT - 1)
                if k % 4 == 3:
                    m.then_inc(weights_used, 1)

            def down(place, first, last, halfway=None):
                h, l = (last_h, last_l) if last else (prod_h, prod_l)
                pieces = [(kk, tt, half) for kk in range(2) for tt in range(TT) for half in range(2)]
                if last:
                    pieces.sort(key=lambda v: v[2])
                for i, (kk, tt, half) in enumerate(pieces):
                    at = kk * D + half * 512
                    m = product(bank(4 + 2 * tt + half), h[:, kk, tt * P:(tt + 1) * P], l[:, kk, tt * P:(tt + 1) * P],
                                wh[:, place % RING, at:at + 512], wl[:, place % RING, at:at + 512],
                                first and kk == 0, last and kk == 1)
                    if last and i == 3:
                        m.then_inc(half_ready, 1)
                    if halfway is not None and i == 3:
                        halfway()
                m.then_inc(weights_used, 1)

            def turn_product(b=2):
                for kk in range(2):
                    for tt in range(TT):
                        at = kk * T + tt * P
                        m = nc.tensor.transpose(ps[:, b, at:at + P], prod[:, tt, kk * P:(kk + 1) * P], ident[:, :])
                m.then_inc(prod_turned, 1)

            def chunk(c, first):
                for half in range(2):
                    pe.wait_ge(split_ready, c * 3 + (n + half))
                    for kk in range(4):
                        gate_up(n + 2 + half, 4 * half + kk)
                pe.wait_ge(prod_low, c + f * NCH)
                pe.wait_ge(split_ready, c * 3 + (n + 2))
                down(n + 4, first, False)
                pe.wait_ge(prod_ready, c + (f * NCH + 1))
                turn_product()

            turn_x(pe, s, 0, FFN_BANKS[0])
            turn_x(pe, s, 1, FFN_BANKS[1])
            if s == 0:
                turn_x(pe, s, 2, FFN_BANKS[2])
                turn_x(pe, s, 3, FFN_BANKS[3])
            take_slot(pe, n)
            for b in range(4):
                turned_by(pe, s, 0, b + 1)
                if b == 2:
                    take_slot(pe, n + 1)
                for k in (2 * b, 2 * b + 1):
                    gate_up(n + b // 2, k)
                if b == 0 and s > 0:
                    turn_x(pe, s, 2, FFN_BANKS[2])
                    turn_x(pe, s, 3, FFN_BANKS[3])
            for half in range(2):
                take_slot(pe, n + 2 + half)
                for kk in range(4):
                    gate_up(n + 2 + half, 4 * half + kk, 2)
                if half == 0:
                    pe.wait_ge(prod_ready, f * NCH + 1)
                    turn_product(0)
            pe.wait_ge(prod_low, f * NCH + 1)
            take_slot(pe, n + 4)
            down(n + 4, True, False)
            pe.wait_ge(prod_ready, f * NCH + 2)
            turn_product()
            with pe.Fori(2, NCH - 1) as c:
                chunk(c, False)

            def turn_last():
                pe.wait_ge(prod_ready, (f + 1) * NCH)
                turn_product()

            c = NCH - 1
            for half in range(2):
                take_slot(pe, n + 3 * c - 1 + half)
                for kk in range(4):
                    gate_up(n + 3 * c - 1 + half, 4 * half + kk)
            pe.wait_ge(prod_low, c + f * NCH)
            take_slot(pe, n + 3 * c + 1)
            down(n + 3 * c + 1, False, False, turn_last)
            pe.wait_ge(prod_low, (f + 1) * NCH)
            take_slot(pe, n + FFN_SLOTS - 1)
            down(n + FFN_SLOTS - 1, False, True)

        def ffn_act(act, n, s, f):
            def silu(used, b=0):
                act.wait_ge(weights_used, used)
                for tt in range(TT):
                    nc.scalar.activation(silu_g[:, tt, :], ps[:, b + tt, 0:HC], ACT.Silu, scale=rstd[:, tt:tt + 1]).then_inc(silu_ready, 1)

            def high(c, b=2, to=prod_h):
                act.wait_ge(prod_turned, c + (f * NCH + 1))
                nc.scalar.activation(to[:, :, :], bank(b).rearrange("p (k t) -> p k t", k=2), ACT.Copy)\
                  .then_inc(prod_high, 1)

            def split(c, j):
                r = (n + j) % RING
                act.wait_ge(raw_loaded[r], c * 32 + 32 * ((n + j) // RING + 1))
                act.wait_ge(weights_used, c * 3 + (n + j - RING + 1))
                nc.scalar.activation(wh[:, r, :], raw[:, r, :], ACT.Copy).then_inc(high_ready, 1)

            norm_act(act, s, FFN_GAIN[f], FFN_BANKS)
            act_ahead.through(act, n + 3)
            rms(act, s)
            silu(n + 2)
            act_ahead.through(act, n + 4)
            high(0, 0)
            act_ahead.through(act, n + 5)
            silu(n + 4, 2)
            act_ahead.through(act, n + 6)
            high(1)
            with act.Fori(2, NCH - 1) as c:
                split(c, 1)
                split(c, 2)
                silu(c * 3 + (n + 1))
                split(c, 3)
                high(c)
            act_ahead.n += 3 * (NCH - 3)
            act_ahead.through(act, n + FFN_SLOTS - 1)
            silu(n + 3 * (NCH - 1) + 1)
            act_ahead.through(act, n + FFN_SLOTS)
            high(NCH - 1, to=last_h)
            act_ahead.before(act, n + FFN_SLOTS - 1)

        def ffn_dve(dve, n, s, f):
            def multiply(c, b=0):
                for tt in range(TT):
                    dve.wait_ge(silu_ready, c * TT + (f * NCH * TT + tt + 1))
                    m = nc.vector.scalar_tensor_tensor(out=prod[:, tt, :], in0=ps[:, b + tt, HC:2 * HC], scalar=rstd[:, tt:tt + 1],
                                                       in1=silu_g[:, tt, :], op0=ALU.mult, op1=ALU.mult)
                m.then_inc(prod_ready, 1)

            def low(c, b=2, to=prod_l, high=prod_h):
                dve.wait_ge(prod_high, c + (f * NCH + 1))
                nc.vector.tensor_tensor(to[:, :, :], bank(b).rearrange("p (k t) -> p k t", k=2),
                                        high[:, :, :].bitcast(f32), ALU.subtract).then_inc(prod_low, 1)

            def split(c, j):
                r = (n + j) % RING
                dve.wait_ge(high_ready, c * 3 + (n + j + 1))
                nc.vector.tensor_tensor(wl[:, r, :], raw[:, r, :], wh[:, r, :].bitcast(f32), ALU.subtract)\
                  .then_inc(split_ready, 1)

            norm_dve(dve, s, FFN_GAIN[f], FFN_BANKS)
            dve_ahead.through(dve, n + 3)
            multiply(0)
            dve_ahead.through(dve, n + 4)
            low(0, 0)
            dve_ahead.through(dve, n + 5)
            multiply(1, 2)
            dve_ahead.through(dve, n + 6)
            low(1)
            with dve.Fori(2, NCH - 1) as c:
                split(c, 1)
                split(c, 2)
                multiply(c)
                split(c, 3)
                low(c)
            dve_ahead.n += 3 * (NCH - 3)
            dve_ahead.through(dve, n + FFN_SLOTS - 1)
            multiply(NCH - 1)
            dve_ahead.through(dve, n + FFN_SLOTS)
            low(NCH - 1, to=last_l, high=last_h)
            add_result(dve, s, 0.5 if f < 4 else 1.0)

        FFN_BANKS = (2, 3, 4, 6)
        last_h, last_l = hth[:, KT - 2:KT, :], htl[:, KT - 2:KT, :]
        FFN_GAIN = [GAINS, GAINS + 2 * KT, GAINS + 5 * KT, GAINS + 7 * KT, FFN2]
        fs = {s: PLAN[:s].count("ffn") for s in range(len(PLAN))}

        ple_gate = Steps(sem("ple_act"), ["sigmoid0", "sigmoid1", "squares0", "squares1"], 2)
        ple_vector = Steps(sem("ple_dve"), ["product0", "product1"], 2)
        ple_rstd = Steps(sem("ple_pool"), ["rstd0", "rstd1"], 2)
        p_loaded = sem("p_loaded")
        tile_ready = sem("tile_ready")
        p_rows = arena[:, 0:TT * HC].rearrange("p (t n) -> p t n", t=TT)
        ple_sq = arena[:, 1024:1024 + TT * D].rearrange("p (t n) -> p t n", t=TT)
        gained = arena[:, 5120:5120 + TT * D].rearrange("p (t n) -> p t n", t=TT)
        ple_ms = arena[:, 4096:4096 + TT]
        ple_rs = arena[:, 4100:4100 + TT]
        ples = {s: PLAN[:s].count("ple") for s in range(len(PLAN))}

        def ple_load(sp, s, l):
            n = base[s]
            v = io["ple_w_proj"][l].rearrange("(k p) n -> p k n", p=P)
            load_slot(sp, n, [(raw_view(n, 2, D)[:, j:j + 1, :], v[:, j:j + 1, :]) for j in range(2)])
            load_square(sp, n + 1, io["ple_w_gate"][l])

        PLE_BANKS = (4, 6, 5, 7)

        def ple_pe(pe, s, l):
            n = base[s]
            pe.wait_ge(p_loaded, 16 * (l + 1))
            turn_bank(0, 2, p_rows, 0)
            for b in range(4):
                turn_x(pe, s, b, PLE_BANKS[b])
            turned_by(pe, s, 0, 1)
            take_slot(pe, n)
            for kk in range(2):
                for tt in range(TT):
                    for half in range(2):
                        c = kk * D + half * 512
                        m = product(bank(2 * tt + half), prod_h[:, kk, tt * P:(tt + 1) * P], prod_l[:, kk, tt * P:(tt + 1) * P],
                                    wh[:, n % RING, c:c + 512], wl[:, n % RING, c:c + 512], kk == 0, kk == 1)
            m.then_inc(weights_used, 1)
            turned_by(pe, s, 1, 4)
            project_out(pe, s, 1, n + 1, by_halves=False)

        def ple_act(act, s, l):
            n = base[s]
            act.wait_ge(x_ready, 4 * (s - 1))
            act.dma_start(gain_row[:, :], io["norm_gains"][l, 4:5, :].partition_broadcast(P)).then_inc(gain_loaded, 16)
            act.dma_start(p_rows, io["p"][l, 0].rearrange("(t p) n -> p t n", p=P)).then_inc(p_loaded, 16)
            turn_act(act, s, 0, 2, dst=prod_h)
            turn_act(act, s, 1, KT, GAINS + (5 * l + 3) * KT, PLE_BANKS)
            norm_act(act, s, None)
            rms(act, s)
            act_ahead.before(act, n + 4)
            for tt in range(TT):
                if tt == 0:
                    act.wait_ge(tile_ready, l + 1)
                else:
                    act.wait_ge(weights_used, n + 5)
                ple_gate.done(nc.scalar.activation(xn[:, tt, :], ps[:, 4 + 2 * tt:6 + 2 * tt, :], ACT.Sigmoid,
                                                   scale=rstd[:, tt:tt + 1]), f"sigmoid{tt}", l)
            for tt in range(TT):
                act.wait_ge(ple_vector.sem, ple_vector.after(f"product{tt}", l))
                ple_gate.done(nc.scalar.activation(ple_sq[:, tt, :], xn[:, tt, :], ACT.Square, scale=1 / math.sqrt(D),
                                                   accum_out=ple_ms[:, tt:tt + 1]), f"squares{tt}", l)

        def ple_pool(pool, s, l):
            pool.wait_ge(gain_loaded, 16 * (l + 1))
            for tt in range(TT):
                pool.wait_ge(ple_gate.sem, ple_gate.after(f"squares{tt}", l))
                pool_link(pool, nc.gpsimd.tensor_scalar(ple_ms[:, tt:tt + 1], ple_ms[:, tt:tt + 1], EPS, None, ALU.add))
                ple_rstd.done(nc.gpsimd.tensor_tensor(ple_rs[:, tt:tt + 1], ple_ms[:, tt:tt + 1], minus_half[:, 0:1],
                                                      ALU.pow), f"rstd{tt}", l)

        def ple_dve(dve, s, l):
            n = base[s]
            turn_dve(dve, s, 0, 2, dst=prod_l, dst_h=prod_h)
            turn_dve(dve, s, 1, KT, GAINS + (5 * l + 3) * KT, PLE_BANKS)
            dve_ahead.before(dve, n + 4)
            dve.wait_ge(gain_loaded, 16 * (l + 1))
            for tt in range(TT):
                dve.wait_ge(ple_gate.sem, ple_gate.after(f"sigmoid{tt}", l))
                ple_vector.done(nc.vector.tensor_tensor(xn[:, tt, :], xn[:, tt, :], ps[:, 2 * tt:2 * tt + 2, :], ALU.mult),
                                f"product{tt}", l)
                dve.wait_ge(ple_vector.sem, ple_vector.after(f"product{tt}", l))
                nc.vector.tensor_tensor(gained[:, tt, :], xn[:, tt, :], gain_row[:, :], ALU.mult).then_inc(dve_chain, 1)
                dve_link.n += 1
            for tt in range(TT):
                dve.wait_ge(ple_rstd.sem, ple_rstd.after(f"rstd{tt}", l))
                dve.wait_ge(dve_chain, dve_link.n - 1 + tt)
                for o, quarters in (((slice(0, D), 1),) if tt == 0 else ((slice(0, D // 2), 1), (slice(D // 2, D), 2))):
                    nc.vector.scalar_tensor_tensor(out=x[:, tt, o], in0=gained[:, tt, o], scalar=ple_rs[:, tt:tt + 1],
                                                   in1=x[:, tt, o], op0=ALU.mult, op1=ALU.add).then_inc(x_ready, quarters)

        class Arena:
            def __init__(self):
                self.at = 0

            def __call__(self, n, pattern=None, **sizes):
                v = arena[:, self.at:self.at + n]
                self.at += n
                assert self.at <= arena.shape[1], self.at
                return v.rearrange(pattern, **sizes) if pattern else v

        def repeated(v, axis, n):
            v = v.unsqueeze(axis)
            return v.broadcast_to([n if i == axis else d for i, d in enumerate(v.shape)])

        def scaled_rows(dst, b, func, w=512):
            for tt in range(TT):
                m = nc.scalar.activation(dst[:, tt, :], bank(b + tt, w), func, scale=rstd[:, tt:tt + 1])
            return m

        H, BC, SB = 4, 64, 8
        NC, NB = T // BC, BC // SB
        AH, AD = 8, 64
        ar = Arena()
        e_f = ar(H * T, "p (h t) -> p h t", h=H)
        e_k = ar(H * T, "p (h t) -> p h t", h=H)
        e_b = ar(H * T, "p (h t) -> p h t", h=H)
        e_mid = ar(H * T, "p (h t) -> p h t", h=H)
        e_exp = ar(H * T, "p (h t) -> p h t", h=H)
        e_last = ar(H * T, "p (h t) -> p h t", h=H)
        e_qm = ar(H * T, "p (h t) -> p h t", h=H)
        e_q0 = ar(H * T, "p (h t) -> p h t", h=H)
        e_kd = [ar(NC * NB * BC, "p (c i s) -> p c i s", c=NC, i=NB) for _ in range(2)]
        e_reset = ar(H * T)
        e_v = ar(TT * 512, "p (t n) -> p t n", t=TT)
        e_keys = ar(TT * 512, "p (t n) -> p t n", t=TT)
        e_mask = silu_g[:, :, :].rearrange("p a b -> p (a b)").rearrange("p (n t) -> p n t", t=BC)
        e_scores = prod[:, :, :].rearrange("p a b -> p (a b)").rearrange("p (n t) -> p n t", t=BC)
        e_state = ar(3 * 512, "p (c h e) -> p c h e", c=3, h=H)
        e_u = ar(TT * 512, "p (t n) -> p t n", t=TT)
        e_av = ar(TT * 512, "p (t n) -> p t n", t=TT)
        e_g = ar(TT * 512, "p (t n) -> p t n", t=TT)
        e_ss = ar(16)
        e_decay = ar(16)
        e_rs = ar(16)
        e_os = ar(8)
        e_or = ar(8)
        e_w = e_keys.rearrange("p h t -> p (h t)").rearrange("p (h s) -> p h s", h=AH)
        e_wt = e_f.rearrange("p h t -> p (h t)").rearrange("p (h s) -> p h s", h=AH)
        e_sq = e_mid.rearrange("p h t -> p (h t)")
        e_o = e_reset.rearrange("p (t n) -> p t n", t=TT)
        EV_PE = Steps(sem("even_pe"), ["w_turned", "scores0", "scores1", "keys_turned", "scores2", "scores3", "deltas", "mixed", "o"])
        EV_ACT = Steps(sem("even_act"), ["sigmoid", "log", "exp_mid", "exp_b", "exp_last", "exp0", "v", "w_cols", "exp1", "av",
                                         "exp2", "u", "keys", "exp3", "g", "o_copied", "o_squared"])
        EV_DVE = Steps(sem("even_dve"), ["f", "floor", "cum", "diff_mid", "diff_last", "decayed", "queries", "keys0", "keys1",
                                         "v_squares", "v_normed", "keys2", "keys3", "states", "masked", "o_squares"])
        EV_POOL = Steps(sem("even_pool"), ["reset", "w_masked", "diff0", "diff1", "zeros", "v_rstd", "diff2", "diff3", "gate", "o_rstd"])
        w_loaded = sem("gmlp_w_loaded")

        def even_load(sp, s):
            n, w = base[s], io["even_w_in"][0]
            for j, c0 in enumerate((1536, 1024, 2048, 512, 0, 2560)):
                load_columns(sp, n + 2 * j, w, c0, 512)
            load_square(sp, n + 12, io["even_w_out"][0])

        def flat(v):
            return v.rearrange("p h t -> p (h t)")

        middles = flat(e_b).rearrange("p (c i s) -> p c i s", i=NB, s=SB)[:, :, :, SB // 2 - 1]
        lasts = flat(e_b).rearrange("p (c s) -> p c s", s=BC)[:, :, BC - 1]

        def even_pe(pe, s):
            n = base[s]

            def scores(h):
                pe.wait_ge(EV_DVE.sem, EV_DVE.after(f"keys{h}"))
                for c in range(NC):
                    p0 = (c % 2) * BC
                    for i in range(NB):
                        o = (h * TT + c // 2) * BC + i * SB
                        m = nc.tensor.matmul(ps[p0:p0 + BC, 0, o:o + SB], e_kd[h % 2][:, c, i, :],
                                             e_qm[:, h, c * BC + i * SB:c * BC + (i + 1) * SB], start=True, stop=True)
                EV_PE.done(m, f"scores{h}")

            for b in range(4):
                turn_x(pe, s, b, b)
            columns_product(pe, n, [bank(4 + h, T) for h in range(H)], 512, first_of=s)
            rms_row_pe(pe, 0, 0)
            pe.wait_ge(r_steps, 3)
            columns_product(pe, n + 2, [bank(h, T) for h in range(H)], 512)
            pe.wait_ge(EV_DVE.sem, EV_DVE.after("f"))
            rows_product(pe, n + 4, [bank(4), bank(5)])
            pe.wait_ge(EV_POOL.sem, EV_POOL.after("w_masked"))
            pe.wait_ge(EV_DVE.sem, EV_DVE.after("queries"))
            for h in range(AH):
                m = nc.tensor.transpose(ps[:, 2 + h // 4, (h % 4) * P:(h % 4 + 1) * P], e_w[:, h, :], ident[:, :])
            EV_PE.done(m, "w_turned")
            scores(0)
            rows_product(pe, n + 6, [bank(6), bank(7)])
            scores(1)
            pe.wait_ge(EV_ACT.sem, EV_ACT.after("w_cols"))
            for tt in range(TT):
                for h in range(H):
                    m = nc.tensor.transpose(ps[:, 1 + tt, h * P:(h + 1) * P], e_last[:, h, tt * P:(tt + 1) * P], ident[:, :])
            EV_PE.done(m, "keys_turned")
            pe.wait_ge(EV_ACT.sem, EV_ACT.after("v"))
            rows_product(pe, n + 8, [bank(4), bank(5)])
            scores(2)
            pe.wait_ge(EV_ACT.sem, EV_ACT.after("av"))
            rows_product(pe, n + 10, [bank(6), bank(7)])
            scores(3)
            pe.wait_ge(EV_ACT.sem, EV_ACT.after("keys"))
            for c, b in ((0, 3), (1, 1), (2, 2)):
                p0 = (c % 2) * BC
                for h in range(H):
                    m = nc.tensor.matmul(ps[:, b, h * P:(h + 1) * P], e_keys[p0:p0 + BC, c // 2, h * P:(h + 1) * P],
                                         e_v[p0:p0 + BC, c // 2, h * P:(h + 1) * P], start=True, stop=True)
            EV_PE.done(m, "deltas")
            pe.wait_ge(EV_DVE.sem, EV_DVE.after("v_normed"))
            pe.wait_ge(EV_ACT.sem, EV_ACT.after("u"))
            for h in range(AH):
                m = nc.tensor.matmul(ps[:, 4 + h // 4, (h % 4) * P:(h % 4 + 1) * P].rearrange("p (t d) -> p t d", t=TT),
                                     e_wt[:, h, :], e_av[:, :, h * AD:(h + 1) * AD], start=True, stop=True)
            EV_PE.done(m, "mixed")
            pe.wait_ge(EV_DVE.sem, EV_DVE.after("masked"))
            pe.wait_ge(EV_ACT.sem, EV_ACT.after("g"))
            for c in range(NC):
                p0, tt = (c % 2) * BC, c // 2
                for h in range(H):
                    o = ps[p0:p0 + BC, 6 + tt, h * P:(h + 1) * P]
                    m = nc.tensor.matmul(o, e_scores[p0:p0 + BC, h * TT + tt, :], e_v[p0:p0 + BC, tt, h * P:(h + 1) * P],
                                         start=True, stop=c == 0)
                    if c:
                        m = nc.tensor.matmul(o, e_q0[:, h, c * BC:(c + 1) * BC], e_state[:, c - 1, h, :], start=False, stop=True)
            EV_PE.done(m, "o")
            pe.wait_ge(rows_ready, TT * call_base[s][1] + 1)
            turn_bank(0, KT, xn, 0)
            turn_bank(1, KT, xn, 1)
            pe.wait_ge(EV_ACT.sem, EV_ACT.after("o_copied"))

            def turn_rest():
                pe.wait_ge(rows_ready, TT * (call_base[s][1] + 1))
                turn_bank(2, KT, xn, 2)
                turn_bank(3, KT, xn, 3)

            project_out(pe, s, 1, n + 12, rest=turn_rest)

        def even_act(act, s):
            n = base[s]
            act.wait_ge(x_ready, 4 * (s - 1))
            act.dma_start(e_w, io["gmlp_w_s"][0].rearrange("h t s -> t h s")).then_inc(w_loaded, 16)
            norm_act(act, s, GAINS + KT)
            act_ahead.before(act, n + 1)
            act.wait_ge(EV_DVE.sem, EV_DVE.after("f"))
            EV_ACT.done(nc.scalar.activation(e_f, e_f, ACT.Sigmoid), "sigmoid")
            act_ahead.before(act, n + 2)
            act.wait_ge(EV_DVE.sem, EV_DVE.after("floor"))
            EV_ACT.done(nc.scalar.activation(e_last, e_f, ACT.Ln), "log")
            act.wait_ge(EV_DVE.sem, EV_DVE.after("diff_mid"))
            EV_ACT.done(nc.scalar.activation(e_mid, e_mid, ACT.Exp), "exp_mid")
            EV_ACT.done(nc.scalar.activation(e_exp, e_b, ACT.Exp), "exp_b")
            act.wait_ge(EV_DVE.sem, EV_DVE.after("diff_last"))
            EV_ACT.done(nc.scalar.activation(e_last, e_last, ACT.Exp), "exp_last")

            def exp(h):
                act.wait_ge(EV_POOL.sem, EV_POOL.after(f"diff{h}"))
                EV_ACT.done(nc.scalar.activation(e_kd[h % 2], e_kd[h % 2], ACT.Exp), f"exp{h}")

            act_ahead.before(act, n + 3)
            exp(0)
            act_ahead.before(act, n + 5)
            rms(act, s)
            act.wait_ge(weights_used, n + 6)
            EV_ACT.done(scaled_rows(e_v, 4, ACT.Copy), "v")
            act.wait_ge(EV_PE.sem, EV_PE.after("w_turned"))
            EV_ACT.done(nc.scalar.activation(e_wt, ps[:, 2:4, :], ACT.Copy), "w_cols")
            exp(1)
            act_ahead.before(act, n + 7)
            act.wait_ge(weights_used, n + 8)
            EV_ACT.done(scaled_rows(e_av, 6, ACT.Gelu_apprx_tanh), "av")
            exp(2)
            act_ahead.before(act, n + 9)
            act.wait_ge(weights_used, n + 10)
            EV_ACT.done(scaled_rows(e_u, 4, ACT.Gelu_apprx_tanh), "u")
            act.wait_ge(EV_PE.sem, EV_PE.after("keys_turned"))
            EV_ACT.done(nc.scalar.activation(e_keys, ps[:, 1:3, :], ACT.Copy), "keys")
            exp(3)
            act_ahead.before(act, n + 11)
            act.wait_ge(weights_used, n + 12)
            EV_ACT.done(scaled_rows(e_g, 6, ACT.Silu), "g")
            act.wait_ge(EV_PE.sem, EV_PE.after("o"))
            EV_ACT.done(nc.scalar.activation(e_o, ps[:, 6:8, :], ACT.Copy), "o_copied")
            act.wait_ge(EV_DVE.sem, EV_DVE.after("v_squares"))
            act.wait_ge(EV_ACT.sem, EV_ACT.after("o_copied"))
            EV_ACT.done(nc.scalar.activation(e_sq, e_o.rearrange("p t n -> p (t n)"), ACT.Square), "o_squared")
            turn_act(act, s, 1, KT, part=(0, 2))
            act_ahead.before(act, n + 12)
            turn_act(act, s, 1, KT, part=(2, 4))
            act_ahead.before(act, n + 15)

        def even_pool(pool, s):
            pool_link(pool, nc.gpsimd.memset(e_reset, 1.0))
            EV_POOL.done(nc.gpsimd.memset(e_reset.rearrange("p (c s) -> p c s", s=BC)[:, :, 0:1], 0.0), "reset")
            pool.wait_ge(w_loaded, 16)
            EV_POOL.done(nc.gpsimd.affine_select(out=e_w, in_=e_w, compare_op=ALU.is_ge, fill=0.0, base=0,
                                                 pattern=[[0, AH], [-1, P]], channel_multiplier=1), "w_masked")

            def diff(h):
                if h == 0:
                    pool.wait_ge(EV_DVE.sem, EV_DVE.after("cum"))
                if h >= 2:
                    pool.wait_ge(EV_PE.sem, EV_PE.after(f"scores{h - 2}"))
                mid = repeated(middles[:, h * NC:(h + 1) * NC, :], 3, BC)
                b = repeated(e_b[:, h, :].rearrange("p (c s) -> p c s", c=NC), 2, NB)
                EV_POOL.done(nc.gpsimd.tensor_tensor(e_kd[h % 2], mid, b, ALU.subtract), f"diff{h}")

            diff(0)
            diff(1)
            pool_link(pool, nc.gpsimd.memset(e_mask, 1.0))
            for p0 in (0, BC):
                v = e_mask[p0:p0 + BC, :, :]
                pool_link(pool, nc.gpsimd.affine_select(out=v, in_=v, compare_op=ALU.is_ge, fill=0.0, base=0,
                                                        pattern=[[0, H * TT], [1, BC]], channel_multiplier=-1))
            EV_POOL.done(nc.gpsimd.memset(e_scores, 0.0), "zeros")
            pool.wait_ge(EV_DVE.sem, EV_DVE.after("v_squares"))
            pool_link(pool, nc.gpsimd.tensor_scalar(e_ss, e_ss, 1.0 / AD, EPS, ALU.mult, ALU.add))
            EV_POOL.done(nc.gpsimd.tensor_tensor(e_rs, e_ss, minus_half[:, 0:16], ALU.pow), "v_rstd")
            diff(2)
            diff(3)
            pool.wait_ge(EV_ACT.sem, EV_ACT.after("g"))
            g8 = e_g.rearrange("p t n -> p (t n)").rearrange("p (n d) -> p n d", d=P)
            EV_POOL.done(nc.gpsimd.tensor_tensor(g8, g8, repeated(onorm[:, :], 1, 8), ALU.mult), "gate")
            pool.wait_ge(EV_DVE.sem, EV_DVE.after("o_squares"))
            pool_link(pool, nc.gpsimd.tensor_scalar(e_os, e_os, 1.0 / P, EPS, ALU.mult, ALU.add))
            EV_POOL.done(nc.gpsimd.tensor_tensor(e_or, e_os, minus_half[:, 0:8], ALU.pow), "o_rstd")

        def even_dve(dve, s):
            n = base[s]
            norm_dve(dve, s, GAINS + KT)
            rms_diagonals(dve, s, 0)
            dve_ahead.before(dve, n + 1)
            rms_row(dve, 0, 0)
            dve.wait_ge(weights_used, n + 2)
            EV_DVE.done(nc.vector.tensor_tensor(e_f, ps[:, 4:8, 0:T], repeated(r_row[:, :], 1, H), ALU.mult), "f")
            dve.wait_ge(EV_ACT.sem, EV_ACT.after("sigmoid"))
            for h in range(H):
                m = nc.vector.tensor_scalar(e_f[:, h, :], e_f[:, h, :], lb[:, 1, h:h + 1], lb[:, 0, h:h + 1], ALU.mult, ALU.add)
            dve_link(dve, m)
            nc.vector.tensor_scalar(e_k, e_f, -1.0, 1.0, ALU.mult, ALU.add)
            EV_DVE.done(nc.vector.tensor_scalar(e_f, e_f, 1e-6, None, ALU.max), "floor")
            dve_ahead.before(dve, n + 2)
            dve.wait_ge(EV_ACT.sem, EV_ACT.after("log"))
            dve.wait_ge(EV_POOL.sem, EV_POOL.after("reset"))
            EV_DVE.done(nc.vector.tensor_tensor_scan(flat(e_b), e_reset, flat(e_last), 0.0, ALU.mult, ALU.add), "cum")
            dve.wait_ge(EV_DVE.sem, EV_DVE.after("cum"))
            b8 = flat(e_b).rearrange("p (c s) -> p c s", s=SB)
            mid = repeated(b8[:, :, SB // 2 - 1], 2, SB)
            EV_DVE.done(nc.vector.tensor_tensor(flat(e_mid).rearrange("p (c s) -> p c s", s=SB), b8, mid, ALU.subtract), "diff_mid")
            b64 = flat(e_b).rearrange("p (c s) -> p c s", s=BC)
            EV_DVE.done(nc.vector.tensor_tensor(flat(e_last).rearrange("p (c s) -> p c s", s=BC), repeated(lasts, 2, BC), b64,
                                                ALU.subtract), "diff_last")
            dve.wait_ge(EV_ACT.sem, EV_ACT.after("exp_last"))
            EV_DVE.done(nc.vector.tensor_tensor(e_last, e_last, e_k, ALU.mult), "decayed")
            nc.vector.tensor_copy(e_decay, flat(e_exp).rearrange("p (c s) -> p c s", s=BC)[:, :, BC - 1])
            nc.vector.tensor_tensor(e_q0, e_exp, repeated(r_row[:, :], 1, H), ALU.mult)
            dve_link(dve, nc.vector.tensor_tensor(e_mid, e_mid, repeated(r_row[:, :], 1, H), ALU.mult))
            dve_ahead.before(dve, n + 3)
            dve.wait_ge(weights_used, n + 4)
            nc.vector.tensor_tensor(e_q0, e_q0, ps[:, 0:4, 0:T], ALU.mult)
            EV_DVE.done(nc.vector.tensor_tensor(e_qm, e_mid, ps[:, 0:4, 0:T], ALU.mult), "queries")

            def keys(h):
                dve.wait_ge(EV_ACT.sem, EV_ACT.after(f"exp{h}"))
                k = repeated(e_k[:, h, :].rearrange("p (c s) -> p c s", c=NC), 2, NB)
                EV_DVE.done(nc.vector.tensor_tensor(e_kd[h % 2], e_kd[h % 2], k, ALU.mult), f"keys{h}")

            keys(0)
            dve_ahead.before(dve, n + 5)
            keys(1)
            dve_ahead.before(dve, n + 7)
            dve.wait_ge(EV_ACT.sem, EV_ACT.after("av"))
            dve_link(dve, nc.vector.tensor_tensor(e_sq, e_av.rearrange("p t n -> p (t n)"), e_av.rearrange("p t n -> p (t n)"), ALU.mult))
            EV_DVE.done(nc.vector.tensor_reduce(e_ss, e_sq.rearrange("p (n d) -> p n d", d=AD), AX.X, ALU.add), "v_squares")
            dve.wait_ge(EV_POOL.sem, EV_POOL.after("v_rstd"))
            av = e_av.rearrange("p t n -> p (t n)").rearrange("p (n d) -> p n d", d=AD)
            dve_link(dve, nc.vector.tensor_tensor(av, av, repeated(e_rs, 2, AD), ALU.mult))
            EV_DVE.done(nc.vector.tensor_tensor(e_av, e_av, repeated(vnorm[:, :], 1, TT), ALU.mult), "v_normed")
            keys(2)
            dve_ahead.before(dve, n + 9)
            keys(3)
            dve_ahead.before(dve, n + 11)
            dve.wait_ge(EV_PE.sem, EV_PE.after("deltas"))
            dve_link(dve, nc.vector.tensor_copy(e_state[:, 0, :, :], bank(3).rearrange("p (h e) -> p h e", h=H)))
            for c in (1, 2):
                for h in range(H):
                    m = nc.vector.scalar_tensor_tensor(out=e_state[:, c, h, :], in0=e_state[:, c - 1, h, :],
                                                       scalar=e_decay[:, h * NC + c:h * NC + c + 1],
                                                       in1=ps[:, c, h * P:(h + 1) * P], op0=ALU.mult, op1=ALU.add)
                if c == 1:
                    dve_link(dve, m)
            EV_DVE.done(m, "states")
            dve.wait_ge(EV_POOL.sem, EV_POOL.after("zeros"))
            EV_DVE.done(nc.vector.copy_predicated(e_scores, e_mask.bitcast(i32), bank(0).rearrange("p (n t) -> p n t", t=BC)), "masked")
            dve.wait_ge(EV_PE.sem, EV_PE.after("mixed"))
            for h in range(AH):
                o = slice(h * AD, (h + 1) * AD)
                m = nc.vector.scalar_tensor_tensor(out=xn[:, :, o], in0=ps[:, 4 + h // 4, (h % 4) * P:(h % 4 + 1) * P].rearrange("p (t d) -> p t d", t=TT),
                                               scalar=cols[:, BS + h:BS + h + 1], in1=e_u[:, :, o], op0=ALU.add, op1=ALU.mult)
            m.then_inc(rows_ready, 1)
            turn_dve(dve, s, 1, KT, part=(0, 2))
            dve_ahead.before(dve, n + 12)
            dve.wait_ge(EV_ACT.sem, EV_ACT.after("o_copied"))
            dve.wait_ge(EV_POOL.sem, EV_POOL.after("gate"))
            dve_link(dve, nc.vector.tensor_tensor(e_o, e_o, e_g, ALU.mult))
            dve.wait_ge(EV_ACT.sem, EV_ACT.after("o_squared"))
            EV_DVE.done(nc.vector.tensor_reduce(e_os, e_sq.rearrange("p (n d) -> p n d", d=P), AX.X, ALU.add), "o_squares")
            dve.wait_ge(EV_POOL.sem, EV_POOL.after("o_rstd"))
            o4 = e_o.rearrange("p t (h d) -> p t h d", h=H)
            rs4 = repeated(e_or.rearrange("p (t h) -> p t h", t=TT), 3, P)
            nc.vector.tensor_tensor(xn[:, :, 512:1024].rearrange("p t (h d) -> p t h d", h=H), o4, rs4, ALU.mult)\
              .then_inc(rows_ready, 1)
            turn_dve(dve, s, 1, KT, part=(2, 4))
            add_result(dve, s, 1.0)

        class Attention:

            def __init__(self, name, heads, dv, parts, value, scale, o_bank, rows, probs, probs_t, small):
                self.heads, self.dv, self.parts, self.value, self.scale = heads, dv, parts, value, scale
                self.o_bank, self.rows, self.probs, self.probs_t, self.small = o_bank, rows, probs, probs_t, small
                names = ["scores0", "scores1"]
                for h in range(heads):
                    names += [f"turned{h}"] + [f"scores{h + 2}"] * (h + 2 < heads) + [f"output{h}"]
                self.pe_done = Steps(sem(name + "_attn_pe"), names)
                names = ["probs0"]
                for h in range(heads):
                    names += [f"columns{h}"] + [f"probs{h + 1}"] * (h + 1 < heads)
                self.act_done = Steps(sem(name + "_attn_act"), names)
                names = ["max0", "max1"]
                for h in range(heads):
                    names += [f"max{h + 2}"] * (h + 2 < heads) + [f"rows{h}"]
                self.dve_done = Steps(sem(name + "_attn_dve"), names)

            def scores(self, h):
                for qt in range(TT):
                    c0, w = qt * P, (qt + 1) * P
                    parts = self.parts(h)
                    for j, (q, k) in enumerate(parts):
                        m = nc.tensor.matmul(ps[:, 4 + h % 2, c0:c0 + w], q[:, qt * P:(qt + 1) * P], k[:, 0:w],
                                             start=j == 0, stop=j == len(parts) - 1)
                self.pe_done.done(m, f"scores{h}")

            def pe(self, pe, outputs_free=None):
                for h in range(self.heads):
                    pe.wait_ge(self.act_done.sem, self.act_done.after(f"probs{h}"))
                    for j in range(3):
                        m = nc.tensor.transpose(ps[:, 6 + h % 2, j * P:(j + 1) * P], self.probs[h % 2][:, j * P:(j + 1) * P],
                                                ident[:, :])
                    self.pe_done.done(m, f"turned{h}")
                    if h + 2 < self.heads:
                        self.scores(h + 2)
                    if h == 0 and outputs_free is not None:
                        outputs_free()
                    pe.wait_ge(self.act_done.sem, self.act_done.after(f"columns{h}"))
                    if h >= 2:
                        pe.wait_ge(self.dve_done.sem, self.dve_done.after(f"rows{h - 2}"))
                    o = [ps[:, self.o_bank + h % 2, qt * self.dv:(qt + 1) * self.dv] for qt in range(TT)]
                    pt = self.probs_t[h % 2]
                    nc.tensor.matmul(o[0], pt[:, 0:P], self.value(h, 0), start=True, stop=True)
                    nc.tensor.matmul(o[1], pt[:, P:2 * P], self.value(h, 0), start=True, stop=False)
                    m = nc.tensor.matmul(o[1], pt[:, 2 * P:3 * P], self.value(h, 1), start=False, stop=True)
                    self.pe_done.done(m, f"output{h}")

            def act(self, act):
                def probs(h):
                    act.wait_ge(self.dve_done.sem, self.dve_done.after(f"max{h}"))
                    pr, sm = self.probs[h % 2], self.small[h % 4]
                    nc.scalar.activation(pr[:, 0:P], pr[:, 0:P], ACT.Exp, bias=sm[:, 0:1], accum_out=sm[:, 2:3])
                    m = nc.scalar.activation(pr[:, P:3 * P], pr[:, P:3 * P], ACT.Exp, bias=sm[:, 1:2], accum_out=sm[:, 3:4])
                    self.act_done.done(m, f"probs{h}")

                probs(0)
                for h in range(self.heads):
                    act.wait_ge(self.pe_done.sem, self.pe_done.after(f"turned{h}"))
                    self.act_done.done(nc.scalar.activation(self.probs_t[h % 2], bank(6 + h % 2, 3 * P), ACT.Copy), f"columns{h}")
                    if h + 1 < self.heads:
                        probs(h + 1)

            def maxima(self, dve, h):
                dve.wait_ge(self.pe_done.sem, self.pe_done.after(f"scores{h}"))
                pr, sm = self.probs[h % 2], self.small[h % 4]
                nc.vector.scalar_tensor_tensor(out=pr[:, 0:P], in0=ps[:, 4 + h % 2, 0:P], scalar=self.scale(h, 0),
                                               in1=causal[:, 0:P], op0=ALU.mult, op1=ALU.add)
                dve_link(dve, nc.vector.scalar_tensor_tensor(out=pr[:, P:3 * P], in0=ps[:, 4 + h % 2, P:3 * P],
                                                             scalar=self.scale(h, 1), in1=causal[:, P:3 * P],
                                                             op0=ALU.mult, op1=ALU.add))
                nc.vector.tensor_reduce(sm[:, 0:1], pr[:, 0:P], AX.X, ALU.max, negate=True)
                self.dve_done.done(nc.vector.tensor_reduce(sm[:, 1:2], pr[:, P:3 * P], AX.X, ALU.max, negate=True), f"max{h}")

            def dve(self, dve, between=()):
                for h in range(self.heads):
                    if h + 2 < self.heads:
                        self.maxima(dve, h + 2)
                    dve.wait_ge(self.pe_done.sem, self.pe_done.after(f"output{h}"))
                    sm = self.small[h % 4]
                    dve_link(dve, nc.vector.reciprocal(sm[:, 4:6], sm[:, 2:4]))
                    for qt in range(TT):
                        m = nc.vector.tensor_scalar(self.rows(h, qt), ps[:, self.o_bank + h % 2, qt * self.dv:(qt + 1) * self.dv],
                                                    sm[:, 4 + qt:5 + qt], None, ALU.mult)
                    self.dve_done.done(m, f"rows{h}")
                    if h < len(between):
                        between[h]()

        causal = silu_g[:, :, :].rearrange("p a b -> p (a b)")[:, 0:3 * P]

        def make_causal(pool):
            pool_link(pool, nc.gpsimd.memset(causal, 0.0))
            nc.gpsimd.affine_select(out=causal[:, 0:P], in_=causal[:, 0:P], compare_op=ALU.is_ge, fill=-1e30, base=0,
                                    pattern=[[-1, P]], channel_multiplier=1)
            return nc.gpsimd.affine_select(out=causal[:, 2 * P:3 * P], in_=causal[:, 2 * P:3 * P], compare_op=ALU.is_ge,
                                           fill=-1e30, base=0, pattern=[[-1, P]], channel_multiplier=1)

        ROW_BANKS = (2, 3, 0, 1)

        MH, NOPE, ROPE, QL, KVL = 8, 128, 64, 384, 256
        QK = NOPE + ROPE
        ar = Arena()
        m_c = ar(TT * (QL + KVL), "p (t n) -> p t n", t=TT)
        m_kr = ar(TT * ROPE, "p (t n) -> p t n", t=TT)
        m_q = ar(TT * MH * QK, "p (t h d) -> p t h d", t=TT, h=MH)
        m_qr = ar(TT * MH * ROPE, "p (t h d) -> p t h d", t=TT, h=MH)
        m_k = ar(TT * MH * NOPE, "p (t h d) -> p t h d", t=TT, h=MH)
        m_krot = ar(TT * MH * ROPE, "p (t h d) -> p t h d", t=TT, h=MH)
        m_v = ar(TT * MH * NOPE, "p (t h d) -> p t h d", t=TT, h=MH)
        m_qt = ar(MH * T, "p (h t) -> p h t", h=MH)
        m_kt = ar(MH * T, "p (h t) -> p h t", h=MH)
        m_ropes = ar(MH * T)
        m_qrt = m_ropes[:, 0:MH // 2 * T].rearrange("p (h t) -> p h t", h=MH // 2)
        m_krt = m_ropes[:, MH // 2 * T:].rearrange("p (h t) -> p h t", h=MH // 2)
        m_pos = ar(TT)
        m_ang = ar(4 * 32, "p (a t f) -> p a t f", a=2, t=TT)
        m_n = ar(4 * 32, "p (a t f) -> p a t f", a=2, t=TT)
        m_cos = ar(4 * ROPE, "p (a t f) -> p a t f", a=2, t=TT)
        m_sin = ar(4 * ROPE, "p (a t f) -> p a t f", a=2, t=TT)
        m_css = ar(4)
        m_crs = ar(4)
        m_ss = ar(2 * TT * MH, "p (a t h) -> p a t h", a=2, t=TT)
        m_rs = ar(2 * TT * MH, "p (a t h) -> p a t h", a=2, t=TT)
        m_krs = ar(TT)
        m_rtmp = ar(2 * TT * ROPE, "p (a t h d) -> p a t h d", a=2, t=TT, h=1)
        m_small = [ar(6) for _ in range(4)]
        m_sq = [m_ropes[:, 0:MH * QK], ar(MH * QK)]
        m_tmp = xn[:, :, :].rearrange("p t n -> p (t n)")
        m_probs = [m_q.rearrange("p t h d -> p (t h d)")[:, j * 384:(j + 1) * 384] for j in range(2)]
        m_probs_t = [m_q.rearrange("p t h d -> p (t h d)")[:, (2 + j) * 384:(3 + j) * 384] for j in range(2)]
        m_ksq = m_tmp.rearrange("p (t h d) -> p t h d", t=TT, h=MH)
        ML_PE = Steps(sem("mla_pe"), ["k_turned", "q_turned", "q_rope_turned", "k_rope_turned"])
        ML_ACT = Steps(sem("mla_act"), ["sin", "c0", "c1", "c_sq", "kv0", "k_sq0", "k_sq1", "q0", "q_sq0", "q1", "q_sq1", "q2", "q_sq2",
                                        "k_cols", "q_cols", "q_rope_cols"])
        ML_DVE = Steps(sem("mla_dve"), ["angles", "k_rotated", "k1", "v1", "k_squares", "k_scaled", "q_rope", "q_squares",
                                        "k_rope_cols"])
        ML_POOL = Steps(sem("mla_pool"), ["causal", "c_rstd", "k_rstd", "k_rope", "q_rstd"])

        mla_attn = Attention(
            "mla", MH, NOPE,
            lambda h: [(m_qt[:, h, :], m_kt[:, h, :]),
                       (m_qrt[64 * (h % 2):64 * (h % 2) + 64, h // 2, :], m_krt[64 * (h % 2):64 * (h % 2) + 64, h // 2, :])],
            lambda h, t: m_v[:, t, h, :], lambda h, t: m_rs[:, 0, t, h:h + 1], 0,
            lambda h, t: xn[:, t, h * NOPE:(h + 1) * NOPE], m_probs, m_probs_t, m_small)

        def mla_load(sp, s):
            n = base[s]
            load_columns(sp, n, io["mla_w_in"][0], 0, 512)
            v = io["mla_w_in"][0].rearrange("(k p) n -> p k n", p=P)
            load_slot(sp, n + 2, [(raw_view(n + 2, 8, 192)[:, 4 * j:4 * j + 4, :], v[:, 4 * j:4 * j + 4, 512:704]) for j in range(2)])
            v = io["mla_w_kv_b"][0].rearrange("(k p) n -> p k n", p=P)
            for c in range(2):
                load_slot(sp, n + 3 + c, [(raw_view(n + 3 + c, 2, D)[:, j:j + 1, :], v[:, j:j + 1, c * D:(c + 1) * D])
                                          for j in range(2)])
            v = io["mla_w_q_b"][0].rearrange("(k p) n -> p k n", p=P)
            for c in range(3):
                load_slot(sp, n + 5 + c, [(raw_view(n + 5 + c, 3, 512)[:, a:b, :], v[:, a:b, c * 512:(c + 1) * 512])
                                          for a, b in ((0, 2), (2, 3))])
            load_square(sp, n + 8, io["mla_w_out"][0])

        Q_BANKS = (4, 6, 0)

        def mla_pe(pe, s):
            n = base[s]
            for b in range(4):
                turn_x(pe, s, b, b)
            rows_product(pe, n, [bank(4), bank(5)], first_of=s)
            take_slot(pe, n + 2)
            for k in range(KT):
                m = by_rows([bank(6, 192), bank(7, 192)], k, n + 2, k, 192, k == 0, k == KT - 1)
            m.then_inc(weights_used, 1)
            pe.wait_ge(ML_ACT.sem, ML_ACT.after("c0"))
            turn_bank(0, 5, m_c, 0)
            turn_bank(1, 5, m_c, 1)
            pe.wait_ge(ML_ACT.sem, ML_ACT.after("c1"))
            turn_bank(2, 5, m_c, 2)
            turned_by(pe, s, 1, 3)
            for c in range(2):
                take_slot(pe, n + 3 + c)
                b = 4 - 4 * c
                for k in range(2):
                    for half in range(2):
                        m = by_rows([bank(b + half), bank(b + 2 + half)], 3 + k, n + 3 + c, k, D, k == 0, k == 1,
                                    off=half * 512, cols_n=512)
                m.then_inc(weights_used, 1)
            for c in range(3):
                if c == 0:
                    pe.wait_ge(ML_ACT.sem, ML_ACT.after("kv0"))
                if c == 2:
                    pe.wait_ge(ML_DVE.sem, ML_DVE.after("v1"))
                take_slot(pe, n + 5 + c)
                for k in range(3):
                    m = by_rows([bank(Q_BANKS[c]), bank(Q_BANKS[c] + 1)], k, n + 5 + c, k, 512, k == 0, k == 2)
                m.then_inc(weights_used, 1)

            def turn(src, first_bank):
                for h in range(MH):
                    for tt in range(TT):
                        at = (h % 2) * T + tt * P
                        m = nc.tensor.transpose(ps[:, first_bank + h // 2, at:at + P], src[:, tt, h, 0:NOPE], ident[:, :])
                return m

            def turn_rope(src, first_bank):
                for h in range(MH // 2):
                    for tt in range(TT):
                        at = (h % 2) * T + tt * P
                        m = nc.tensor.transpose(ps[:, first_bank + h // 2, at:at + P],
                                                src[:, tt, 2 * h:2 * h + 2, :].rearrange("p h d -> p (h d)"), ident[:, :])
                return m

            pe.wait_ge(ML_ACT.sem, ML_ACT.after("q1"))
            pe.wait_ge(ML_DVE.sem, ML_DVE.after("k_scaled"))
            ML_PE.done(turn(m_k, 4), "k_turned")
            pe.wait_ge(ML_ACT.sem, ML_ACT.after("q2"))
            ML_PE.done(turn(m_q, 0), "q_turned")
            pe.wait_ge(ML_ACT.sem, ML_ACT.after("k_cols"))
            pe.wait_ge(ML_DVE.sem, ML_DVE.after("q_rope"))
            ML_PE.done(turn_rope(m_qr, 4), "q_rope_turned")
            pe.wait_ge(ML_POOL.sem, ML_POOL.after("k_rope"))
            ML_PE.done(turn_rope(m_krot, 6), "k_rope_turned")
            pe.wait_ge(ML_ACT.sem, ML_ACT.after("q_rope_cols"))
            pe.wait_ge(ML_DVE.sem, ML_DVE.after("k_rope_cols"))
            mla_attn.scores(0)
            mla_attn.scores(1)
            mla_attn.pe(pe)
            pe.wait_ge(mla_attn.dve_done.sem, mla_attn.dve_done.after(f"rows{MH // 2 - 1}"))
            turn_bank(0, KT, xn, ROW_BANKS[0])
            turn_bank(1, KT, xn, ROW_BANKS[1])

            def turn_rest():
                pe.wait_ge(mla_attn.dve_done.sem, mla_attn.dve_done.after(f"rows{MH - 1}"))
                turn_bank(2, KT, xn, ROW_BANKS[2])
                turn_bank(3, KT, xn, ROW_BANKS[3])

            project_out(pe, s, 2, n + 8, rest=turn_rest)

        def mla_act(act, s):
            n = base[s]
            norm_act(act, s, GAINS + (5 + 1) * KT)
            rms(act, s)
            act.wait_ge(ML_DVE.sem, ML_DVE.after("angles"))
            ML_ACT.done(nc.scalar.activation(m_ang, m_ang, ACT.Sin), "sin")
            act_ahead.before(act, n + 1)
            act.wait_ge(weights_used, n + 2)
            ML_ACT.done(scaled_rows(m_c[:, :, 0:512], 4, ACT.Copy), "c0")
            act_ahead.before(act, n + 2)
            act.wait_ge(weights_used, n + 3)
            scaled_rows(m_c[:, :, 512:640], 6, ACT.Copy, 128)
            for tt in range(TT):
                m = nc.scalar.activation(m_kr[:, tt, :], ps[:, 6 + tt, 128:192], ACT.Copy, scale=rstd[:, tt:tt + 1])
            ML_ACT.done(m, "c1")
            act.wait_ge(ML_ACT.sem, ML_ACT.after("c1"))
            turn_act(act, s, 1, 5, QA)
            for j, (a, b) in enumerate(((0, QL), (QL, QL + KVL))):
                for tt in range(TT):
                    m = nc.scalar.activation(m_sq[j][:, tt * 384:tt * 384 + b - a], m_c[:, tt, a:b], ACT.Square,
                                             scale=1 / math.sqrt(b - a), accum_out=m_css[:, TT * j + tt:TT * j + tt + 1])
            ML_ACT.done(m, "c_sq")
            act.wait_ge(ML_POOL.sem, ML_POOL.after("c_rstd"))
            act_ahead.before(act, n + 3)
            act.wait_ge(weights_used, n + 4)
            kv = ps[:, 4:8, :].rearrange("p b n -> p (b n)").rearrange("p (t h d) -> p t h d", t=TT, h=4)
            for dst, part in ((m_k, slice(0, NOPE)), (m_v, slice(NOPE, 2 * NOPE))):
                for tt in range(TT):
                    m = nc.scalar.activation(dst[:, tt, 0:4, :], kv[:, tt, :, part], ACT.Copy, scale=m_crs[:, TT + tt:TT + tt + 1])
            ML_ACT.done(m, "kv0")
            act.wait_ge(ML_ACT.sem, ML_ACT.after("kv0"))
            ML_ACT.done(nc.scalar.activation(m_ksq[:, :, 0:4, :], m_k[:, :, 0:4, :], ACT.Square), "k_sq0")
            act_ahead.before(act, n + 4)
            act.wait_ge(ML_DVE.sem, ML_DVE.after("k1"))
            ML_ACT.done(nc.scalar.activation(m_ksq[:, :, 4:8, :], m_k[:, :, 4:8, :], ACT.Square), "k_sq1")
            q = m_q.rearrange("p t h d -> p t (h d)")
            for c in range(3):
                act_ahead.before(act, n + 5 + c)
                act.wait_ge(weights_used, n + 6 + c)
                o = slice(c * 512, (c + 1) * 512)
                for tt in range(TT):
                    m = nc.scalar.activation(q[:, tt, o], bank(Q_BANKS[c] + tt), ACT.Copy, scale=m_crs[:, tt:tt + 1])
                ML_ACT.done(m, f"q{c}")
                act.wait_ge(ML_ACT.sem, ML_ACT.after(f"q{c}"))
                for tt in range(TT):
                    m = nc.scalar.activation(m_sq[tt][:, o], q[:, tt, o], ACT.Square)
                ML_ACT.done(m, f"q_sq{c}")
            act.wait_ge(ML_PE.sem, ML_PE.after("k_turned"))
            ML_ACT.done(nc.scalar.activation(m_kt, ps[:, 4:8, :], ACT.Copy, scale=cols[:, KN:KN + 1]), "k_cols")
            act.wait_ge(ML_PE.sem, ML_PE.after("q_turned"))
            ML_ACT.done(nc.scalar.activation(m_qt, ps[:, 0:4, :], ACT.Copy, scale=cols[:, QN:QN + 1]), "q_cols")
            act.wait_ge(ML_PE.sem, ML_PE.after("q_rope_turned"))
            act.wait_ge(ML_DVE.sem, ML_DVE.after("q_squares"))
            ML_ACT.done(nc.scalar.activation(m_qrt, ps[:, 4:6, :], ACT.Copy), "q_rope_cols")
            mla_attn.act(act)
            turn_act(act, s, 2, KT, banks=ROW_BANKS, part=(0, 2))
            act_ahead.before(act, n + 8)
            turn_act(act, s, 2, KT, banks=ROW_BANKS, part=(2, 4))
            act_ahead.before(act, n + 11)

        def mla_pool(pool, s):
            ML_POOL.done(make_causal(pool), "causal")
            pool.wait_ge(ML_ACT.sem, ML_ACT.after("c_sq"))
            pool_link(pool, nc.gpsimd.tensor_scalar(m_css, m_css, EPS, None, ALU.add))
            ML_POOL.done(nc.gpsimd.tensor_tensor(m_crs, m_css, minus_half[:, 0:4], ALU.pow), "c_rstd")
            for a, name in ((1, "k"), (0, "q")):
                pool.wait_ge(ML_DVE.sem, ML_DVE.after(name + "_squares"))
                ss, rs = (v[:, a, :, :].rearrange("p t h -> p (t h)") for v in (m_ss, m_rs))
                pool_link(pool, nc.gpsimd.tensor_scalar(ss, ss, 1.0 / QK, EPS, ALU.mult, ALU.add))
                m = nc.gpsimd.tensor_tensor(rs, ss, minus_half[:, :], ALU.pow)
                if name == "q":
                    pool_link(pool, m)
                    m = nc.gpsimd.tensor_scalar(rs, rs, QK ** -0.5, None, ALU.mult)
                ML_POOL.done(m, name + "_rstd")
                if name == "k":
                    pool.wait_ge(ML_POOL.sem, ML_POOL.after("k_rstd"))
                    ML_POOL.done(nc.gpsimd.tensor_tensor(m_krot, repeated(m_rtmp[:, 1, :, 0, :], 2, MH),
                                                         repeated(m_rs[:, 1, :, :], 3, ROPE), ALU.mult), "k_rope")

        def mla_dve(dve, s):
            n = base[s]
            norm_dve(dve, s, GAINS + (5 + 1) * KT)
            dve_link(dve, nc.vector.tensor_copy(m_pos, pos_i[:, :]))
            for a in range(2):
                for tt in range(TT):
                    m = nc.vector.tensor_scalar(m_ang[:, a, tt, :], inv_freq[:, :], m_pos[:, tt:tt + 1], None, ALU.mult)
            dve_link(dve, m)
            for a in range(2):
                m = nc.vector.tensor_scalar(m_n[:, a, :, :], m_ang[:, a, :, :], 1 / (2 * math.pi), 0.25 * a, ALU.mult, ALU.add)
            dve_link(dve, m)
            dve_link(dve, nc.vector.tensor_scalar(m_n, m_n, 1.5 * 2 ** 23, None, ALU.add))
            dve_link(dve, nc.vector.tensor_scalar(m_n, m_n, -1.5 * 2 ** 23, None, ALU.add))
            rest, part = 2 * math.pi, 6.28125
            for _ in range(3):
                dve_link(dve, nc.vector.scalar_tensor_tensor(out=m_ang, in0=m_n, scalar=-part, in1=m_ang, op0=ALU.mult, op1=ALU.add))
                rest -= part
                part = math.ldexp(round(math.ldexp(rest, 20)), -20) if _ == 0 else rest
            dve_link(dve, nc.vector.tensor_scalar(m_ang[:, 1, :, :], m_ang[:, 1, :, :], math.pi / 2, None, ALU.add))
            ML_DVE.done(nc.vector.tensor_scalar(m_ang, m_ang, 3.1415925, -3.1415925, ALU.min, ALU.max), "angles")
            dve.wait_ge(ML_ACT.sem, ML_ACT.after("sin"))
            for a in range(2):
                for half in range(2):
                    f = slice(half * 32, half * 32 + 32)
                    other = slice(32 - half * 32, 64 - half * 32)
                    nc.vector.tensor_tensor(m_cos[:, a, :, f], m_ang[:, 1, :, :], repeated(qk_norm[:, a, f], 1, TT), ALU.mult)
                    m = nc.vector.tensor_tensor(m_sin[:, a, :, f], m_ang[:, 0, :, :], repeated(qk_norm[:, a, other], 1, TT), ALU.mult)
            dve_link(dve, m)
            dve_link(dve, nc.vector.tensor_scalar(m_sin[:, :, :, 0:32], m_sin[:, :, :, 0:32], -1.0, None, ALU.mult))
            dve_ahead.before(dve, n + 1)
            dve_ahead.before(dve, n + 2)
            turn_dve(dve, s, 1, 5, QA)
            dve_ahead.before(dve, n + 3)

            def sum_squares(a, src, h0, h1):
                for tt in range(TT):
                    m = nc.vector.tensor_reduce(m_ss[:, a, tt, h0:h1], src(tt)[:, h0:h1, :], AX.X, ALU.add)
                return m

            def rotate(dst, src, a, tmp):
                c, sn = m_cos[:, a, :, :], m_sin[:, a, :, :]
                nh = src.shape[2]
                nc.vector.tensor_tensor(tmp, src, repeated(c, 2, nh), ALU.mult)
                nc.vector.tensor_tensor(dst[:, :, :, 0:32], src[:, :, :, 32:64], repeated(sn[:, :, 0:32], 2, nh), ALU.mult)
                dve_link(dve, nc.vector.tensor_tensor(dst[:, :, :, 32:64], src[:, :, :, 0:32], repeated(sn[:, :, 32:64], 2, nh), ALU.mult))
                return nc.vector.tensor_tensor(dst, dst, tmp, ALU.add)

            dve_link(dve, nc.vector.tensor_tensor(m_qr[:, :, 0, :], m_kr, m_kr, ALU.mult))
            dve_link(dve, nc.vector.tensor_reduce(m_krs, m_qr[:, :, 0, :], AX.X, ALU.add))
            tmp1, rot = m_rtmp[:, 0], m_rtmp[:, 1]
            ML_DVE.done(rotate(rot, m_kr.unsqueeze(2), 1, tmp1), "k_rotated")
            dve_ahead.before(dve, n + 4)
            k_sq = lambda tt: m_ksq[:, tt, :, :]
            dve.wait_ge(ML_ACT.sem, ML_ACT.after("k_sq0"))
            sum_squares(1, k_sq, 0, 4)
            dve.wait_ge(weights_used, n + 5)
            kv = ps[:, 0:4, :].rearrange("p b n -> p (b n)").rearrange("p (t h d) -> p t h d", t=TT, h=4)
            for dst, part, name in ((m_k, slice(0, NOPE), "k1"), (m_v, slice(NOPE, 2 * NOPE), "v1")):
                for tt in range(TT):
                    m = nc.vector.tensor_scalar(dst[:, tt, 4:8, :], kv[:, tt, :, part], m_crs[:, TT + tt:TT + tt + 1], None, ALU.mult)
                ML_DVE.done(m, name)
            dve.wait_ge(ML_ACT.sem, ML_ACT.after("k_sq1"))
            dve_link(dve, sum_squares(1, k_sq, 4, 8))
            ML_DVE.done(nc.vector.tensor_tensor(m_ss[:, 1, :, :], m_ss[:, 1, :, :], repeated(m_krs, 2, MH), ALU.add), "k_squares")
            dve_ahead.before(dve, n + 5)
            dve.wait_ge(ML_POOL.sem, ML_POOL.after("k_rstd"))
            ML_DVE.done(nc.vector.tensor_tensor(m_k, m_k, repeated(m_rs[:, 1, :, :], 3, NOPE), ALU.mult), "k_scaled")
            dve_ahead.before(dve, n + 6)
            dve.wait_ge(ML_ACT.sem, ML_ACT.after("q2"))
            tmp = m_tmp[:, 0:TT * MH * ROPE].rearrange("p (t h d) -> p t h d", t=TT, h=MH)
            ML_DVE.done(rotate(m_qr, m_q[:, :, :, NOPE:QK], 0, tmp), "q_rope")
            dve.wait_ge(ML_ACT.sem, ML_ACT.after("q_sq2"))
            ML_DVE.done(sum_squares(0, lambda tt: m_sq[tt].rearrange("p (h d) -> p h d", h=MH), 0, MH), "q_squares")
            dve.wait_ge(ML_DVE.sem, ML_DVE.after("q_squares"))
            dve.wait_ge(ML_PE.sem, ML_PE.after("k_rope_turned"))
            ML_DVE.done(nc.vector.tensor_copy(m_krt, ps[:, 6:8, :]), "k_rope_cols")
            dve_ahead.before(dve, n + 7)
            dve.wait_ge(ML_POOL.sem, ML_POOL.after("q_rstd"))
            mla_attn.maxima(dve, 0)
            mla_attn.maxima(dve, 1)
            mla_attn.dve(dve)
            turn_dve(dve, s, 2, KT, banks=ROW_BANKS, part=(0, 2))
            dve_ahead.before(dve, n + 8)
            turn_dve(dve, s, 2, KT, banks=ROW_BANKS, part=(2, 4))
            add_result(dve, s, 1.0)

        GH, GD = 6, 64
        SH, SD, SG, SN, CONV = 6, 64, 2, 128, 4
        SR = SH // SG
        XT = 7
        PADC, PADP = 4, 16
        ar = Arena()
        h_u = ar(TT * 1536, "p (t n) -> p t n", t=TT)
        h_x = ar(XT * (T + PADC), "p (k t) -> p k t", k=XT)
        h_c = ar(XT * T, "p (k t) -> p k t", k=XT)
        h_p = ar(2 * (T + PADP), "p (k t) -> p k t", k=2)
        h_sum = [ar(2 * (T + PADP), "p (k t) -> p k t", k=2) for _ in range(2)]
        h_diff = ar(2 * T, "p (k t) -> p k t", k=2)
        h_count = ar(2 * T, "p (k t) -> p k t", k=2)
        h_pw = ar(2 * P, "p (k d) -> p k d", k=2)
        h_tri = ar(P)
        h_neg = ar(P)
        h_decay = ar(TT * SH * P, "p (n l) -> p n l", l=P)
        h_xs = ar(TT * SH * SD, "p (t n) -> p t n", t=TT)
        h_xdt = ar(TT * SH * SD, "p (t n) -> p t n", t=TT)
        h_b = ar(SG * SN, "p (g n) -> p g n", g=SG)
        h_xw = ar(SH * SD)
        h_state = ar(SH * SD)
        h_qkt = ar(6 * T, "p (k t) -> p k t", k=6)
        h_y = ar(TT * SH * SD, "p (t n) -> p t n", t=TT)
        h_prow = ar(TT * HC, "p (t n) -> p t n", t=TT)
        h_ysq = ar(TT * SH * SD, "p (t n) -> p t n", t=TT)
        h_z = ar(TT * SH * SD, "p (t n) -> p t n", t=TT)
        h_probs = [ar(3 * P) for _ in range(2)]
        h_probs_t = [ar(3 * P) for _ in range(2)]
        h_small = [ar(6) for _ in range(4)]
        N12 = TT * SH
        h_raw, h_abs, h_e, h_s, h_s2, h_q, h_dt, h_da, h_acum, h_eacum = (ar(N12) for _ in range(10))
        h_ea = ar(SH)
        h_yss, h_yrs = ar(4), ar(4)
        HY_PE = Steps(sem("hyb_pe"), ["p_turned", "xs_turned", "cumulated", "state", "cb_pool", "qk_turned", "y"])
        HY_ACT = Steps(sem("hyb_act"), ["ea", "p_rows", "conv", "u2", "silu_z", "xs_rows", "exp_dt", "u0", "decay", "exp_acum",
                                        "u1", "qk_cols"])
        HY_DVE = Steps(sem("hyb_dve"), ["xa", "xb", "conv", "dt_raw", "abs", "tail", "diff", "da", "xdt", "acum", "decay", "xw",
                                        "scores", "state", "y_off", "y_squares", "y_rows"])
        HY_POOL = Steps(sem("hyb_pool"), ["tri", "counts", "causal", "y_rstd"])
        pw_loaded = sem("pool_w_loaded")
        hyb_attn = Attention(
            "hyb", GH, GD,
            lambda h: [(h_qkt[64 * (h % 2):64 * (h % 2) + 64, h // 2, :], h_qkt[64 * (h % 2):64 * (h % 2) + 64, 3 + h // 2, :])],
            lambda h, t: h_u[:, t, 768 + h * GD:768 + (h + 1) * GD], lambda h, t: GD ** -0.5, 2,
            lambda h, t: xn[:, t, h * GD:(h + 1) * GD], h_probs, h_probs_t, h_small)

        def hybrid_load(sp, s):
            n, w = base[s], io["w_in_2"][0]
            load_columns(sp, n, w, 1536, 512)
            load_columns(sp, n + 2, w, 2048, 384)
            load_columns(sp, n + 4, w, 2432, 262)
            for j, c0 in enumerate((1024, 0, 512)):
                load_columns(sp, n + 6 + 2 * j, w, c0, 512)
            load_square(sp, n + 12, io["w_out_2"][0], OUT_ORDER)

        OUT_ORDER = (2, 3, 0, 1)

        def hybrid_pe(pe, s):
            n = base[s]
            for b in range(4):
                turn_x(pe, s, b, b)
            columns_product(pe, n, [bank(4 + j, T) for j in range(4)], 512, first_of=s)
            rms_row_pe(pe, 1, 3)
            columns_product(pe, n + 2, [bank(j, T) for j in range(3)], 384)
            pe.wait_ge(HY_DVE.sem, HY_DVE.after("xa"))
            for half in range(2):
                take_slot(pe, n + 4 + half)
                for kk in range(4):
                    m = by_rows([bank(4, 262), bank(5, 262)], 4 * half + kk, n + 4 + half, kk, 262, half + kk == 0, half + kk == 4)
                m.then_inc(weights_used, 1)

            def turn_p():
                pe.wait_ge(HY_ACT.sem, HY_ACT.after("p_rows"))
                for k in range(2):
                    for tt in range(TT):
                        m = nc.tensor.transpose(ps[:, 6, k * T + tt * P:k * T + (tt + 1) * P], h_prow[:, tt, k * P:(k + 1) * P],
                                                ident[:, :])
                HY_PE.done(m, "p_turned")

            pe.wait_ge(HY_DVE.sem, HY_DVE.after("xb"))
            rows_product(pe, n + 6, [bank(0), bank(1)], halfway=turn_p)
            pe.wait_ge(HY_ACT.sem, HY_ACT.after("conv"))
            pe.wait_ge(HY_DVE.sem, HY_DVE.after("dt_raw"))
            for tt in range(TT):
                for k in range(3):
                    nc.tensor.transpose(ps[:, 2 + tt, k * P:(k + 1) * P], h_c[:, k, tt * P:(tt + 1) * P], ident[:, :])
            for g in range(SG):
                m = nc.tensor.transpose(ps[:, 2 + g, 3 * P:4 * P], h_c[:, 3 + g, 0:P], ident[:, :])
            HY_PE.done(m, "xs_turned")
            rows_product(pe, n + 8, [bank(4), bank(5)])
            pe.wait_ge(HY_DVE.sem, HY_DVE.after("da"))
            pe.wait_ge(HY_ACT.sem, HY_ACT.after("xs_rows"))
            for tt in range(TT):
                for h in range(SH):
                    j = tt * SH + h
                    nc.tensor.matmul(ps[:, j // 4, (j % 4) * P:(j % 4 + 1) * P], h_da[:, j:j + 1].broadcast_to([P, P]), h_tri,
                                     start=True, stop=True)
            for tt in range(TT):
                m = nc.tensor.matmul(ps[:, 3, tt * SH:(tt + 1) * SH], h_tri, h_da[:, tt * SH:(tt + 1) * SH], start=True, stop=True)
            HY_PE.done(m, "cumulated")
            pe.wait_ge(HY_DVE.sem, HY_DVE.after("tail"))
            rows_product(pe, n + 10, [bank(6), bank(7)])
            pe.wait_ge(HY_DVE.sem, HY_DVE.after("xw"))
            for g in range(SG):
                c = slice(g * SR * SD, (g + 1) * SR * SD)
                m = nc.tensor.matmul(ps[:, 2, c], h_b[:, g, :], h_xw[:, c], start=True, stop=True)
            HY_PE.done(m, "state")
            pe.wait_ge(HY_ACT.sem, HY_ACT.after("u0"))
            pe.wait_ge(HY_DVE.sem, HY_DVE.after("diff"))
            pe.wait_ge(pw_loaded, 32)
            for tt in range(TT):
                for g in range(SG):
                    o = (tt * SG + g) * P
                    nc.tensor.matmul(ps[:, 4, o:o + P], h_c[:, 3 + g, tt * P:(tt + 1) * P], h_c[:, 5 + g, tt * P:(tt + 1) * P],
                                     start=True, stop=True)
            for tt in range(TT):
                for k in range(2):
                    m = nc.tensor.matmul(ps[:, 5, (tt * 2 + k) * P:(tt * 2 + k + 1) * P],
                                         h_diff[:, k, tt * P:(tt + 1) * P], h_pw[:, k, :], start=True, stop=True)
            HY_PE.done(m, "cb_pool")
            pe.wait_ge(HY_ACT.sem, HY_ACT.after("u1"))
            pe.wait_ge(HY_DVE.sem, HY_DVE.after("acum"))
            for k in range(6):
                b = (6, 7, 3)[k // 2]
                for tt in range(TT):
                    at = (k % 2) * T + tt * P
                    m = nc.tensor.transpose(ps[:, b, at:at + P], h_u[:, tt, k * P:(k + 1) * P], ident[:, :])
            HY_PE.done(m, "qk_turned")
            pe.wait_ge(HY_DVE.sem, HY_DVE.after("scores"))
            for tt in range(TT):
                for h in range(SH):
                    c = slice(h * SD, (h + 1) * SD)
                    nc.tensor.matmul(ps[:, tt, c], h_decay[:, tt * SH + h, :], h_xdt[:, tt, c], start=True, stop=True)
            pe.wait_ge(HY_ACT.sem, HY_ACT.after("qk_cols"))
            hyb_attn.scores(0)
            hyb_attn.scores(1)
            pe.wait_ge(HY_DVE.sem, HY_DVE.after("state"))
            for g in range(SG):
                c = slice(g * SR * SD, (g + 1) * SR * SD)
                m = nc.tensor.matmul(ps[:, 3, c], h_c[:, 5 + g, P:T], h_state[:, c], start=True, stop=True)
            HY_PE.done(m, "y")
            hyb_attn.pe(pe, lambda: pe.wait_ge(HY_DVE.sem, HY_DVE.after("y_off")))
            pe.wait_ge(HY_DVE.sem, HY_DVE.after("y_rows"))
            turn_bank(2, KT, xn, ROW_BANKS[2])
            turn_bank(3, KT, xn, ROW_BANKS[3])

            def turn_rest():
                pe.wait_ge(hyb_attn.dve_done.sem, hyb_attn.dve_done.after(f"rows{GH - 1}"))
                turn_bank(0, KT, xn, ROW_BANKS[0])
                turn_bank(1, KT, xn, ROW_BANKS[1])

            project_out(pe, s, 1, n + 12, rest=turn_rest, order=OUT_ORDER)

        def hybrid_act(act, s):
            n = base[s]
            norm_act(act, s, MIX2)
            HY_ACT.done(nc.scalar.activation(h_ea, a_log[:, :], ACT.Exp), "ea")
            rms(act, s)
            act_ahead.before(act, n + 5)
            act.wait_ge(weights_used, n + 6)
            for tt in range(TT):
                m = nc.scalar.activation(h_prow[:, tt, :], ps[:, 4 + tt, SH:SH + HC], ACT.Copy, scale=rstd[:, tt:tt + 1])
            HY_ACT.done(m, "p_rows")
            act_ahead.before(act, n + 6)
            act.wait_ge(HY_DVE.sem, HY_DVE.after("conv"))
            for k in range(XT):
                m = nc.scalar.activation(h_c[:, k, :], h_c[:, k, :], ACT.Silu, bias=conv_cols[:, CONVB + k:CONVB + k + 1])
            HY_ACT.done(m, "conv")
            act_ahead.before(act, n + 7)
            act.wait_ge(weights_used, n + 8)
            HY_ACT.done(scaled_rows(h_u[:, :, 1024:1536], 0, ACT.Copy), "u2")
            act.wait_ge(HY_ACT.sem, HY_ACT.after("u2"))
            HY_ACT.done(nc.scalar.activation(h_z, h_u[:, :, 1152:1536], ACT.Silu), "silu_z")
            act.wait_ge(HY_PE.sem, HY_PE.after("xs_turned"))
            nc.scalar.activation(h_xs, ps[:, 2:4, 0:3 * P], ACT.Copy)
            HY_ACT.done(nc.scalar.activation(h_b, ps[:, 2:4, 3 * P:4 * P], ACT.Copy), "xs_rows")
            act.wait_ge(HY_DVE.sem, HY_DVE.after("abs"))
            HY_ACT.done(nc.scalar.activation(h_e, h_abs, ACT.Exp, scale=-1.0), "exp_dt")
            act_ahead.before(act, n + 9)
            act.wait_ge(weights_used, n + 10)
            HY_ACT.done(scaled_rows(h_u[:, :, 0:512], 4, ACT.Copy), "u0")
            act_ahead.before(act, n + 10)
            act.wait_ge(HY_DVE.sem, HY_DVE.after("decay"))
            HY_ACT.done(nc.scalar.activation(h_decay, h_decay, ACT.Exp), "decay")
            HY_ACT.done(nc.scalar.activation(h_eacum, h_acum, ACT.Exp), "exp_acum")
            act_ahead.before(act, n + 11)
            act.wait_ge(weights_used, n + 12)
            HY_ACT.done(scaled_rows(h_u[:, :, 512:1024], 6, ACT.Copy), "u1")
            act.wait_ge(HY_PE.sem, HY_PE.after("qk_turned"))
            nc.scalar.activation(h_qkt[:, 0:4, :], ps[:, 6:8, :], ACT.Copy)
            HY_ACT.done(nc.scalar.activation(h_qkt[:, 4:6, :], ps[:, 3, :], ACT.Copy), "qk_cols")
            hyb_attn.act(act)
            turn_act(act, s, 1, KT, banks=ROW_BANKS, part=(0, 2), order=OUT_ORDER)
            act_ahead.before(act, n + 12)
            turn_act(act, s, 1, KT, banks=ROW_BANKS, part=(2, 4), order=OUT_ORDER)
            act_ahead.before(act, n + 15)

        def hybrid_pool(pool, s):
            pool_link(pool, nc.gpsimd.memset(h_pw, 0.0))
            for b in range(2):
                pool.dma_start(h_pw[64 * b:64 * b + 64, :, 64 * b:64 * b + 64],
                               io["pool_w_2"][0].rearrange("(a b) c d -> b c a d", b=2)[b]).then_inc(pw_loaded, 16)
            nc.gpsimd.memset(h_x[:, :, 0:PADC], 0.0)
            nc.gpsimd.memset(h_p[:, :, 0:PADP], 0.0)
            for j in range(2):
                nc.gpsimd.memset(h_sum[j][:, :, 0:PADP], 0.0)
            nc.gpsimd.memset(h_tri, 1.0)
            pool_link(pool, nc.gpsimd.memset(h_neg, 0.0))
            nc.gpsimd.affine_select(out=h_tri, in_=h_tri, compare_op=ALU.is_ge, fill=0.0, base=0, pattern=[[1, P]],
                                    channel_multiplier=-1)
            HY_POOL.done(nc.gpsimd.affine_select(out=h_neg, in_=h_neg, compare_op=ALU.is_ge, fill=-1e30, base=0,
                                                 pattern=[[1, P]], channel_multiplier=-1), "tri")
            for g, w in enumerate((2, 4, 8, 16)):
                v = h_count[64 * (g % 2):64 * (g % 2) + 64, g // 2, :]
                for t in range(w - 1):
                    nc.gpsimd.memset(v[:, t:t + 1], 1.0 / (t + 1))
                pool_link(pool, nc.gpsimd.memset(v[:, w - 1:T], 1.0 / w))
            HY_POOL.done(nc.gpsimd.memset(h_yss, 0.0), "counts")
            pool.wait_ge(r_steps, 3 + 2)
            HY_POOL.done(make_causal(pool), "causal")
            pool.wait_ge(HY_DVE.sem, HY_DVE.after("y_squares"))
            pool_link(pool, nc.gpsimd.tensor_scalar(h_yss, h_yss, 1.0 / (SR * SD), EPS, ALU.mult, ALU.add))
            HY_POOL.done(nc.gpsimd.tensor_tensor(h_yrs, h_yss, minus_half[:, 0:4], ALU.pow), "y_rstd")

        def hybrid_dve(dve, s):
            n = base[s]
            norm_dve(dve, s, MIX2)
            rms_diagonals(dve, s, 1)
            dve_ahead.before(dve, n + 1)
            rms_row(dve, 1, 3)

            def convolve(ks):
                done = {}
                for j in range(CONV):
                    for k in ks:
                        w = conv_cols[:, CONVW + j * XT + k:CONVW + j * XT + k + 1]
                        v = h_x[:, k, PADC - CONV + 1 + j:PADC - CONV + 1 + j + T]
                        if j == 0:
                            m = nc.vector.tensor_scalar(h_c[:, k, :], v, w, None, ALU.mult)
                        else:
                            dve.wait_ge(dve_chain, done[k])
                            m = nc.vector.scalar_tensor_tensor(out=h_c[:, k, :], in0=v, scalar=w, in1=h_c[:, k, :], op0=ALU.mult, op1=ALU.add)
                        if j < CONV - 1:
                            m.then_inc(dve_chain, 1)
                            dve_link.n += 1
                            done[k] = dve_link.n
                return m

            dve.wait_ge(weights_used, n + 2)
            HY_DVE.done(nc.vector.tensor_tensor(h_x[:, 0:4, PADC:PADC + T], ps[:, 4:8, 0:T], repeated(r_row[:, :], 1, 4), ALU.mult), "xa")
            dve_ahead.before(dve, n + 2)
            dve.wait_ge(HY_POOL.sem, HY_POOL.after("counts"))
            dve.wait_ge(HY_DVE.sem, HY_DVE.after("xa"))
            convolve(range(4))
            dve_ahead.before(dve, n + 3)
            dve.wait_ge(weights_used, n + 4)
            HY_DVE.done(nc.vector.tensor_tensor(h_x[:, 4:7, PADC:PADC + T], ps[:, 0:3, 0:T], repeated(r_row[:, :], 1, 3), ALU.mult), "xb")
            dve_ahead.before(dve, n + 4)
            dve.wait_ge(HY_DVE.sem, HY_DVE.after("xb"))
            HY_DVE.done(convolve(range(4, XT)), "conv")
            dve_ahead.before(dve, n + 5)
            dve.wait_ge(HY_ACT.sem, HY_ACT.after("p_rows"))
            for tt in range(TT):
                m = nc.vector.scalar_tensor_tensor(out=h_raw[:, tt * SH:(tt + 1) * SH], in0=bank(4 + tt, SH),
                                                   scalar=rstd[:, tt:tt + 1], in1=dt_bias[:, :], op0=ALU.mult, op1=ALU.add)
            HY_DVE.done(m, "dt_raw")
            dve.wait_ge(HY_DVE.sem, HY_DVE.after("dt_raw"))
            HY_DVE.done(nc.vector.scalar_tensor_tensor(out=h_abs, in0=h_raw, scalar=-1.0, in1=h_raw, op0=ALU.mult, op1=ALU.max), "abs")

            dve_ahead.before(dve, n + 6)
            dve.wait_ge(HY_PE.sem, HY_PE.after("p_turned"))
            HY_DVE.done(nc.vector.tensor_copy(h_p[:, :, PADP:PADP + T], bank(6).rearrange("p (k t) -> p k t", k=2)), "tail")
            dve.wait_ge(HY_DVE.sem, HY_DVE.after("tail"))
            src = h_p
            for g in range(4):
                dst, w = h_sum[g % 2], 2 ** g
                dve_link(dve, nc.vector.tensor_tensor(dst[:, :, PADP:PADP + T], src[:, :, PADP:PADP + T], src[:, :, PADP - w:PADP - w + T], ALU.add))
                rows = slice(64 * (g % 2), 64 * (g % 2) + 64)
                d = h_diff[rows, g // 2, :]
                dve_link(dve, nc.vector.tensor_tensor(d, dst[rows, g // 2, PADP:PADP + T], h_count[rows, g // 2, :], ALU.mult))
                m = nc.vector.tensor_tensor(d, d, h_p[rows, g // 2, PADP:PADP + T], ALU.subtract)
                src = dst
            HY_DVE.done(m, "diff")
            dve_ahead.before(dve, n + 7)

            dve.wait_ge(HY_ACT.sem, HY_ACT.after("exp_dt"))
            dve_link(dve, nc.vector.tensor_scalar(h_s, h_e, 2.0, None, ALU.add))
            dve_link(dve, nc.vector.reciprocal(h_s, h_s))
            dve_link(dve, nc.vector.tensor_tensor(h_s, h_s, h_e, ALU.mult))
            dve_link(dve, nc.vector.tensor_tensor(h_s2, h_s, h_s, ALU.mult))
            dve_link(dve, nc.vector.tensor_scalar(h_q, h_s2, 1 / 17, None, ALU.mult))
            for d in (15, 13, 11, 9, 7, 5, 3):
                dve_link(dve, nc.vector.scalar_tensor_tensor(out=h_q, in0=h_q, scalar=1 / d, in1=h_s2, op0=ALU.add, op1=ALU.mult))
            dve_link(dve, nc.vector.scalar_tensor_tensor(out=h_q, in0=h_q, scalar=1.0, in1=h_s, op0=ALU.add, op1=ALU.mult))
            dve_link(dve, nc.vector.tensor_scalar(h_raw, h_raw, 0.0, None, ALU.max))
            dve_link(dve, nc.vector.scalar_tensor_tensor(out=h_dt, in0=h_q, scalar=2.0, in1=h_raw, op0=ALU.mult, op1=ALU.add))
            dve.wait_ge(HY_ACT.sem, HY_ACT.after("ea"))
            v2 = h_dt.rearrange("p (t h) -> p t h", t=TT)
            HY_DVE.done(nc.vector.scalar_tensor_tensor(out=h_da.rearrange("p (t h) -> p t h", t=TT), in0=v2, scalar=-1.0,
                                                       in1=repeated(h_ea, 1, TT), op0=ALU.mult, op1=ALU.mult), "da")
            dve.wait_ge(HY_ACT.sem, HY_ACT.after("xs_rows"))
            xs = h_xs.rearrange("p t n -> p (t n)").rearrange("p (n d) -> p n d", d=SD)
            xdt = h_xdt.rearrange("p t n -> p (t n)").rearrange("p (n d) -> p n d", d=SD)
            HY_DVE.done(nc.vector.tensor_tensor(xdt, xs, repeated(h_dt, 2, SD), ALU.mult), "xdt")
            y = h_y.rearrange("p t n -> p (t n)").rearrange("p (n d) -> p n d", d=SD)
            skip(y, xs)
            dve_ahead.before(dve, n + 9)
            dve_ahead.before(dve, n + 10)
            dve.wait_ge(HY_PE.sem, HY_PE.after("cumulated"))
            HY_DVE.done(nc.vector.tensor_copy(h_acum, bank(3, N12)), "acum")
            dve.wait_ge(HY_DVE.sem, HY_DVE.after("acum"))
            acb = ps[:, 0:3, :].rearrange("p b n -> p (b n)").rearrange("p (n l) -> p n l", l=P)
            dve_link(dve, nc.vector.tensor_tensor(h_decay, acb, repeated(h_acum, 2, P), ALU.subtract))
            HY_DVE.done(nc.vector.tensor_tensor(h_decay, h_decay, repeated(h_neg, 1, N12), ALU.add), "decay")
            dve.wait_ge(HY_ACT.sem, HY_ACT.after("decay"))
            xw = h_xw.rearrange("p (h d) -> p h d", d=SD)
            HY_DVE.done(nc.vector.tensor_tensor(xw, xdt[:, 0:SH, :], repeated(h_decay[:, 0:SH, P - 1], 2, SD), ALU.mult), "xw")
            dve_ahead.before(dve, n + 11)
            dve.wait_ge(HY_DVE.sem, HY_DVE.after("xw"))
            dve.wait_ge(HY_PE.sem, HY_PE.after("cb_pool"))
            for tt in range(TT):
                cb = bank(4)[:, tt * SG * P:(tt + 1) * SG * P].rearrange("p (g l) -> p g l", g=SG)
                v = h_decay[:, tt * SH:(tt + 1) * SH, :].rearrange("p (g r) l -> p g r l", g=SG)
                nc.vector.tensor_tensor(v, v, repeated(cb, 2, SR), ALU.mult)
            HY_DVE.done(nc.vector.tensor_tensor(xn[:, :, 768:1024], bank(5).rearrange("p (t n) -> p t n", t=TT),
                                                repeated(pool_gain[:, :], 1, TT), ALU.mult), "scores")
            HY_DVE.done(nc.vector.tensor_copy(h_state, bank(2, SH * SD)), "state")
            dve.wait_ge(HY_POOL.sem, HY_POOL.after("causal"))
            hyb_attn.maxima(dve, 0)
            hyb_attn.maxima(dve, 1)
            dve.wait_ge(HY_PE.sem, HY_PE.after("y"))
            dve.wait_ge(HY_ACT.sem, HY_ACT.after("exp_acum"))
            yo = h_ysq[:, 1, :].rearrange("p (h d) -> p h d", d=SD)
            nc.vector.tensor_tensor(h_y, h_y, ps[:, 0:2, 0:SH * SD], ALU.add)
            HY_DVE.done(nc.vector.tensor_tensor(yo, bank(3, SH * SD).rearrange("p (h d) -> p h d", d=SD),
                                                repeated(h_eacum[:, SH:N12], 2, SD), ALU.mult), "y_off")

            def y_sum():
                dve.wait_ge(HY_DVE.sem, HY_DVE.after("y_off"))
                dve_link(dve, nc.vector.tensor_tensor(h_y[:, 1, :], h_y[:, 1, :], h_ysq[:, 1, :], ALU.add))

            def y_gate():
                dve.wait_ge(HY_ACT.sem, HY_ACT.after("silu_z"))
                dve_link(dve, nc.vector.tensor_tensor(h_y, h_y, h_z, ALU.mult))

            def y_square():
                dve_link(dve, nc.vector.tensor_tensor(h_ysq, h_y, h_y, ALU.mult))

            def y_sum_squares():
                HY_DVE.done(nc.vector.tensor_reduce(h_yss, h_ysq.rearrange("p t n -> p (t n)").rearrange("p (n d) -> p n d", d=SR * SD),
                                                    AX.X, ALU.add), "y_squares")

            def y_norm():
                dve_link(dve, nc.vector.tensor_tensor(h_y, h_y, repeated(ssd_gain[:, :], 1, TT), ALU.mult))
                dve.wait_ge(HY_POOL.sem, HY_POOL.after("y_rstd"))
                HY_DVE.done(nc.vector.tensor_tensor(xn[:, :, 384:768].rearrange("p t (g d) -> p t g d", g=SG),
                                                    h_y.rearrange("p t (g d) -> p t g d", g=SG),
                                                    repeated(h_yrs.rearrange("p (t g) -> p t g", t=TT), 3, SR * SD), ALU.mult), "y_rows")

            hyb_attn.dve(dve, (y_sum, y_gate, y_square, y_sum_squares, y_norm))
            turn_dve(dve, s, 1, KT, banks=ROW_BANKS, part=(0, 2), order=OUT_ORDER)
            dve_ahead.before(dve, n + 12)
            turn_dve(dve, s, 1, KT, banks=ROW_BANKS, part=(2, 4), order=OUT_ORDER)
            add_result(dve, s, 1.0)

        def skip(y, xs):
            for tt in range(TT):
                m = nc.vector.tensor_tensor(y[:, tt * SH:(tt + 1) * SH, :], xs[:, tt * SH:(tt + 1) * SH, :],
                                            repeated(d_skip[:, :], 2, SD), ALU.mult)
            return m

        PARAM_ROWS = [(rows_a, GAINS, io["norm_gains"].rearrange("l n (k p) -> (l n k) p", p=P)),
                      (rows_a, MIX2, io["norm_mix_2"].rearrange("o (k p) -> (o k) p", p=P)),
                      (rows_a, FFN2, io["norm_ffn_2"].rearrange("o (k p) -> (o k) p", p=P)),
                      (rows_a, QA, io["mla_q_a_norm"].rearrange("o (k p) -> (o k) p", p=P)),
                      (rows_a, KVA, io["mla_kv_a_norm"].rearrange("o (k p) -> (o k) p", p=P)),
                      (rows_a, BS, io["gmlp_b_s"].rearrange("o h p -> (o h) p")),
                      (rows_a, LB, io["hgrn_lb_raw"].rearrange("o (k p) -> (o k) p", p=P)),
                      (rows_a, QN, io["mla_q_norm"][:, 0:P]),
                      (rows_a, KN, io["mla_k_norm"][:, 0:P]),
                      (rows_b, CONVW, io["conv_w_2"].rearrange("o w (k p) -> (o w k) p", p=P)),
                      (rows_b, CONVB, io["conv_b_2"].rearrange("o (k p) -> (o k) p", p=P))]

        def load_rows(q, which):
            for dst, at, v in which:
                q.dma_start(dst[at:at + v.shape[0], :], v).then_inc(rows_loaded, 16)

        def load_repeated(q):
            q.dma_start(pos_i[:, :], io["positions"].rearrange("o (t p) -> p (o t)", p=P),
                        allow_slow_non_contiguous=True).then_inc(params_loaded, 16)
            for dst, v in ((vnorm[:, :], io["gmlp_v_norm"].rearrange("o h d -> o (h d)")), (onorm[:, :], io["hgrn_out_norm"]),
                           (qk_norm[:, 0, :], io["mla_q_norm"][:, P:]), (qk_norm[:, 1, :], io["mla_k_norm"][:, P:]),
                           (ssd_gain[:, :], io["ssd_norm_2"]), (pool_gain[:, :], io["pool_scale_2"]), (dt_bias[:, :], io["dt_bias_2"]),
                           (a_log[:, :], io["a_log_2"]), (d_skip[:, :], io["d_skip_2"])):
                q.dma_start(dst, v.partition_broadcast(P)).then_inc(params_loaded, 16)
        ROWS_DMAS, PARAM_DMAS = len(PARAM_ROWS), 10

        def final_dve(dve):
            last = len(PLAN)
            dve.wait_ge(gain_loaded, 16 * (PLAN.count("ple") + 1))
            for tt in range(TT):
                dve.wait_ge(rstd_ready, TT * last + tt + 1)
                nc.vector.scalar_tensor_tensor(out=xn[:, tt, :], in0=x[:, tt, :], scalar=rstd[:, tt:tt + 1],
                                               in1=gain_row[:, :], op0=ALU.mult, op1=ALU.mult).then_inc(rows_ready, 1)

        block = stack.enter_context(nc.Block())

        @block.sync
        def _(sp):
            for tt in range(TT):
                sp.dma_start(x[:, tt, :], io["x"][0, tt * P:(tt + 1) * P, :]).then_inc(x_loaded, 16)
            load_rows(sp, PARAM_ROWS[6:])
            for s, name in enumerate(PLAN):
                n, f = base[s], fs[s]
                if name == "even":
                    even_load(sp, s)
                if name == "mla":
                    mla_load(sp, s)
                if name == "hybrid":
                    hybrid_load(sp, s)
                if name == "ple":
                    ple_load(sp, s, ples[s])
                if name == "ffn":
                    if f < 4:
                        l, j = divmod(f, 2)
                        ffn_load(sp, n, io["ffn_w_gate"][l, j], io["ffn_w_up"][l, j], io["ffn_w_down"][l, j])
                    else:
                        gu = io["w_gate_up_2"][0]
                        ffn_load(sp, n, gu[:, 0:FF], gu[:, FF:2 * FF], io["w_down_2"][0])
            for tt in range(TT):
                sp.wait_ge(rows_ready, TT * calls_so_far + tt + 1)
                sp.dma_start(out[0, tt * P:(tt + 1) * P, :], xn[:, tt, :]).then_inc(stored, 16)
            sp.wait_ge(stored, 16 * TT)

        @block.gpsimd
        def _(pool):
            pool_link(pool, nc.gpsimd.memset(ident[:, :], 0.0))
            nc.gpsimd.affine_select(out=ident[:, :], in_=ident[:, :], compare_op=ALU.not_equal, fill=1.0, base=0,
                                    pattern=[[-1, P]], channel_multiplier=1).then_inc(ident_ready, 1)
            pool_link(pool, nc.gpsimd.memset(minus_half[:, :], -0.5))
            for j in range(32):
                m = nc.gpsimd.memset(inv_freq[:, j:j + 1], 10000.0 ** (-2 * j / 64))
            m.then_inc(consts_ready, 1)
            nc.gpsimd.memset(ones[:, :], 1.0).then_inc(consts_ready, 1)
            load_repeated(pool)
            for s, name in enumerate(PLAN):
                norm_pool(pool, s)
                if name == "even":
                    even_pool(pool, s)
                if name == "mla":
                    mla_pool(pool, s)
                if name == "hybrid":
                    hybrid_pool(pool, s)
                if name == "ple":
                    ple_pool(pool, s, ples[s])
            norm_pool(pool, len(PLAN))

        @block.scalar
        def _(act):
            load_rows(act, PARAM_ROWS[0:6])
            act.wait_ge(cols_turned, 1)
            nc.scalar.activation(cols[:, :], ps[:, 3, 0:ROWS_A], ACT.Copy).then_inc(cols_ready, 1)
            nc.scalar.activation(conv_cols[:, :], ps[:, 3, P:P + ROWS_B], ACT.Copy).then_inc(cols_ready, 1)
            act.wait_ge(cols_ready, 2)
            act.wait_ge(lb_steps, 1)
            nc.scalar.activation(lb[:, 1, :], lb[:, 0, :], ACT.Exp).then_inc(lb_steps, 1)
            for s, name in enumerate(PLAN):
                if name == "even":
                    even_act(act, s)
                if name == "mla":
                    mla_act(act, s)
                if name == "hybrid":
                    hybrid_act(act, s)
                if name == "ple":
                    ple_act(act, s, ples[s])
                if name == "ffn":
                    if s == len(PLAN) - 1:
                        act.wait_ge(x_ready, 4 * s)
                        act.dma_start(gain_row[:, :], io["norm_final_2"].rearrange("(o n) -> o n", o=1).partition_broadcast(P))\
                           .then_inc(gain_loaded, 16)
                    ffn_act(act, base[s], s, fs[s])
            norm_act(act, len(PLAN), None)

        @block.vector
        def _(dve):
            dve.wait_ge(cols_ready, 2)
            dve.wait_ge(consts_ready, 2)
            nc.vector.tensor_tensor(lb[:, 0, :], cols[:, LB:LB + 4], cols[:, LB:LB + 4], ALU.subtract).then_inc(lb_steps, 1)
            dve.wait_ge(lb_steps, 2)
            dve_link(dve, nc.vector.reciprocal(lb[:, 2, :], lb[:, 1, :]))
            dve_link(dve, nc.vector.tensor_tensor(lb[:, 2, :], lb[:, 2, :], lb[:, 1, :], ALU.mult))
            dve_link(dve, nc.vector.tensor_tensor(lb[:, 0, :], lb[:, 2, :], lb[:, 2, :], ALU.subtract))
            dve_link(dve, nc.vector.tensor_scalar(lb[:, 0, :], lb[:, 0, :], 0.0, 0.999, ALU.max, ALU.min))
            dve_link(dve, nc.vector.tensor_scalar(lb[:, 1, :], lb[:, 0, :], -1.0, 1.0, ALU.mult, ALU.add))
            for s, name in enumerate(PLAN):
                if s == 1:
                    dve.wait_ge(params_loaded, 16 * PARAM_DMAS)
                if name == "even":
                    even_dve(dve, s)
                if name == "mla":
                    mla_dve(dve, s)
                if name == "hybrid":
                    hybrid_dve(dve, s)
                if name == "ple":
                    ple_dve(dve, s, ples[s])
                if name == "ffn":
                    ffn_dve(dve, base[s], s, fs[s])
            final_dve(dve)

        @block.tensor
        def _(pe):
            pe.wait_ge(rows_loaded, 16 * ROWS_DMAS)
            pe.wait_ge(ident_ready, 1)
            nc.tensor.transpose(ps[:, 3, 0:ROWS_A], rows_a[0:ROWS_A, :], ident[0:ROWS_A, 0:ROWS_A])
            nc.tensor.transpose(ps[:, 3, P:P + ROWS_B], rows_b[0:ROWS_B, :], ident[0:ROWS_B, 0:ROWS_B]).then_inc(cols_turned, 1)
            pe.wait_ge(cols_ready, 2)
            for s, name in enumerate(PLAN):
                if name == "even":
                    even_pe(pe, s)
                if name == "mla":
                    mla_pe(pe, s)
                if name == "hybrid":
                    hybrid_pe(pe, s)
                if name == "ple":
                    ple_pe(pe, s, ples[s])
                if name == "ffn":
                    ffn_pe(pe, base[s], s, fs[s])


INPUTS = ["x", "p", "positions", "norm_gains", "ffn_w_gate", "ffn_w_up", "ffn_w_down", "ple_w_gate", "ple_w_proj",
          "even_w_in", "gmlp_v_norm", "gmlp_w_s", "gmlp_b_s", "hgrn_lb_raw", "hgrn_out_norm", "even_w_out",
          "mla_w_in", "mla_q_a_norm", "mla_kv_a_norm", "mla_w_q_b", "mla_w_kv_b", "mla_q_norm", "mla_k_norm",
          "mla_w_out", "norm_mix_2", "w_in_2", "conv_w_2", "conv_b_2", "dt_bias_2", "a_log_2", "d_skip_2",
          "ssd_norm_2", "pool_w_2", "pool_scale_2", "w_out_2", "norm_ffn_2", "w_gate_up_2", "w_down_2", "norm_final_2"]


def kernel(**inputs):
    import numpy as np
    import concourse.bacc as bacc
    from concourse.bass_utils import run_bass_kernel_spmd

    nc = bacc.Bacc("TRN2", target_bir_lowering=False, num_devices=1)
    arrays, io = {}, {}
    for name in INPUTS:
        a = np.ascontiguousarray(inputs[name])
        arrays["in_" + name] = a
        io[name] = nc.dram_tensor("in_" + name, a.shape, mybir.dt.from_np(a.dtype), kind="ExternalInput").ap()
    out = nc.dram_tensor("out", inputs["x"].shape, mybir.dt.float32, kind="ExternalOutput").ap()
    build_block(nc, io, out)
    r = run_bass_kernel_spmd(nc, [arrays], core_ids=[0])
    return r.results[0]["out"]
```
